# Optimizing a Trainium2 kernel written in Bass

```python
import math
import jax, jax.numpy as jnp
from jax import lax
import numpy as np

D_MODEL = 1024
BATCH = 1
SEQ = 256
DEPTH = 1
DEC_BATCH = 8
DEC_SEQ = 8
PAST_LEN = 2048
PAGE_SIZE = 128

DN_HEADS = 8
DN_DK = 128
DN_DV = 128
DN_CONV = 4
DN_CHUNK = 64
GM_WIDTH = 1024
GM_GROUPS = 8
GM_CHUNK = 128
N_EXPERTS = 32
TOP_K = 4
D_EXPERT = 1024
SWIGLU_LIMIT = 7.0
SWIGLU_ALPHA = 1.702
MOE_BLOCK = 128
PLE_DIM = 256
EPS = 1e-6

QK_W = DN_HEADS * DN_DK
V_W = DN_HEADS * DN_DV
QKV_W = 2 * QK_W + V_W
IN_SIZES = (QKV_W, DN_HEADS, DN_HEADS, V_W, GM_WIDTH, GM_WIDTH, D_MODEL, D_MODEL)
IN_COLS = sum(IN_SIZES)

kernel_name = 'hybrid_gdn_chunkmlp_moe_step'

def rmsnorm(x, g):
    xf = x.astype(jnp.float32)
    y = xf * lax.rsqrt(jnp.mean(xf * xf, axis=-1, keepdims=True) + EPS)
    return (y * g.astype(jnp.float32)).astype(x.dtype)

def layernorm(x, g, b):
    xf = x.astype(jnp.float32)
    mu = jnp.mean(xf, axis=-1, keepdims=True)
    xc = xf - mu
    y = xc * lax.rsqrt(jnp.mean(xc * xc, axis=-1, keepdims=True) + EPS)
    return (y * g.astype(jnp.float32) + b.astype(jnp.float32)).astype(x.dtype)

def l2norm(x):
    xf = x.astype(jnp.float32)
    return xf * lax.rsqrt(jnp.sum(xf * xf, axis=-1, keepdims=True) + EPS)

def short_conv(x, buf, w):
    L = x.shape[1]
    xc = jnp.concatenate([buf.astype(x.dtype), x], axis=1)
    y = xc[:, 0:L] * w[0]
    for i in range(1, DN_CONV):
        y = y + xc[:, i:i + L] * w[i]
    return jax.nn.silu(y), xc[:, -(DN_CONV - 1):]

def gated_delta_rule(q, k, v, g, beta, s0):
    B, L, H, DK = q.shape
    DV = v.shape[-1]
    C = math.gcd(L, DN_CHUNK)
    NC = L // C

    def to_chunks(t):
        t = t.reshape((B, NC, C, H) + t.shape[3:])
        return t.transpose((1, 0, 3, 2) + tuple(range(4, t.ndim)))

    qc, kc, vc = to_chunks(q), to_chunks(k), to_chunks(v)
    bc = to_chunks(beta)
    gcum = jnp.cumsum(to_chunks(g), axis=-1)
    idx = jnp.arange(C)
    incl = idx[:, None] >= idx[None, :]
    strict = idx[:, None] > idx[None, :]
    decay = jnp.exp(jnp.where(incl, gcum[..., :, None] - gcum[..., None, :], -jnp.inf))
    kk = jnp.einsum('nbhcd,nbhsd->nbhcs', kc, kc)
    a_low = jnp.where(strict, kk * decay * bc[..., None, :], 0.0)
    t_mat = a_low + jnp.eye(C, dtype=jnp.float32)
    gam = jnp.exp(gcum)
    rhs = jnp.concatenate([vc, gam[..., None] * kc], axis=-1)
    sol = lax.linalg.triangular_solve(t_mat, rhs, left_side=True, lower=True, unit_diagonal=True)
    u_base, w_state = sol[..., :DV], sol[..., DV:]
    m_intra = jnp.einsum('nbhcd,nbhsd->nbhcs', qc, kc) * decay * bc[..., None, :]
    q_dec = gam[..., None] * qc
    k_dec = kc * (bc * jnp.exp(gcum[..., -1:] - gcum))[..., None]
    g_end = gam[..., -1]

    def step(S, xs):
        ub_c, w_c, m_c, qd_c, kd_c, ge_c = xs
        u = ub_c - jnp.einsum('bhck,bhkv->bhcv', w_c, S)
        o = jnp.einsum('bhck,bhkv->bhcv', qd_c, S) + jnp.einsum('bhcs,bhsv->bhcv', m_c, u)
        S = ge_c[..., None, None] * S + jnp.einsum('bhck,bhcv->bhkv', kd_c, u)
        return S, o

    s_fin, o = lax.scan(step, s0, (u_base, w_state, m_intra, q_dec, k_dec, g_end))
    o = o.transpose(1, 0, 3, 2, 4).reshape(B, L, H, DV)
    return o, s_fin

def deltanet_branch(qkv_pre, a_raw, b_raw, z_gate, conv_buf, s0, conv_w, a_log, dt_bias, onorm_g, w_proj):
    B, L, _ = qkv_pre.shape
    qkv, new_buf = short_conv(qkv_pre, conv_buf, conv_w)
    q = qkv[..., :QK_W].reshape(B, L, DN_HEADS, DN_DK)
    k = qkv[..., QK_W:2 * QK_W].reshape(B, L, DN_HEADS, DN_DK)
    v = qkv[..., 2 * QK_W:].reshape(B, L, DN_HEADS, DN_DV).astype(jnp.float32)
    q = l2norm(q) * (DN_DK ** -0.5)
    k = l2norm(k)
    g = -jnp.exp(a_log.astype(jnp.float32)) * jax.nn.softplus(a_raw.astype(jnp.float32) + dt_bias.astype(jnp.float32))
    beta = jax.nn.sigmoid(b_raw.astype(jnp.float32))
    o, s_new = gated_delta_rule(q, k, v, g, beta, s0.astype(jnp.float32))
    o = rmsnorm(o, onorm_g) * jax.nn.silu(z_gate.reshape(B, L, DN_HEADS, DN_DV).astype(jnp.float32))
    y = o.reshape(B, L, V_W).astype(qkv_pre.dtype) @ w_proj
    return y, s_new.astype(qkv_pre.dtype), new_buf

def chunk_mlp_branch(gu, gv, ln_g, ln_b, ws, bs, w_proj):
    B, L, _ = gu.shape
    C = min(GM_CHUNK, L)
    NC = L // C
    u = jax.nn.gelu(gu, approximate=False)
    v = layernorm(jax.nn.gelu(gv, approximate=False), ln_g, ln_b)
    tri = jnp.tril(jnp.ones((C, C), dtype=bool))
    w_mix = jnp.where(tri, ws[:, :C, :C], 0.0).astype(v.dtype)
    vc = v.reshape(B, NC, C, GM_GROUPS, GM_WIDTH // GM_GROUPS)
    s = jnp.einsum('gts,bnsgc->bntgc', w_mix, vc) + bs[:, :C].T[:, :, None]
    y = (u * s.reshape(B, L, GM_WIDTH)) @ w_proj
    return y, v

def moe_ffn(h, router_w, router_b, w1, b1, w2, b2):
    n, d = h.shape
    nk = n * TOP_K
    logits = h.astype(jnp.float32) @ router_w.astype(jnp.float32) + router_b.astype(jnp.float32)
    top_vals, top_idx = lax.top_k(logits, TOP_K)
    gates = jax.nn.softmax(top_vals, axis=-1).astype(h.dtype)
    flat_e = top_idx.reshape(-1)
    flat_tok = jnp.arange(nk, dtype=jnp.int32) // TOP_K
    order = jnp.argsort(flat_e)
    sorted_e = flat_e[order]
    counts = jnp.bincount(flat_e, length=N_EXPERTS)
    padded = (counts + MOE_BLOCK - 1) // MOE_BLOCK * MOE_BLOCK
    pad_end = jnp.cumsum(padded)
    pad_start = pad_end - padded
    start = jnp.cumsum(counts) - counts
    dest = pad_start[sorted_e] + jnp.arange(nk) - start[sorted_e]
    n_blocks = -(-nk // MOE_BLOCK) + N_EXPERTS
    rows = n_blocks * MOE_BLOCK
    row_tok = jnp.full((rows,), n, jnp.int32).at[dest].set(flat_tok[order])
    row_gate = jnp.zeros((rows,), h.dtype).at[dest].set(gates.reshape(-1)[order])
    block_e = jnp.minimum(jnp.searchsorted(pad_end, jnp.arange(n_blocks) * MOE_BLOCK, side='right'), N_EXPERTS - 1)
    h_pad = jnp.concatenate([h, jnp.zeros((1, d), h.dtype)], axis=0)
    xb = h_pad[row_tok].reshape(n_blocks, MOE_BLOCK, d)

    def expert_block(args):
        xe, e = args
        hid = xe @ w1[e] + b1[e]
        gate = jnp.minimum(hid[:, :D_EXPERT], SWIGLU_LIMIT)
        up = jnp.clip(hid[:, D_EXPERT:], -SWIGLU_LIMIT, SWIGLU_LIMIT)
        act = gate * jax.nn.sigmoid(SWIGLU_ALPHA * gate) * (up + 1.0)
        return act @ w2[e] + b2[e]

    yb = lax.map(expert_block, (xb, block_e)).reshape(rows, d) * row_gate[:, None]
    return jnp.zeros((n + 1, d), h.dtype).at[row_tok].add(yb)[:n]

def hybrid_layer(x, p, s0, conv_buf, lw):
    B, L, D = x.shape
    h = rmsnorm(x, lw['norm1_g'])
    z = h @ lw['w_in']
    cuts = [int(c) for c in np.cumsum(IN_SIZES)[:-1]]
    qkv_pre, a_raw, b_raw, z_gate, gu, gv, m_a, m_b = jnp.split(z, cuts, axis=-1)
    y_a, s_new, buf_new = deltanet_branch(qkv_pre, a_raw, b_raw, z_gate, conv_buf, s0, lw['conv_w'],
                                          lw['a_log'], lw['dt_bias'], lw['dn_norm_g'], lw['w_proj_a'])
    y_b, v_rows = chunk_mlp_branch(gu, gv, lw['gm_ln_g'], lw['gm_ln_b'], lw['gm_ws'], lw['gm_bs'], lw['w_proj_b'])
    mixed = jax.nn.sigmoid(m_a) * y_a + jax.nn.sigmoid(m_b) * y_b
    x = x + mixed @ lw['w_out']
    h2 = rmsnorm(x, lw['norm2_g']).reshape(B * L, D)
    x = x + moe_ffn(h2, lw['router_w'], lw['router_b'], lw['moe_w1'], lw['moe_b1'],
                    lw['moe_w2'], lw['moe_b2']).reshape(B, L, D)
    h3 = rmsnorm(x, lw['norm3_g'])
    x = x + jax.nn.sigmoid(h3 @ lw['ple_gate_w']) * (p.astype(x.dtype) @ lw['ple_w'])
    return x, s_new, buf_new, v_rows

def setup_inputs(seed: int = 0) -> dict:
    key = jax.random.key(seed)
    ks = iter(jax.random.split(key, 40))

    def nrm(shape, scale):
        return jax.random.normal(next(ks), shape, jnp.float32) * scale

    a_log = jnp.log(jax.random.uniform(next(ks), (DEPTH, DN_HEADS), jnp.float32, 1.0, 16.0))
    dt = jnp.exp(jax.random.uniform(next(ks), (DEPTH, DN_HEADS), jnp.float32, math.log(1e-3), math.log(1e-1)))
    dt_bias = dt + jnp.log(-jnp.expm1(-dt))
    return {
        'x_prompt': nrm((BATCH, SEQ, D_MODEL), 1.0),
        'x_sample': nrm((DEC_BATCH, DEC_SEQ, D_MODEL), 1.0),
        'state_delta': nrm((DEPTH, DEC_BATCH, DN_HEADS, DN_DK, DN_DV), 0.5),
        'state_conv': nrm((DEPTH, DEC_BATCH, DN_CONV - 1, QKV_W), 1.0),
        'p_prompt': nrm((DEPTH, BATCH, SEQ, PLE_DIM), 1.0),
        'p_sample': nrm((DEPTH, DEC_BATCH, DEC_SEQ, PLE_DIM), 1.0),
        'norm1_g': 1.0 + nrm((DEPTH, D_MODEL), 0.02),
        'w_in': nrm((DEPTH, D_MODEL, IN_COLS), D_MODEL ** -0.5),
        'conv_w': nrm((DEPTH, DN_CONV, QKV_W), DN_CONV ** -0.5),
        'a_log': a_log,
        'dt_bias': dt_bias,
        'dn_norm_g': 1.0 + nrm((DEPTH, DN_DV), 0.02),
        'w_proj_a': nrm((DEPTH, V_W, D_MODEL), V_W ** -0.5),
        'gm_ln_g': 1.0 + nrm((DEPTH, GM_WIDTH), 0.02),
        'gm_ln_b': nrm((DEPTH, GM_WIDTH), 0.02),
        'gm_ws': nrm((DEPTH, GM_GROUPS, GM_CHUNK, GM_CHUNK), 0.5 * GM_CHUNK ** -0.5),
        'gm_bs': 1.0 + nrm((DEPTH, GM_GROUPS, GM_CHUNK), 0.02),
        'w_proj_b': nrm((DEPTH, GM_WIDTH, D_MODEL), GM_WIDTH ** -0.5),
        'w_out': nrm((DEPTH, D_MODEL, D_MODEL), D_MODEL ** -0.5),
        'norm2_g': 1.0 + nrm((DEPTH, D_MODEL), 0.02),
        'router_w': nrm((DEPTH, D_MODEL, N_EXPERTS), D_MODEL ** -0.5),
        'router_b': nrm((DEPTH, N_EXPERTS), 0.01),
        'moe_w1': nrm((DEPTH, N_EXPERTS, D_MODEL, 2 * D_EXPERT), D_MODEL ** -0.5),
        'moe_b1': nrm((DEPTH, N_EXPERTS, 2 * D_EXPERT), 0.01),
        'moe_w2': nrm((DEPTH, N_EXPERTS, D_EXPERT, D_MODEL), D_EXPERT ** -0.5),
        'moe_b2': nrm((DEPTH, N_EXPERTS, D_MODEL), 0.01),
        'norm3_g': 1.0 + nrm((DEPTH, D_MODEL), 0.02),
        'ple_w': nrm((DEPTH, PLE_DIM, D_MODEL), PLE_DIM ** -0.5),
        'ple_gate_w': nrm((DEPTH, D_MODEL, D_MODEL), D_MODEL ** -0.5),
        'final_norm_g': 1.0 + nrm((D_MODEL,), 0.02),
    }

def reference(x_prompt, x_sample, state_delta, state_conv, p_prompt, p_sample,
              norm1_g, w_in, conv_w, a_log, dt_bias, dn_norm_g, w_proj_a,
              gm_ln_g, gm_ln_b, gm_ws, gm_bs, w_proj_b, w_out, norm2_g,
              router_w, router_b, moe_w1, moe_b1, moe_w2, moe_b2,
              norm3_g, ple_w, ple_gate_w, final_norm_g):
    xp, xs = x_prompt, x_sample
    bp = x_prompt.shape[0]
    sd_p, sc_p, sd_s, sc_s, gv_s = [], [], [], [], []
    for i in range(DEPTH):
        lw = {
            'norm1_g': norm1_g[i], 'w_in': w_in[i], 'conv_w': conv_w[i], 'a_log': a_log[i],
            'dt_bias': dt_bias[i], 'dn_norm_g': dn_norm_g[i], 'w_proj_a': w_proj_a[i],
            'gm_ln_g': gm_ln_g[i], 'gm_ln_b': gm_ln_b[i], 'gm_ws': gm_ws[i], 'gm_bs': gm_bs[i],
            'w_proj_b': w_proj_b[i], 'w_out': w_out[i], 'norm2_g': norm2_g[i],
            'router_w': router_w[i], 'router_b': router_b[i], 'moe_w1': moe_w1[i],
            'moe_b1': moe_b1[i], 'moe_w2': moe_w2[i], 'moe_b2': moe_b2[i],
            'norm3_g': norm3_g[i], 'ple_w': ple_w[i], 'ple_gate_w': ple_gate_w[i],
        }
        s0_p = jnp.zeros((bp, DN_HEADS, DN_DK, DN_DV), jnp.float32)
        buf0_p = jnp.zeros((bp, DN_CONV - 1, QKV_W), xp.dtype)
        xp, s_p, b_p, _ = hybrid_layer(xp, p_prompt[i], s0_p, buf0_p, lw)
        xs, s_s, b_s, v_s = hybrid_layer(xs, p_sample[i], state_delta[i], state_conv[i], lw)
        sd_p.append(s_p)
        sc_p.append(b_p)
        sd_s.append(s_s)
        sc_s.append(b_s)
        gv_s.append(v_s)
    y_prompt = rmsnorm(xp, final_norm_g)
    y_sample = rmsnorm(xs, final_norm_g)
    new_state_delta_prompt = jnp.stack(sd_p, axis=0)
    new_state_conv_prompt = jnp.stack(sc_p, axis=0)
    new_state_delta_sample = jnp.stack(sd_s, axis=0)
    new_state_conv_sample = jnp.stack(sc_s, axis=0)
    new_gm_v_sample = jnp.stack(gv_s, axis=0)
    return (y_prompt, y_sample, new_state_delta_prompt, new_state_conv_prompt,
            new_state_delta_sample, new_state_conv_sample, new_gm_v_sample)


_drawn_inputs = setup_inputs


def setup_inputs(seed=0):
    import zlib

    import numpy as np

    out = dict(_drawn_inputs(seed))
    spreads = {}
    factors = {'dn_norm_g': 2.8,
     'gm_ln_g': 7.525,
     'gm_ln_b': 7.883,
     'router_b': 3.159,
     'moe_b1': 8.0,
     'moe_b2': 8.0,
     'norm3_g': 51.169,
     'final_norm_g': 8.469,
     'gm_bs': 3.61}
    for name, (base, spread) in spreads.items():
        noise = np.random.default_rng([zlib.crc32(name.encode()), seed]).standard_normal(out[name].shape)
        drawn = base * np.exp(spread * noise) if base else spread * noise
        out[name] = __import__('jax').numpy.asarray(drawn.astype(out[name].dtype))
    for name, factor in factors.items():
        out[name] = (out[name] * factor).astype(out[name].dtype)
    return out
```

```python
from contextlib import ExitStack

import numpy as np
import concourse.bass as bass
from concourse import mybir

F32 = mybir.dt.float32
BF16 = mybir.dt.bfloat16
I32 = mybir.dt.int32
U32 = mybir.dt.uint32
ALU = mybir.AluOpType
ACT = mybir.ActivationFunctionType
AX = mybir.AxisListType

P = 128
D = 1024
KD = D // P
SEQ, DB, DS = 256, 8, 8
TOK = SEQ + DB * DS
TILES = ((0, 128), (128, 128), (256, 64))
H = 8
QKV = 3 * D
FT = QKV // P
TAPS = 4
G = 8
NE, TOPK = 32, 4
SLOTS = 64
MAXB = NE + TOK * TOPK // SLOTS
PLE = 256
EPS = 1e-6
LIMIT, ALPHA = 7.0, 1.702
COL_AB, COL_GATE, COL_U, COL_V, COL_MA, COL_MB = 3072, 3088, 4112, 5136, 6160, 7184
LEVELS = (7, 7, 3)
FAR = 16384.0

CONST = {}


def _constants():
    i = np.arange(P)
    row, col = i[:, None], i[None, :]
    same8 = (row // DS == col // DS)
    parts = [("ident", row == col), ("ones", np.ones((P, P))),
             ("tri", col >= row), ("tri8", (col >= row) & same8), ("same8", same8),
             ("before", row < col)]
    for lev in range(7):
        n = 1 << lev
        parts.append((f"level{lev}", (row // (2 * n) == col // (2 * n)) & ((row // n) % 2 == 0) & ((col // n) % 2 == 1)))
    parts += [("seq8", row // DS == i[None, :DB]),
              ("slot", np.broadcast_to(i[None, :] % SLOTS, (P, P))),
              ("block", np.broadcast_to(i[None, :SLOTS], (P, SLOTS))),
              ("expert", np.broadcast_to(i[None, :NE], (P, NE))),
              ("eps", np.full((P, 1), EPS)), ("qscale", np.full((P, 1), -0.5 * np.log(128.0))),
              ("thr", np.broadcast_to(64.0 * np.arange(1, 5)[None, :], (P, 4))),
              ("eid", np.arange(P)[:, None] % NE)]
    at, out = 0, []
    for name, a in parts:
        CONST[name] = (at, a.shape[1])
        at += a.shape[1]
        out.append(np.asarray(a, np.float32))
    return np.ascontiguousarray(np.concatenate(out, axis=1))


CONSTS = _constants()
NCONST = CONSTS.shape[1]


def hybrid_layer(nc, t):
    ctx = ExitStack()
    with ctx:
        sems = {}

        def sem(name):
            if name not in sems:
                sems[name] = ctx.enter_context(nc.semaphore(name))
            return sems[name]

        arena_words = 53000
        arena = ctx.enter_context(nc.sbuf_tensor("arena", [P, arena_words], F32))
        top = [0]

        def region(words):
            at = top[0]
            top[0] += words
            assert top[0] <= arena_words, top[0]
            return at

        def view(at, *dims):
            n = int(np.prod(dims))
            v = arena[:, at:at + n]
            if len(dims) == 1:
                return v
            names = "abcd"[:len(dims)]
            return v.rearrange(f"p ({' '.join(names)}) -> p {' '.join(names)}",
                               **{k: d for k, d in zip(names, dims)})

        UNIT = 4096
        slot_at = [region(UNIT) for _ in range(6)]
        FRONT_SLOTS = 2
        scratch = slot_at[4]
        cst_at = region(NCONST)
        x_at = region(3 * D)
        hT_at = region(KD * TOK)
        qkv_at = region(FT * TOK)
        gate_at = region(KD * TOK)
        u_at = region(KD * TOK)
        v_at = region(3 * D)
        big_at = region(3 * D)
        small_at = region(1100)

        def cst(name, rows=P, cols=None):
            at, n = CONST[name]
            return arena[0:rows, cst_at + at:cst_at + at + (n if cols is None else cols)]

        ident = cst("ident")
        slots = [view(a, KD, 512) for a in slot_at]

        x = view(x_at, 3, D)
        hT = view(hT_at, KD, TOK)
        qkvT = view(qkv_at, FT, TOK)
        gateT = view(gate_at, KD, TOK)
        uT = view(u_at, KD, TOK)
        vtok = view(slot_at[2], 3, D)
        oT = view(qkv_at, H, TOK)
        maT = view(slot_at[2] + 3 * D, H, TOK)
        mbT = view(slot_at[2] + 3 * D + H * TOK, H, TOK)
        rs = view(slot_at[2], 2 * H, TOK)

        ZW = 3 + SEQ + DB * (3 + DS)
        CW = ZW - 3
        zpad = [view(scratch + i * ZW, ZW) for i in range(3)]
        cv = [view(scratch + (3 + i) * ZW, ZW) for i in range(2)]
        sg = [view(scratch + (5 + i) * ZW, ZW) for i in range(2)]
        last_at = scratch + 7 * ZW
        last3 = view(last_at, FT, 27)
        oldT = view(last_at + FT * 27, FT, 24)
        sc_rows = view(v_at, QKV)
        new_rows = view(big_at, QKV)
        sq = [view(last_at + FT * 51 + i * TOK, TOK) for i in range(2)]
        assert last_at + FT * 51 + 2 * TOK <= scratch + 8192

        def heads(at):
            return view(at, H, P)
        DBm, AT, mT, X, XT, W, rT, r = [heads(scratch + i * 1024) for i in range(8)]
        Al = [DBm, r]
        qd, kd, qS = [heads(x_at + i * 1024) for i in range(3)]
        GR, S, S0x = [heads(big_at + i * 1024) for i in range(3)]
        S0 = [view(v_at + i * 1024, DB, P) for i in range(3)] + [view(big_at + 2048, DB, P)]
        sgm = view(scratch, KD, TOK)
        bsb = view(scratch + 2560, G, P)
        wnat = view(scratch + 3584, G, P)
        wnat8 = view(scratch + 4608, G, 64)
        WT = view(scratch + 5120, G, P)
        WT8 = view(scratch + 6144, G, 64)
        stmp = view(scratch + 6656, 512)
        stmp2 = view(scratch + 7168, 512)
        lng = view(big_at, D)
        lnb = view(big_at + D, D)
        mixT = gateT

        sm = [small_at]

        def small(*dims):
            n = int(np.prod(dims))
            v = view(sm[0], *dims) if len(dims) > 1 else arena[:, sm[0]:sm[0] + n]
            sm[0] += n
            assert sm[0] <= small_at + 1100
            return v

        wab = small(KD, 16)
        rows_in = small(P)
        colsT = small(P)
        ssq = small(3)
        rstd = small(3)
        ab = small(3, 16)
        gg = small(3, 8)
        beta = small(3, 8)
        alog = small(8)
        dtb = small(8)
        gce = small(3, 16)
        dcol = small(3, 8)
        gend = small(3, 8)
        tA = small(3, 8)
        tB = small(3, 8)
        msum = small(3)
        mvar = small(3)
        mrs = small(3)
        g_conv = colsT[:, 0:FT * TAPS].rearrange("p (t f) -> p t f", f=FT)
        g1, g2, g3 = (colsT[:, 96 + 8 * i:104 + 8 * i] for i in range(3))
        dng = colsT[:, 120:121]

        mo = [hT_at]
        uslot3 = 5

        def moe(*dims):
            n = int(np.prod(dims))
            v = view(mo[0], *dims) if len(dims) > 1 else arena[:, mo[0]:mo[0] + n]
            mo[0] += n
            assert mo[0] <= small_at
            return v

        h2T = moe(KD, TOK)
        h2 = moe(3, D)
        rw = moe(KD, NE)
        rbias = moe(NE)
        b12 = moe(D + 2 * D)
        b12c = moe(D // 2 + D).bitcast(BF16)
        b12s = moe(D // 2 + D).bitcast(BF16)
        logit = moe(3, NE)
        top8 = moe(3, 8)
        idx8 = moe(3, 8)
        idxf = moe(3, 8)
        gates = moe(3, 8)
        gsum = moe(3)
        mask = moe(3, NE)
        gmat = moe(3, NE)
        pos = moe(3, NE)
        etmp = moe(3, NE)
        posT = moe(TOK)
        gmT = moe(TOK)
        cnt = moe(16)
        Eb = moe(SLOTS)
        Eb3 = moe(SLOTS // 2).bitcast(BF16)
        Eb3f = moe(SLOTS)
        posb = moe(3, SLOTS)
        gateb = moe(3, SLOTS)
        tabf = moe(160)
        tab = moe(160).bitcast(I32)
        Psel = moe(3, SLOTS)
        Pg = moe(3, P)
        PgT = moe(3 * P)
        xsel = moe(512)
        xselT = moe(KD, SLOTS)
        Ebc = moe(SLOTS // 2).bitcast(BF16)
        g_sb, u_sb, s_sb, a_sb = moe(512), moe(512), moe(512), moe(512)
        actT = moe(4, P)
        y_sb = moe(512)
        fng = view(slot_at[uslot3], D)
        ptok = view(slot_at[uslot3] + D, 3, PLE)
        pT = moe(2, TOK)
        h3T = h2T
        assert mo[0] <= small_at, (mo[0], small_at)

        ps = ctx.enter_context(nc.psum_tensor("ps", [P, 8, 512], F32))
        pj = [ps[:, 0, :], ps[:, 1, :]]

        def pair(b, n=P):
            return ps[:, b:b + 2, :].rearrange("p a (h c) -> p (a h) c", c=P)[:, :, 0:n]

        G01, G23, G45 = (lambda n=P: pair(2, n)), (lambda n=P: pair(4, n)), (lambda n=P: pair(6, n))

        w_in = t["w_in"][0].rearrange("(k p) n -> p k n", p=P)
        chunk_src = [w_in[:, :, c * 512:(c + 1) * 512] for c in range(6)]
        for col in (COL_GATE, COL_U, COL_V, COL_MA, COL_MB):
            chunk_src += [w_in[:, :, col + c * 512:col + (c + 1) * 512] for c in range(2)]
        for name in ("w_proj_a", "w_proj_b", "w_out"):
            w = t[name][0].rearrange("(k p) n -> p k n", p=P)
            chunk_src += [w[:, :, c * 512:(c + 1) * 512] for c in range(2)]
        NCH = len(chunk_src)
        C_GATE, C_U, C_V, C_MA, C_MB, C_PA, C_PB, C_WO = 6, 8, 10, 12, 14, 16, 18, 20
        landed = [sem(f"weights_landed{s}") for s in range(6)]
        used = [sem(f"weights_used{s}") for s in range(6)]

        N_QKV, N_AB, N_GATE, N_U, N_V, N_MA, N_MB, N_YA, N_YB, N_WO, N_END = (
            0, 24, 25, 33, 41, 47, 55, 63, 71, 79, 85)
        free_at = [4 * (c + 1) for c in range(6)]
        for n0, per in ((N_GATE, 4), (N_U, 4), (N_V, 3), (N_MA, 4), (N_MB, 4), (N_YA, 4), (N_YB, 4), (N_WO, 3)):
            free_at += [n0 + per, n0 + 2 * per]
        proj_done = sem("projection_done")
        bank_free = [sem("projection_bank0_free"), sem("projection_bank1_free")]

        def bank_wait(pe, n):
            if n >= 2:
                pe.wait_ge(bank_free[n % 2], n // 2)

        def evacuated(eng, n):
            eng.wait_ge(bank_free[n % 2], n // 2 + 1)

        def chunk_wait(eng, c):
            eng.wait_ge(landed[c % FRONT_SLOTS], 16 * (c // FRONT_SLOTS + 1))
        before = [len([c for c in range(NCH) if c % FRONT_SLOTS == s]) for s in range(6)]
        uslot = [(u + 2) % 6 for u in range(6)]

        class Chain:

            def __init__(self, eng, s):
                self.eng, self.s, self.n = eng, s, 0

            def __call__(self, ins):
                self.n += 1
                ins.then_inc(self.s, 1)

            def wait(self):
                self.eng.wait_ge(self.s, self.n)

            def link(self, ins):
                self(ins)
                self.wait()

        block = ctx.enter_context(nc.Block())

        @block.sync
        def _(sp):
            sp.dma_start(arena[:, cst_at:cst_at + NCONST], t["consts"]).then_inc(sem("consts_in"), 16)
            sp.dma_start(x[:, 0:2, :], t["x_prompt"][0].rearrange("(a p) d -> p a d", p=P)).then_inc(sem("x_in"), 16)
            sp.dma_start(x[0:64, 2, :], t["x_sample"].rearrange("b s d -> (b s) d")).then_inc(sem("x_in"), 16)
            sp.dma_start(rows_in[0:96, :], t["conv_w"][0].rearrange("t (f p) -> (t f) p", p=P)).then_inc(sem("rows_loaded"), 16)
            for i, name in enumerate(("norm1_g", "norm2_g", "norm3_g")):
                sp.dma_start(rows_in[96 + 8 * i:104 + 8 * i, :],
                             t[name][0].rearrange("(k p) -> k p", p=P)).then_inc(sem("rows_loaded"), 16)
            sp.dma_start(rows_in[120:121, :], t["dn_norm_g"]).then_inc(sem("rows_loaded"), 16)
            sp.dma_start(sc_rows[0:24, :], t["state_conv"][0].rearrange("b r n -> (b r) n")).then_inc(sem("rows_loaded"), 16)
            for c in range(FRONT_SLOTS):
                sp.dma_start(slots[c], chunk_src[c]).then_inc(landed[c], 16)
                if c == 0:
                    sp.dma_start(wab, w_in[:, :, COL_AB:COL_AB + 16]).then_inc(sem("ab_in"), 16)
                    sp.dma_start(alog, t["a_log"].broadcast_to([P, H])).then_inc(sem("ab_in"), 16)
                    sp.dma_start(dtb, t["dt_bias"].broadcast_to([P, H])).then_inc(sem("ab_in"), 16)

            def chunk(c):
                sp.wait_ge(proj_done, free_at[c - FRONT_SLOTS])
                sp.dma_start(slots[c % FRONT_SLOTS], chunk_src[c]).then_inc(landed[c % FRONT_SLOTS], 16)

            for c in range(FRONT_SLOTS, C_PA + 1):
                chunk(c)
            sp.wait_ge(sem("S_ready"), 2)
            sp.dma_start(t["out_sd_p"][0, 0].rearrange("h k v -> k h v"), S[:, :, :]).then_inc(sem("stored"), 16)
            for h in range(H):
                sp.wait_ge(sem("S0_new"), h + 1)
                sp.dma_start(t["out_sd_s"][0, :, h].rearrange("b k v -> k b v"), S0[h % 4]).then_inc(sem(f"S0_stored{h % 4}"), 16)
            chunk(C_PA + 1)
            sp.wait_ge(sem("o_normed"), 3)
            sp.wait_ge(sem("S0_product"), 2 * H)
            sp.wait_ge(sem("stored"), 16)
            sp.dma_start(lng, t["gm_ln_g"].broadcast_to([P, D])).then_inc(sem("mlp_in"), 16)
            sp.dma_start(lnb, t["gm_ln_b"].broadcast_to([P, D])).then_inc(sem("mlp_in"), 16)
            sp.dma_start(bsb.rearrange("p g t -> p (g t)"),
                         t["gm_bs"].rearrange("a g t -> a (g t)").broadcast_to([P, G * P])).then_inc(sem("mlp_in"), 16)
            sp.dma_start(wnat, t["gm_ws"][0].rearrange("g t s -> t g s")).then_inc(sem("mlp_in"), 16)
            sp.wait_ge(sem("wnat8_zero"), 1)
            for b in range(DB):
                sp.dma_start(wnat8[DS * b:DS * b + DS, :, DS * b:DS * b + DS],
                             t["gm_ws"][0, :, 0:DS, 0:DS].rearrange("g t s -> t g s")).then_inc(sem("mlp_in"), 16)
            sp.dma_start(x[:, 0:2, :], t["x_prompt"][0].rearrange("(a p) d -> p a d", p=P)).then_inc(sem("x_in"), 16)
            sp.dma_start(x[0:64, 2, :], t["x_sample"].rearrange("b s d -> (b s) d")).then_inc(sem("x_in"), 16)
            for c in range(C_PA + 2, NCH):
                chunk(c)
            sp.wait_ge(sem("vnorm_ready"), 3)
            sp.dma_start(t["out_gv"][0].rearrange("b s d -> (b s) d"), vtok[0:64, 2, :]).then_inc(sem("stored"), 16)
            sp.wait_ge(sem("merged"), KD)
            sp.dma_start(rw, t["router_w"][0].rearrange("(k p) e -> p k e", p=P)).then_inc(sem("router_in"), 16)
            sp.dma_start(rbias, t["router_b"].broadcast_to([P, NE])).then_inc(sem("router_in"), 16)
            sp.dma_start(b12[0:NE, 0:2 * D], t["moe_b1"][0]).then_inc(sem("router_in"), 16)
            sp.dma_start(b12[0:NE, 2 * D:3 * D], t["moe_b2"][0]).then_inc(sem("router_in"), 16)

            def unit_src(e, u):
                if u < 4:
                    return t["moe_w1"][0, e, u * 256:(u + 1) * 256, :].rearrange("(k p) n -> p k n", p=P)
                return t["moe_w2"][0, e, (u - 4) * 512:(u - 3) * 512, :].rearrange("(k p) n -> p k n", p=P)

            def unit_dst(u):
                return slots[uslot[u]].rearrange("p k n -> p (k n)").rearrange("p (k n) -> p k n", k=2 if u < 4 else 4)

            for u in range(6):
                s = uslot[u]
                if s < FRONT_SLOTS:
                    sp.wait_ge(proj_done, free_at[NCH - FRONT_SLOTS + s])
                elif u == 0:
                    sp.wait_ge(sem("merged"), KD)
                    sp.wait_ge(sem("stored"), 32)
                sp.dma_start(unit_dst(u), t["moe_w1"][0, 0, u * 256:(u + 1) * 256, :].rearrange("(k p) n -> p k n", p=P)
                             if u < 4 else unit_src(0, u)).then_inc(landed[s], 16)
            sp.wait_ge(sem("tables_ready"), 1)
            w1 = t["moe_w1"][0].rearrange("e (u k p) n -> (e u) p k n", u=4, p=P)
            w2 = t["moe_w2"][0].rearrange("e (u k p) n -> (e u) p k n", u=2, p=P)
            with sp.Fori(0, NE - 1) as e:
                through = sp.value_load(tab[0:1, bass.ds(96 + e, 1)], min_val=1, max_val=MAXB)
                for u in range(6):
                    s = uslot[u]
                    sp.wait_ge(used[s], through)
                    src = w1[bass.ds(e * 4 + 4 + u, 1)] if u < 4 else w2[bass.ds(e * 2 + 2 + u - 4, 1)]
                    sp.dma_start(unit_dst(u), src.rearrange("a p k n -> p (a k) n")).then_inc(landed[s], 16)
            wg = t["ple_gate_w"][0].rearrange("(k p) n -> p k n", p=P)
            nb = sp.value_load(tab[0:1, 96 + NE - 1:96 + NE], min_val=1, max_val=MAXB)
            for c in range(2):
                sp.wait_ge(used[uslot[c]], nb)
                sp.dma_start(slots[uslot[c]], wg[:, :, c * 512:(c + 1) * 512]).then_inc(landed[uslot[c]], 16)
            sp.wait_ge(used[uslot[2]], nb)
            sp.dma_start(slots[uslot[2]].rearrange("p k n -> p (k n)")[:, 0:2048].rearrange("p (k n) -> p k n", k=2),
                         t["ple_w"][0].rearrange("(k p) n -> p k n", p=P)).then_inc(landed[uslot[2]], 16)
            sp.wait_ge(used[uslot[3]], nb)
            sp.dma_start(ptok[:, 0:2, :], t["p_prompt"][0, 0].rearrange("(a p) d -> p a d", p=P)).then_inc(sem("ple_in"), 16)
            sp.dma_start(ptok[0:64, 2, :], t["p_sample"][0].rearrange("b s d -> (b s) d")).then_inc(sem("ple_in"), 16)
            sp.dma_start(fng, t["final_norm_g"].rearrange("(a d) -> a d", a=1).broadcast_to([P, D])).then_inc(sem("ple_in"), 16)
            for tt, (t0, tn) in enumerate(TILES):
                sp.wait_ge(sem("y_ready"), tt + 1)
                dst = t["out_yp"][0, t0:t0 + tn, :] if tt < 2 else t["out_ys"].rearrange("b s d -> (b s) d")
                sp.dma_start(dst, x[0:tn, tt, :]).then_inc(sem("stored"), 16)
            sp.wait_ge(sem("stored"), 16 * 5)
            sp.wait_ge(sem("newrows_stored"), 32)

        @block.gpsimd
        def _(pool):
            for i in range(3):
                pool.memset(zpad[i], 0.0).then_inc(sem("zpad_zero"), 1)
            pool.wait_ge(sem("zpad_zero"), 3)

            def fill_old(n):
                if n >= 3:
                    pool.wait_ge(sem("conv_done"), n - 2)
                    pool.wait_ge(sem("last3_done"), 2 * (n - 2))
                pool.wait_ge(sem("old_turned"), n // 4 + 1)
                zs = zpad[n % 3][:, 3 + SEQ:].rearrange("p (b j) -> p b j", b=DB)
                pool.tensor_copy(zs[:, :, 0:3], oldT[:, n, :].rearrange("p (b j) -> p b j", b=DB)).then_inc(sem("old_filled"), 1)

            def keep_last(n):
                evacuated(pool, n)
                zs = zpad[n % 3][:, 3 + SEQ:].rearrange("p (b j) -> p b j", b=DB)
                pool.tensor_copy(last3[:, n, 0:3], zpad[n % 3][:, SEQ:SEQ + 3]).then_inc(sem("last3_done"), 1)
                pool.tensor_copy(last3[:, n, 3:27].rearrange("p (b j) -> p b j", b=DB), zs[:, :, DS:DS + 3]).then_inc(sem("last3_done"), 1)

            fill_old(0)
            for n in range(FT):
                if n + 1 < FT:
                    fill_old(n + 1)
                keep_last(n)
                m = n - 2
                if 0 <= m < 2 * H:
                    pool.wait_ge(sem("silu_done"), 2 * (m + 1))
                    if m >= 2:
                        pool.wait_ge(sem("sumsq_done"), m - 1)
                    pool.tensor_tensor(sq[m % 2], qkvT[:, m, :], qkvT[:, m, :], ALU.mult).then_inc(sem("sq_ready"), 1)

            def load_state(i):
                pool.dma_start(S0[i % 4], t["state_delta"][0, :, i % H].rearrange("b k v -> k b v")).then_inc(sem(f"S0_in{i % 4}"), 16)

            pool.wait_ge(sem("newrows_ready"), 6)
            pool.dma_start(t["out_sc_p"][0, 0], new_rows[0:3, :]).then_inc(sem("newrows_stored"), 16)
            pool.dma_start(t["out_sc_s"][0].rearrange("b r n -> (b r) n"), new_rows[3:27, :]).then_inc(sem("newrows_stored"), 16)
            pool.wait_ge(sem("newrows_stored"), 32)
            pool.wait_ge(sem("old_turned"), 6)
            for i in range(4):
                load_state(i)
            for tt, (t0, tn) in enumerate(TILES):
                pool.wait_ge(sem("GR_ready"), tt + 1)
                pool.wait_ge(sem("qk_normed"), 2)
                if tt == 2:
                    pool.wait_ge(sem("kS_done"), 1)
                pool.tensor_tensor(qd[:, :, 0:tn], qkvT[:, 0:H, t0:t0 + tn], GR[:, :, 0:tn], ALU.mult).then_inc(sem("qd_ready"), 1)
                pool.wait_ge(sem("AT_ready"), tt + 1)
                pool.wait_ge(sem("mT_ready"), tt + 1)
                for lev in range(LEVELS[tt]):
                    done = sum(LEVELS[:tt]) + lev
                    if lev == 0 and tt:
                        pool.wait_ge(sem("u_done"), tt)
                    if lev >= 2:
                        pool.wait_ge(sem("W_done"), done - 1)
                    if lev == 2:
                        pool.wait_ge(sem("X_ready"), done - 1)
                    pool.tensor_tensor(Al[lev % 2][0:tn, :, 0:tn], AT[0:tn, :, 0:tn],
                                       cst(f"level{lev}", tn, tn).rearrange("p (a c) -> p a c", a=1).broadcast_to([tn, H, tn]),
                                       ALU.mult).then_inc(sem("Al_ready"), 1)
            for i in range(4, 12):
                pool.wait_ge(sem("kS_head"), i - 3)
                load_state(i)
            for h in range(H):
                if h >= 4:
                    pool.wait_ge(sem(f"S0_stored{h % 4}"), 16)
                    load_state(8 + h)
                pool.wait_ge(sem("u_ready"), 3)
                if h >= 2:
                    pool.wait_ge(sem("S0_product"), 2 * (h - 1))
                pool.tensor_tensor([X, XT][h % 2][0:64], W[0:64, h, :].rearrange("p (a c) -> p a c", a=1).broadcast_to([64, DB, P]),
                                   cst("seq8", 64).rearrange("p (a c) -> p a c", c=1).broadcast_to([64, DB, P]),
                                   ALU.mult).then_inc(sem("uexp_ready"), 1)
            pool.wait_ge(sem("o_normed"), 3)
            pool.wait_ge(sem("S0_product"), 2 * H)
            pool.memset(wnat8[0:64], 0.0).then_inc(sem("wnat8_zero"), 1)
            pool.wait_ge(sem("router_in"), 16 * 4)
            for n in (N_WO + 4, N_WO + 5):
                evacuated(pool, n)
            part0, part1 = b12s[0:NE, :], b12c[0:NE, :]
            link = lambda ins, n: (ins.then_inc(sem("bias_chain"), 1), pool.wait_ge(sem("bias_chain"), n))
            link(pool.tensor_copy(part0, b12[0:NE, :]), 1)
            link(pool.tensor_tensor(b12[0:NE, :], b12[0:NE, :], part0, ALU.subtract), 2)
            link(pool.tensor_copy(part1, b12[0:NE, :]), 3)
            pool.dma_start(b12s[32:64, :], part1).then_inc(sem("bias_moved"), 16)
            link(pool.tensor_tensor(b12[0:NE, :], b12[0:NE, :], part1, ALU.subtract), 4)
            pool.wait_ge(sem("bias_moved"), 16)
            link(pool.tensor_copy(part1, b12[0:NE, :]), 5)
            pool.dma_start(b12s[64:96, :], part1).then_inc(sem("bias_moved"), 16)

        @block.tensor
        def _(pe):
            def mm(out, lhsT, rhs, first, last):
                return pe.matmul(out, lhsT, rhs, start=first, stop=last, skip_group_check=True)

            pe.wait_ge(sem("consts_in"), 16)
            pe.wait_ge(sem("rows_loaded"), 16 * 6)
            pe.transpose(ps[:, 0, 0:121], rows_in[0:121, :], ident[0:121, 0:121]).then_inc(sem("rows_turned"), 1)
            for g in range(6):
                for i in range(4):
                    f = 4 * g + i
                    m = pe.transpose(ps[:, 2 + g, 24 * i:24 * i + 24], sc_rows[0:24, f * P:(f + 1) * P], ident[0:24, 0:24])
                m.then_inc(sem("old_done"), 1)
            pe.wait_ge(sem("xn_ready"), 3)
            pe.wait_ge(sem("cols_ready"), 1)
            for k in range(KD):
                if k >= 2:
                    pe.wait_ge(sem("hT_ready"), k - 1)
                for tt, (t0, tn) in enumerate(TILES):
                    m = pe.transpose(pj[k % 2][:, t0:t0 + tn], x[0:tn, tt, k * P:(k + 1) * P], ident[0:tn, 0:tn])
                m.then_inc(sem("hT_done"), 1)

            def features(n, c, m, rhs):
                chunk_wait(pe, c)
                bank_wait(pe, n)
                for k in range(KD):
                    last = mm(pj[n % 2][:, 0:TOK], slots[c % FRONT_SLOTS][:, k, m * P:(m + 1) * P], rhs[:, k, :], k == 0, k == KD - 1)
                last.then_inc(proj_done, 1)

            def rows(n, c, tt, lhs):
                t0, tn = TILES[tt]
                chunk_wait(pe, c)
                bank_wait(pe, n)
                for k in range(KD):
                    last = mm(pj[n % 2][0:tn, :], lhs[:, k, t0:t0 + tn], slots[c % FRONT_SLOTS][:, k, :], k == 0, k == KD - 1)
                last.then_inc(proj_done, 1)

            pe.wait_ge(sem("hT_ready"), KD)
            for n in range(FT):
                features(n, n // 4, n % 4, hT)
                m = n - 3
                if 0 <= m < 2 * H:
                    pe.wait_ge(sem("sq_ready"), m + 1)
                    if m >= 6:
                        pe.wait_ge(sem("ln_done"), m - 5)
                    else:
                        pe.wait_ge(sem("old_turned"), 6)
                    mm(ps[:, 2 + m % 6, 0:TOK], cst("ones"), sq[m % 2], True, True).then_inc(sem("sumsq_done"), 1)
            pe.wait_ge(sem("ab_in"), 48)
            bank_wait(pe, N_AB)
            for tt, (t0, tn) in enumerate(TILES):
                for k in range(KD):
                    last = mm(pj[0][0:tn, 16 * tt:16 * tt + 16], hT[:, k, t0:t0 + tn], wab[:, k, :], k == 0, k == KD - 1)
            last.then_inc(proj_done, 1)
            pe.wait_ge(sem("last3_done"), 2 * FT)
            pe.wait_ge(sem("ln_done"), 2 * H)
            for g in range(6):
                for i in range(4):
                    m = pe.transpose(ps[0:27, 2 + g, P * i:P * i + P], last3[:, 4 * g + i, :], ident)
                m.then_inc(sem("newrows_done"), 1)
            filled = [N_GATE]

            def fill(count=1):
                for _ in range(count):
                    n = filled[0]
                    filled[0] += 1
                    if n < N_V:
                        features(n, C_GATE + (n - N_GATE) // 4, (n - N_GATE) % 4, hT)
                    elif n < N_MA:
                        rows(n, C_V + (n - N_V) // 3, (n - N_V) % 3, hT)
                    else:
                        features(n, C_MA + (n - N_MA) // 4, (n - N_MA) % 4, hT)

            pe.wait_ge(sem("newrows_ready"), 6)
            pe.wait_ge(sem("g_ready"), 3)
            for tt, (t0, tn) in enumerate(TILES):
                mm(ps[0:tn, 7, 16 * tt:16 * tt + 8], cst("tri8" if tt == 2 else "tri", tn, tn), gg[0:tn, tt, :], True, True)
                m = mm(ps[0:tn, 7, 16 * tt + 8:16 * tt + 16], cst("same8" if tt == 2 else "ones", tn, tn), gg[0:tn, tt, :], True, True)
            m.then_inc(sem("cum_done"), 1)
            fill(3)
            pe.wait_ge(sem("qk_normed"), 2)
            pe.wait_ge(sem("silu_done"), 2 * FT)

            for tt, (t0, tn) in enumerate(TILES):
                L0 = sum(LEVELS[:tt])
                pe.wait_ge(sem("RH_ready"), tt + 1)
                if tt == 0:
                    pe.wait_ge(sem("gce_ready"), 1)
                else:
                    pe.wait_ge(sem("S_ready"), tt)
                for a in range(2):
                    m = mm(G45(tn)[:, 4 * a:4 * a + 4, :], cst("ones", tn), X[0:tn, 4 * a:4 * a + 4, 0:tn], True, True)
                m.then_inc(sem("gcrow_done"), 1)
                if tt:
                    pe.wait_ge(sem("ln_done"), 2 * H + tt)
                    pe.wait_ge(sem("o_ready"), tt)
                for h in range(H):
                    mm(G01(tn)[0:tn, h, :], qkvT[:, H + h, t0:t0 + tn], qkvT[:, H + h, t0:t0 + tn], True, True)
                    m = mm(G23(tn)[0:tn, h, :], qkvT[:, H + h, t0:t0 + tn], qkvT[:, h, t0:t0 + tn], True, True)
                m.then_inc(sem("kk_done"), 1)
                fill()
                pe.wait_ge(sem("AT_ready"), tt + 1)
                for h in range(H):
                    m = pe.transpose(G01()[0:tn, h, :], qkvT[:, H + h, t0:t0 + tn], ident)
                m.then_inc(sem("kt_done"), 1)
                fill()
                for lev in range(LEVELS[tt]):
                    i = L0 + lev
                    pe.wait_ge(sem("Al_ready"), i + 1)
                    if lev == 0:
                        pe.wait_ge(sem("dd_ready"), tt + 1)
                        pe.wait_ge(sem("GR_ready"), tt + 1)
                    else:
                        pe.wait_ge(sem("X_ready"), i)
                    for h in range(H):
                        rhs = ident[0:tn, 0:tn] if lev == 0 else X[0:tn, h, 0:tn]
                        m = mm(G45(tn)[0:tn, h, :], Al[lev % 2][0:tn, h, 0:tn], rhs, True, True)
                    m.then_inc(sem("W_done"), 1)
                    if lev or tt < 2:
                        fill()
                    if lev:
                        pe.wait_ge(sem("W_ready"), i - tt)
                        if lev == 1:
                            pe.wait_ge(sem("kd_ready"), tt + 1)
                            pe.wait_ge(sem("mT_ready"), tt + 1)
                        if lev < LEVELS[tt] - 1:
                            for h in range(H):
                                mm(G01(tn)[0:tn, h, :], XT[0:tn, h, 0:tn], W[0:tn, h, 0:tn], True, True)
                        for h in range(H):
                            m = mm(G23(tn)[0:tn, h, :], W[0:tn, h, 0:tn], XT[0:tn, h, 0:tn], True, True)
                        m.then_inc(sem("D_done"), 1)
                        if lev % 2 and tt < 2:
                            fill()
                if tt:
                    pe.wait_ge(sem("X_ready"), L0 + LEVELS[tt])
                    pe.wait_ge(sem("qd_ready"), tt + 1)
                if tt == 1:
                    for h in range(H):
                        mm(G01(tn)[:, h, :], S[:, h, :], qkvT[:, H + h, t0:t0 + tn], True, True)
                        m = mm(G23(tn)[:, h, :], S[:, h, :], qd[:, h, 0:tn], True, True)
                    m.then_inc(sem("kS_done"), 1)
                if tt == 2:
                    for h in range(H):
                        pe.wait_ge(sem(f"S0_in{h % 4}"), 16 * (h // 4 + 1))
                        for b in range(DB):
                            c0 = t0 + DS * b
                            mm(G01()[:, h, DS * b:DS * b + DS], S0[h % 4][:, b, :], qkvT[:, H + h, c0:c0 + DS], True, True)
                            m = mm(G23()[:, h, DS * b:DS * b + DS], S0[h % 4][:, b, :], qd[:, h, DS * b:DS * b + DS], True, True)
                        m.then_inc(sem("kS_head"), 1)
                pe.wait_ge(sem("rT_ready"), tt + 1)
                for h in range(H):
                    m = pe.transpose(G45()[0:tn, h, :], rT[:, h, 0:tn], ident)
                m.then_inc(sem("r_done"), 1)
                pe.wait_ge(sem("r_ready"), tt + 1)
                pe.wait_ge(sem("X_ready"), L0 + LEVELS[tt])
                for h in range(H):
                    m = mm(G01()[0:tn, h, :], XT[0:tn, h, 0:tn], r[0:tn, h, :], True, True)
                m.then_inc(sem("u_done"), 1)
                pe.wait_ge(sem("u_ready"), tt + 1)
                if tt:
                    pe.wait_ge(sem("qS_ready"), tt)
                for h in range(H):
                    m = mm(G23(tn)[:, h, :], W[0:tn, h, :], mT[0:tn, h, 0:tn], True, True)
                m.then_inc(sem("o_done"), 1)
                if tt < 2:
                    for h in range(H):
                        m = mm(G45()[:, h, :], kd[0:tn, h, :], W[0:tn, h, :], True, True)
                    m.then_inc(sem("S_done"), 1)
                fill()
                pe.wait_ge(sem("osq_ready"), tt + 1)
                for a in range(2):
                    m = mm(G01(tn)[:, 4 * a:4 * a + 4, :], cst("ones"), qS[:, 4 * a:4 * a + 4, 0:tn], True, True)
                m.then_inc(sem("sumsq_done"), 1)
            for h in range(H):
                pe.wait_ge(sem("uexp_ready"), h + 1)
                if h >= 2:
                    pe.wait_ge(sem("S0_new"), h - 1)
                elif h == 1:
                    pe.wait_ge(sem("o_ready"), 3)
                for a in range(2):
                    mm(ps[:, [6, 4][h % 2] + a, :], kd[0:64, h, :], [X, XT][h % 2][0:64, 4 * a:4 * a + 4, :], True, True).then_inc(sem("S0_product"), 1)
                if h % 2:
                    fill()
            assert filled[0] == N_YA

            pe.wait_ge(sem("mlp_in"), 16 * 12)
            for g in range(G):
                pe.transpose(G01()[:, g, :], wnat[:, g, :], ident)
            for g in range(G):
                m = pe.transpose(G23(64)[0:64, g, :], wnat8[0:64, g, :], ident[0:64, 0:64])
            m.then_inc(sem("wT_done"), 1)
            pe.wait_ge(sem("gated_ready"), 1)
            for i in range(8):
                features(N_YA + i, C_PA + i // 4, i % 4, oT)
            pe.wait_ge(sem("vnorm_ready"), 3)
            pe.wait_ge(sem("WT_ready"), 2)
            for tt, (t0, tn) in enumerate(TILES):
                for a in range(2):
                    for g in range(4 * a, 4 * a + 4):
                        wt = WT[:, g, :] if tt < 2 else WT8[0:64, g, :]
                        m = mm(ps[:, 2 + 2 * tt + a, P * (g % 4):P * (g % 4) + tn], vtok[0:tn, tt, g * P:(g + 1) * P], wt, True, True)
                    m.then_inc(sem("mix_done"), 1)
            pe.wait_ge(sem("us_ready"), 6)
            for i in range(8):
                features(N_YB + i, C_PB + i // 4, i % 4, uT)
            pe.wait_ge(sem("merged"), KD)
            for half in range(2):
                for tt in range(3):
                    rows(N_WO + 3 * half + tt, C_WO + half, tt, mixT)

            pe.wait_ge(sem("xn_ready"), 6)
            for k in range(KD):
                bank_wait(pe, N_END + k)
                for tt, (t0, tn) in enumerate(TILES):
                    m = pe.transpose(pj[(N_END + k) % 2][:, t0:t0 + tn], h2[0:tn, tt, k * P:(k + 1) * P], ident[0:tn, 0:tn])
                m.then_inc(sem("hT_done"), 1)
            evacuated(pe, N_END + 6)
            evacuated(pe, N_END + 7)
            pe.wait_ge(sem("router_in"), 16 * 4)
            for tt, (t0, tn) in enumerate(TILES):
                for k in range(KD):
                    m = mm(ps[0:tn, 5 + tt, 0:NE], h2T[:, k, t0:t0 + tn], rw[:, k, :], k == 0, k == KD - 1)
                m.then_inc(sem("logits_done"), 1)
            pe.wait_ge(sem("mask_ready"), 3)
            for tt, (t0, tn) in enumerate(TILES):
                for s in range(tt + 1):
                    lhs = cst("before", tn, tn) if s == tt else cst("ones", P, tn)
                    m = mm(ps[0:tn, 3, NE * tt:NE * tt + NE], lhs, mask[0:TILES[s][1], s, :], s == 0, s == tt)
            for tt, (t0, tn) in enumerate(TILES):
                m = mm(ps[0:NE, 4, 0:1], mask[0:tn, tt, :], cst("ones", tn, 1), tt == 0, tt == 2)
            m.then_inc(sem("rank_done"), 1)
            pe.wait_ge(sem("blocks_ready"), 1)
            mm(ps[0:NE, 4, 8:9], cst("tri", NE, NE), cnt[0:NE, 4:5], True, True).then_inc(sem("through_done"), 1)
            pe.wait_ge(sem("rank_ready"), 3)
            for tt, (t0, tn) in enumerate(TILES):
                pe.transpose(ps[0:NE, 5, t0:t0 + tn], pos[0:tn, tt, :], ident[0:tn, 0:tn])
                m = pe.transpose(ps[0:NE, 6, t0:t0 + tn], gmat[0:tn, tt, :], ident[0:tn, 0:tn])
            m.then_inc(sem("rankT_done"), 1)
            pe.wait_ge(sem("E_ready"), 1)
            pe.wait_ge(sem("rankT_ready"), 2)
            for tt, (t0, tn) in enumerate(TILES):
                mm(ps[0:tn, 7, SLOTS * tt:SLOTS * tt + SLOTS], posT[0:NE, t0:t0 + tn], Eb[0:NE, :], True, True)
                mm(ps[0:tn, 7, 256 + SLOTS * tt:256 + SLOTS * tt + SLOTS], gmT[0:NE, t0:t0 + tn], Eb[0:NE, :], True, True)
            mm(ps[0:1, 4, 128:192], cst("eid", NE), Eb[0:NE, :], True, True)
            mm(ps[0:1, 4, 192:224], cnt[0:NE, 5:6], ident[0:NE, 0:NE], True, True).then_inc(sem("perblock_done"), 1)

            def select(value):
                pe.wait_ge(sem("psel_ready"), value)
                for tt, (t0, tn) in enumerate(TILES):
                    for g in range(2):
                        m = mm(ps[64 * g:64 * g + 64, 3, :], Psel[0:tn, tt, :], h2[0:tn, tt, 512 * g:512 * g + 512], tt == 0, tt == 2)
                m.then_inc(sem("sel_done"), 1)

            def turn_rows(value):
                pe.wait_ge(sem("xsel_ready"), value)
                for j in range(4):
                    m = pe.transpose(ps[:, 5, P * j:P * j + P], xsel[:, P * j:P * j + P], ident)
                m.then_inc(sem("xT_done"), 1)

            def combine(tt, y_value, free_value):
                t0, tn = TILES[tt]
                if tt == 0:
                    pe.wait_ge(sem("ysb_ready"), y_value)
                    pe.wait_ge(sem("pgT_ready"), y_value)
                pe.wait_ge(sem("comb_free"), free_value)
                for g in range(2):
                    m = mm(ps[:, 6 + g, :], PgT[64 * g:64 * g + 64, t0:t0 + P], y_sb[64 * g:64 * g + 64, :], True, True)
                m.then_inc(sem("comb_done"), 1)

            pe.wait_ge(sem("tables_ready"), 1)
            nb = pe.value_load(tab[0:1, 96 + NE - 1:96 + NE], min_val=1, max_val=MAXB)
            pe.nop().then_inc(sem("pgT_done"), 1)
            select(1)
            turn_rows(1)
            pe.wait_ge(sem("bias_moved"), 32)
            pe.wait_ge(sem("bias_chain"), 5)
            with pe.Fori(0, nb) as b:
                e = pe.value_load(tab[0:1, bass.ds(b, 1)], min_val=0, max_val=NE - 1)
                hid_free = sem("hid_free")
                pe.wait_ge(hid_free, b + 1)
                pe.wait_ge(sem("xselT_ready"), b + 1)
                for u in range(4):
                    s = uslot[u]
                    w = slots[s].rearrange("p k n -> p (k n)").rearrange("p (k n) -> p k n", k=2)
                    pe.wait_ge(landed[s], e * 16 + 16 * (before[s] + 1))
                    for kk in range(2):
                        k = 2 * u + kk
                        for part in range(2):
                            for g in range(2):
                                c0 = 1024 * part + 512 * g
                                m = mm(ps[64 * g:64 * g + 64, part, :], xselT[:, k, :], w[:, kk, c0:c0 + 512], k == 0, False)
                    m.then_inc(used[s], 1)
                    if u < 3:
                        combine(u, b + 1, b * 3 + u + 1)
                pe.wait_ge(sem("ebc_ready"), b + 1)
                for part in range(2):
                    for g in range(2):
                        c0 = 1024 * part + 512 * g
                        m = mm(ps[64 * g:64 * g + 64, part, :], Ebc[0:96, :], b12s[0:96, c0:c0 + 512], False, True)
                m.then_inc(sem("hid_done"), 1)
                select(b + 2)
                turn_rows(b + 2)
                pe.wait_ge(sem("act_ready"), b + 1)
                for j in range(4):
                    m = pe.transpose(ps[:, 4, P * j:P * j + P], a_sb[:, P * j:P * j + P], ident)
                m.then_inc(sem("actT_done"), 1)
                pe.wait_ge(sem("actT_ready"), b + 1)
                for u in range(4, 6):
                    s = uslot[u]
                    w = slots[s].rearrange("p k n -> p (k n)").rearrange("p (k n) -> p k n", k=4)
                    pe.wait_ge(landed[s], e * 16 + 16 * (before[s] + 1))
                    for kk in range(4):
                        k = 4 * (u - 4) + kk
                        for g in range(2):
                            m = mm(ps[64 * g:64 * g + 64, 2, :], actT[:, k % 4, 64 * (k // 4):64 * (k // 4) + 64],
                                   w[:, kk, 512 * g:512 * g + 512], k == 0, False)
                    m.then_inc(used[s], 1)
                for g in range(2):
                    c0 = 2048 + 512 * g
                    m = mm(ps[64 * g:64 * g + 64, 2, :], Ebc[0:96, :], b12s[0:96, c0:c0 + 512], False, True)
                m.then_inc(sem("y_done"), 1)
                pe.wait_ge(sem("pg_ready"), b + 1)
                for tt, (t0, tn) in enumerate(TILES):
                    m = pe.transpose(ps[:, 4, t0:t0 + tn], Pg[0:tn, tt, :], ident[0:tn, 0:tn])
                m.then_inc(sem("pgT_done"), 1)
            for tt in range(3):
                combine(tt, nb + 1, nb * 3 + tt + 1)

            pe.wait_ge(sem("ple_in"), 48)
            pe.wait_ge(sem("xn_ready"), 9)
            for k in range(KD + 2):
                if k >= 2:
                    pe.wait_ge(sem("hT_ready"), KD + k - 1)
                for tt, (t0, tn) in enumerate(TILES):
                    src = h2[0:tn, tt, k * P:(k + 1) * P] if k < KD else ptok[0:tn, tt, (k - KD) * P:(k - KD + 1) * P]
                    m = pe.transpose(ps[:, k % 2, t0:t0 + tn], src, ident[0:tn, 0:tn])
                m.then_inc(sem("hT_done"), 1)
            pe.wait_ge(sem("hT_ready"), 2 * KD + 2)
            pe.wait_ge(landed[uslot[2]], 16 * (before[uslot[2]] + NE + 1))
            for half in range(2):
                s = uslot[half]
                pe.wait_ge(landed[s], 16 * (before[s] + NE + 1))
                for tt, (t0, tn) in enumerate(TILES):
                    n = 3 * half + tt
                    if n >= 2:
                        pe.wait_ge(sem("ple_added"), n - 1)
                    for k in range(KD):
                        m = mm(ps[0:tn, 2 + n % 2, :], h3T[:, k, t0:t0 + tn], slots[s][:, k, :], k == 0, k == KD - 1)
                    m.then_inc(sem("ple_done"), 1)
                    wp = slots[uslot[2]].rearrange("p k n -> p (k n)")[:, 0:2048].rearrange("p (k n) -> p k n", k=2)
                    for k in range(2):
                        m = mm(ps[0:tn, 4 + n % 2, :], pT[:, k, t0:t0 + tn], wp[:, k, 512 * half:512 * half + 512], k == 0, k == 1)
                    m.then_inc(sem("ple_done"), 1)

        @block.scalar
        def _(act):
            ch = Chain(act, sem("act_chain"))
            ACTF = nc.scalar.activation

            act.wait_ge(sem("x_in"), 32)
            act.wait_ge(sem("consts_in"), 16)
            act.wait_ge(sem("zeroed"), 4)
            for tt, (t0, tn) in enumerate(TILES):
                ch(ACTF(view(qkv_at + tt * D, D)[0:tn], x[0:tn, tt, :], ACT.Square, accum_out=ssq[0:tn, tt:tt + 1]))
            ch.wait()
            ACTF(rstd, ssq, ACT.Sqrt, bias=cst("eps"), scale=1.0 / D).then_inc(sem("rms_ready"), 1)
            act.wait_ge(sem("cols_ready"), 1)
            for k in range(KD):
                act.wait_ge(sem("hT_done"), k + 1)
                ACTF(hT[:, k, :], pj[k % 2][:, 0:TOK], ACT.Copy, scale=g1[:, k:k + 1]).then_inc(sem("hT_ready"), 1)

            def silu_part(n):
                act.wait_ge(sem("conv_done"), n + 1)
                if n >= 2:
                    act.wait_ge(sem("silu_done"), 2 * (n - 1))
                ACTF(sg[n % 2][:, 0:CW], cv[n % 2][:, 0:CW], ACT.Sigmoid).then_inc(sem("sig_done"), 1)

            act.wait_ge(sem("zpad_zero"), 3)
            for n in range(FT):
                act.wait_ge(proj_done, n + 1)
                if n >= 3:
                    act.wait_ge(sem("conv_done"), n - 2)
                    act.wait_ge(sem("last3_done"), 2 * (n - 2))
                zs = zpad[n % 3][:, 3 + SEQ:].rearrange("p (b j) -> p b j", b=DB)
                ACTF(zs[:, :, 3:3 + DS], pj[n % 2][:, SEQ:TOK].rearrange("p (b j) -> p b j", b=DB), ACT.Copy)
                ACTF(zpad[n % 3][:, 3:3 + SEQ], pj[n % 2][:, 0:SEQ], ACT.Copy).then_inc(bank_free[n % 2], 1)
                if n:
                    silu_part(n - 1)
                m = n - 4
                if 0 <= m < 2 * H:
                    act.wait_ge(sem("sumsq_done"), m + 1)
                    ACTF(rs[:, m, :], ps[:, 2 + m % 6, 0:TOK], ACT.Copy).then_inc(sem("ln_done"), 1)
            silu_part(FT - 1)
            act.wait_ge(sem("ab_in"), 48)
            act.wait_ge(sem("abs_ready"), 1)
            ch(ACTF(alog, alog, ACT.Exp))
            ch(ACTF(beta, beta, ACT.Exp, scale=-1.0))
            ch.link(ACTF(tB, tB, ACT.Exp, scale=-1.0))
            ACTF(tB, tB, ACT.Ln, bias=1.0).then_inc(sem("softplus_ready"), 1)
            act.wait_ge(sem("ln_done"), 2 * H)
            ch.link(ACTF(rs, rs, ACT.Ln, bias=cst("eps")))
            ACTF(rs[:, 0:H], rs[:, 0:H], ACT.Exp, bias=cst("qscale"), scale=-0.5).then_inc(sem("rs_ready"), 1)
            ACTF(rs[:, H:2 * H], rs[:, H:2 * H], ACT.Exp, scale=-0.5).then_inc(sem("rs_ready"), 1)

            left = [N_GATE]

            def keep(count=1):
                for _ in range(count):
                    n = left[0]
                    left[0] += 1
                    act.wait_ge(proj_done, n + 1)
                    if N_V <= n < N_MA:
                        half, tt = divmod(n - N_V, 3)
                        tn = TILES[tt][1]
                        if n == N_V:
                            act.wait_ge(sem("qk_normed"), 2)
                        ACTF(vtok[0:tn, tt, 512 * half:512 * half + 512], pj[n % 2][0:tn, :], ACT.Copy).then_inc(bank_free[n % 2], 1)
                    else:
                        dst = gateT if n < N_U else uT if n < N_V else maT if n < N_MB else mbT
                        i = (n - N_GATE) % 8 if n < N_V else (n - N_MA) % 8
                        ACTF(dst[:, i, :], pj[n % 2][:, 0:TOK], ACT.Copy).then_inc(bank_free[n % 2], 1)

            act.wait_ge(sem("gce_ready"), 1)
            ch(ACTF(dcol, dcol, ACT.Exp))
            ch.link(ACTF(gend, gend, ACT.Exp))
            keep(3)
            act.wait_ge(sem("newrows_stored"), 32)

            for tt, (t0, tn) in enumerate(TILES):
                L0 = sum(LEVELS[:tt])
                act.wait_ge(sem("gcrow_done"), tt + 1)
                if tt:
                    act.wait_ge(sem("qd_ready"), tt)
                    act.wait_ge(sem("rT_ready"), tt)
                ACTF(GR[:, :, 0:tn], G45(tn), ACT.Exp).then_inc(sem("GR_ready"), 1)
                act.wait_ge(sem("dd_ready"), tt + 1)
                ACTF(DBm[0:tn, :, 0:tn], DBm[0:tn, :, 0:tn], ACT.Exp).then_inc(sem("dec_ready"), 1)
                keep()
                act.wait_ge(sem("kt_done"), tt + 1)
                act.wait_ge(sem("dcol_ready"), 1)
                for h in range(H):
                    m = ACTF(kd[0:tn, h, :], G01()[0:tn, h, :], ACT.Copy, scale=dcol[0:tn, tt, h:h + 1])
                m.then_inc(sem("kd_ready"), 1)
                keep()
                for lev in range(LEVELS[tt]):
                    i = L0 + lev
                    if lev:
                        act.wait_ge(sem("W_done"), i + 1)
                        ACTF(W[0:tn, :, 0:tn], G45(tn)[0:tn], ACT.Copy).then_inc(sem("W_ready"), 1)
                    if lev or tt < 2:
                        keep(2 if lev % 2 and tt < 2 else 1)
                act.wait_ge(sem("r_done"), tt + 1)
                ACTF(r[0:tn], G45()[0:tn], ACT.Copy).then_inc(sem("r_ready"), 1)
                act.wait_ge(sem("u_done"), tt + 1)
                ACTF(W[0:tn], G01()[0:tn], ACT.Copy).then_inc(sem("u_ready"), 1)
                keep()
                act.wait_ge(sem("sumsq_done"), 2 * H + tt + 1)
                ACTF(rT[:, :, 0:tn], G01(tn), ACT.Ln, bias=cst("eps"), scale=1.0 / P).then_inc(sem("ln_done"), 1)
                act.wait_ge(sem("ln_done"), 2 * H + tt + 1)
                ACTF(rT[:, :, 0:tn], rT[:, :, 0:tn], ACT.Exp, scale=-0.5).then_inc(sem("rs_ready"), 1)

            act.wait_ge(sem("o_normed"), 3)
            keep()
            ACTF(sgm, gateT, ACT.Sigmoid).then_inc(sem("branch_sig_ready"), 1)
            keep(3)
            assert left[0] == N_YA
            for n in (N_YA - 1, N_YA - 2):
                evacuated(act, n)
            for tt, (t0, tn) in enumerate(TILES):
                ACTF(vtok[0:tn, tt, :], vtok[0:tn, tt, :], ACT.Gelu, accum_out=msum[0:tn, tt:tt + 1]).then_inc(sem("gelu_ready"), 1)
            ACTF(uT, uT, ACT.Gelu).then_inc(sem("ugelu_ready"), 1)

            for tt, (t0, tn) in enumerate(TILES):
                act.wait_ge(sem("vc_ready"), tt + 1)
                ch.link(ACTF(view(scratch + 6656, D)[0:tn], vtok[0:tn, tt, :], ACT.Square, accum_out=mvar[0:tn, tt:tt + 1]))
            ACTF(mrs, mvar, ACT.Sqrt, bias=cst("eps"), scale=1.0 / D).then_inc(sem("ln_std_ready"), 1)
            ACTF(maT, maT, ACT.Sigmoid).then_inc(sem("branch_sig_ready"), 1)
            ACTF(mbT, mbT, ACT.Sigmoid).then_inc(sem("branch_sig_ready"), 1)

            def rms(ready):
                for tt, (t0, tn) in enumerate(TILES):
                    ready(tt)
                    ch(ACTF(h2[0:tn, tt, :], x[0:tn, tt, :], ACT.Square, accum_out=ssq[0:tn, tt:tt + 1]))
                ch.wait()
                ACTF(rstd, ssq, ACT.Sqrt, bias=cst("eps"), scale=1.0 / D).then_inc(sem("rms_ready"), 1)

            rms(lambda tt: evacuated(act, N_WO + 3 + tt))
            for k in range(KD):
                n = N_END + k
                act.wait_ge(sem("hT_done"), KD + k + 1)
                ACTF(h2T[:, k, :], pj[n % 2][:, 0:TOK], ACT.Copy, scale=g2[:, k:k + 1]).then_inc(bank_free[n % 2], 1)
            for tt, (t0, tn) in enumerate(TILES):
                act.wait_ge(sem("top_ready"), tt + 1)
                ACTF(gates[0:tn, tt, 0:TOPK], top8[0:tn, tt, 0:TOPK], ACT.Exp, bias=gates[0:tn, tt, 7:8],
                     accum_out=gsum[0:tn, tt:tt + 1]).then_inc(sem("gexp_ready"), 1)

            act.wait_ge(sem("tables_ready"), 1)
            nb = act.value_load(tab[0:1, 96 + NE - 1:96 + NE], min_val=1, max_val=MAXB)

            def rows_out(value):
                act.wait_ge(sem("sel_done"), value)
                ACTF(xsel, ps[:, 3, :], ACT.Copy).then_inc(sem("xsel_ready"), 1)

            rows_out(1)
            with act.Fori(0, nb) as b:
                act.wait_ge(sem("glu_gate_ready"), b + 1)
                ACTF(s_sb, g_sb, ACT.Sigmoid, scale=ALPHA).then_inc(sem("glu_sig_ready"), 1)
                rows_out(b + 2)
                act.wait_ge(sem("actT_done"), b + 1)
                ACTF(actT.rearrange("p j c -> p (j c)"), ps[:, 4, :], ACT.Copy).then_inc(sem("actT_ready"), 1)
                act.wait_ge(sem("y_done"), b + 1)
                ACTF(y_sb, ps[:, 2, :], ACT.Copy).then_inc(sem("ysb_ready"), 1)
                act.wait_ge(sem("pgT_done"), b + 2)
                ACTF(PgT[:, 0:TOK], ps[:, 4, 0:TOK], ACT.Copy).then_inc(sem("pgT_ready"), 1)

            rms(lambda tt: act.wait_ge(sem("comb_free"), nb * 3 + 4))
            for k in range(KD + 2):
                act.wait_ge(sem("hT_done"), 2 * KD + k + 1)
                if k < KD:
                    m = ACTF(h3T[:, k, :], ps[:, k % 2, 0:TOK], ACT.Copy, scale=g3[:, k:k + 1])
                else:
                    m = ACTF(pT[:, k - KD, :], ps[:, k % 2, 0:TOK], ACT.Copy)
                m.then_inc(sem("hT_ready"), 1)
            for n in range(6):
                tn = TILES[n % 3][1]
                act.wait_ge(sem("ple_done"), 2 * n + 1)
                if n >= 2:
                    act.wait_ge(sem("ple_added"), n - 1)
                ACTF([g_sb, u_sb][n % 2][0:tn], ps[0:tn, 2 + n % 2, :], ACT.Sigmoid).then_inc(sem("ple_sig_ready"), 1)
            rms(lambda tt: act.wait_ge(sem("ple_added"), 4 + tt))

        @block.vector
        def _(dve):
            ch = Chain(dve, sem("dve_chain"))
            TT, TS, STT = dve.tensor_tensor, dve.tensor_scalar, dve.scalar_tensor_tensor

            def over_heads(ap, rows, n):
                return ap.rearrange("p (a c) -> p a c", a=1).broadcast_to([rows, H, n])

            dve.memset(ssq, 1.0).then_inc(sem("zeroed"), 1)
            dve.memset(mvar, 1.0).then_inc(sem("zeroed"), 1)
            dve.memset(msum, 0.0).then_inc(sem("zeroed"), 1)
            dve.memset(ab, 0.0).then_inc(sem("zeroed"), 1)
            dve.wait_ge(sem("rows_turned"), 1)
            dve.tensor_copy(colsT[:, 0:121], ps[:, 0, 0:121]).then_inc(sem("cols_ready"), 1)
            for g in range(6):
                dve.wait_ge(sem("old_done"), g + 1)
                dve.tensor_copy(oldT[:, 4 * g:4 * g + 4, :], ps[:, 2 + g, 0:96].rearrange("p (f j) -> p f j", f=4)).then_inc(sem("old_turned"), 1)

            def normalise(k, dst):
                dve.wait_ge(sem("rms_ready"), k)
                ch.link(dve.reciprocal(rstd, rstd))
                for tt, (t0, tn) in enumerate(TILES):
                    yield TS(dst[0:tn, tt, :], x[0:tn, tt, :], rstd[0:tn, tt:tt + 1], None, ALU.mult)

            for m in normalise(1, x):
                m.then_inc(sem("xn_ready"), 1)

            def samples(w):
                return w[:, 3 + SEQ:3 + SEQ + DB * (3 + DS)].rearrange("p (b j) -> p b j", b=DB)[:, :, 0:DS]

            def silu_mul(n):
                dve.wait_ge(sem("sig_done"), n + 1)
                TT(qkvT[:, n, 0:SEQ], cv[n % 2][:, 0:SEQ], sg[n % 2][:, 0:SEQ], ALU.mult).then_inc(sem("silu_done"), 1)
                TT(qkvT[:, n, SEQ:TOK].rearrange("p (b j) -> p b j", b=DB), samples(cv[n % 2]), samples(sg[n % 2]),
                   ALU.mult).then_inc(sem("silu_done"), 1)

            dve.wait_ge(sem("cols_ready"), 1)
            for n in range(FT):
                evacuated(dve, n)
                dve.wait_ge(sem("old_filled"), n + 1)
                z, a = zpad[n % 3], cv[n % 2][:, 0:CW]
                if n >= 2:
                    dve.wait_ge(sem("silu_done"), 2 * (n - 1))
                ch.link(TS(a, z[:, 0:CW], g_conv[:, 0, n:n + 1], None, ALU.mult))
                for i in range(1, TAPS - 1):
                    ch.link(STT(a, z[:, i:i + CW], g_conv[:, i, n:n + 1], a, ALU.mult, ALU.add))
                STT(a, z[:, TAPS - 1:TAPS - 1 + CW], g_conv[:, TAPS - 1, n:n + 1], a, ALU.mult, ALU.add).then_inc(sem("conv_done"), 1)
                if n:
                    silu_mul(n - 1)
            silu_mul(FT - 1)

            dve.wait_ge(proj_done, N_AB + 1)
            dve.wait_ge(sem("zeroed"), 4)
            dve.wait_ge(sem("ab_in"), 48)
            ch(dve.tensor_copy(ab[0:64, 2, :], pj[0][0:64, 32:48]))
            dve.tensor_copy(ab[:, 0:2, :], pj[0][:, 0:32].rearrange("p (a c) -> p a c", a=2)).then_inc(bank_free[0], 1)
            evacuated(dve, N_AB)
            ch.wait()

            def wide8(ap):
                return ap.rearrange("p (a c) -> p a c", a=1).broadcast_to([P, 3, 8])
            ch(TS(beta, ab[:, :, 8:16], -80.0, None, ALU.max))
            ch.link(TT(tA, ab[:, :, 0:8], wide8(dtb), ALU.add))
            ch.link(TS(tB, tA, -1.0, None, ALU.mult))
            TT(tB, tB, tA, ALU.max).then_inc(sem("abs_ready"), 1)
            dve.wait_ge(sem("softplus_ready"), 1)
            ch(TS(beta, beta, 1.0, None, ALU.add))
            ch.link(STT(tA, tA, 0.0, tB, ALU.max, ALU.add))
            ch(dve.reciprocal(beta, beta))
            STT(gg, tA, -1.0, wide8(alog), ALU.mult, ALU.mult).then_inc(sem("g_ready"), 3)

            for g in range(6):
                dve.wait_ge(sem("newrows_done"), g + 1)
                dve.tensor_copy(new_rows[0:27, 512 * g:512 * g + 512], ps[0:27, 2 + g, :]).then_inc(sem("newrows_ready"), 1)
            for i in range(2):
                dve.wait_ge(sem("rs_ready"), i + 1)
                TT(qkvT[:, H * i:H * i + H, :], qkvT[:, H * i:H * i + H, :], rs[:, H * i:H * i + H, :], ALU.mult).then_inc(sem("qk_normed"), 1)
            dve.memset(gce, 0.0).then_inc(sem("zeroed"), 1)
            dve.wait_ge(sem("zeroed"), 5)
            dve.wait_ge(sem("cum_done"), 1)
            ch(dve.tensor_copy(gce[0:64, 2, :], ps[0:64, 7, 32:48]))
            ch.link(dve.tensor_copy(gce[:, 0:2, :], ps[:, 7, 0:32].rearrange("p (a c) -> p a c", a=2)))
            ch(dve.tensor_copy(gend, gce[:, :, 8:16]))
            TT(dcol, gce[:, :, 8:16], gce[:, :, 0:8], ALU.subtract).then_inc(sem("gce_ready"), 1)

            for tt, (t0, tn) in enumerate(TILES):
                L0 = sum(LEVELS[:tt])
                tri = cst("tri8" if tt == 2 else "tri", tn, tn)
                if tt:
                    dve.wait_ge(sem("u_done"), tt)
                else:
                    dve.wait_ge(sem("g_ready"), 3)
                    dve.wait_ge(sem("newrows_ready"), 6)
                TT(X[0:tn, :, 0:tn], over_heads(tri, tn, tn),
                   gg[0:tn, tt, :].rearrange("p (a c) -> p a c", c=1).broadcast_to([tn, H, tn]), ALU.mult).then_inc(sem("RH_ready"), 1)
                dve.wait_ge(sem("GR_ready"), tt + 1)
                if tt:
                    dve.wait_ge(sem("X_ready"), L0)
                for h in range(H):
                    m = TS(DBm[0:tn, h, 0:tn], G45(tn)[0:tn, h, :], gce[0:tn, tt, h:h + 1], 0.0, ALU.subtract, ALU.min)
                m.then_inc(sem("dd_ready"), 1)
                if tt == 0:
                    dve.wait_ge(sem("act_chain"), 9)
                    TT(dcol, dcol, beta, ALU.mult).then_inc(sem("dcol_ready"), 1)
                dve.wait_ge(sem("dec_ready"), tt + 1)
                for h in range(H):
                    m = STT(DBm[0:tn, h, 0:tn], DBm[0:tn, h, 0:tn], beta[0:tn, tt, h:h + 1], tri, ALU.mult, ALU.mult)
                ch.link(m)
                dve.wait_ge(sem("kk_done"), tt + 1)
                if tt:
                    dve.wait_ge(sem("o_done"), tt)
                    dve.wait_ge(sem("Al_ready"), L0)
                TT(AT[0:tn, :, 0:tn], G01(tn)[0:tn], DBm[0:tn, :, 0:tn], ALU.mult).then_inc(sem("AT_ready"), 1)
                TT(mT[0:tn, :, 0:tn], G23(tn)[0:tn], DBm[0:tn, :, 0:tn], ALU.mult).then_inc(sem("mT_ready"), 1)
                for lev in range(LEVELS[tt]):
                    i = L0 + lev
                    last = lev == LEVELS[tt] - 1
                    if lev == 0:
                        dve.wait_ge(sem("Al_ready"), i + 1)
                        dve.wait_ge(sem("W_done"), i + 1)
                        ch(TT(XT[0:tn, :, 0:tn], over_heads(cst("ident", tn, tn), tn, tn), Al[0][0:tn, :, 0:tn], ALU.subtract))
                        TT(X[0:tn, :, 0:tn], over_heads(cst("ident", tn, tn), tn, tn), G45(tn)[0:tn], ALU.subtract).then_inc(sem("X_ready"), 1)
                    else:
                        dve.wait_ge(sem("D_done"), i - tt)
                        dve.wait_ge(sem("X_ready"), i)
                        if not last:
                            ch(TT(X[0:tn, :, 0:tn], X[0:tn, :, 0:tn], G01(tn)[0:tn], ALU.subtract))
                        TT(XT[0:tn, :, 0:tn], XT[0:tn, :, 0:tn], G23(tn)[0:tn], ALU.subtract).then_inc(sem("X_ready"), 1)
                vT = qkvT[:, 2 * H:3 * H, t0:t0 + tn]
                if tt == 0:
                    dve.tensor_copy(rT[:, :, 0:tn], vT).then_inc(sem("rT_ready"), 1)
                else:
                    if tt == 1:
                        dve.wait_ge(sem("kS_done"), 1)
                    else:
                        dve.wait_ge(sem("kS_head"), H)
                    ch.link(TT(rT[:, :, 0:tn], G01(tn), GR[:, :, 0:tn], ALU.mult))
                    TT(rT[:, :, 0:tn], vT, rT[:, :, 0:tn], ALU.subtract).then_inc(sem("rT_ready"), 1)
                    dve.tensor_copy(qS[:, :, 0:tn], G23(tn)).then_inc(sem("qS_ready"), 1)
                o = oT[:, :, t0:t0 + tn]
                dve.wait_ge(sem("o_done"), tt + 1)
                dve.wait_ge(sem("qd_ready"), tt + 1)
                if tt == 0:
                    ch.link(dve.tensor_copy(o, G23(tn)))
                else:
                    dve.wait_ge(sem("qS_ready"), tt)
                    ch.link(TT(o, qS[:, :, 0:tn], G23(tn), ALU.add))
                TT(qS[:, :, 0:tn], o, o, ALU.mult).then_inc(sem("osq_ready"), 1)
                dve.wait_ge(sem("osq_ready"), tt + 1)
                dve.nop().then_inc(sem("o_ready"), 1)
                if tt == 0:
                    dve.wait_ge(sem("S_done"), 1)
                    dve.tensor_copy(S, G45()).then_inc(sem("S_ready"), 1)
                elif tt == 1:
                    dve.wait_ge(sem("S_done"), 2)
                    dve.wait_ge(sem("S_ready"), 1)
                    for h in range(H):
                        m = STT(S[:, h, :], S[:, h, :], gend[:, 1, h:h + 1], G45()[:, h, :], ALU.mult, ALU.add)
                    m.then_inc(sem("S_ready"), 1)
                dve.wait_ge(sem("rs_ready"), 2 + tt + 1)
                TT(o, o, rT[:, :, 0:tn], ALU.mult).then_inc(sem("o_normed"), 1)
            for h in range(H):
                dve.wait_ge(sem(f"S0_in{h % 4}"), 16 * (3 + h // 4))
                ch.link(TT(S0[h % 4], S0[h % 4], GR[:, h, DS - 1:64:DS].rearrange("p (a c) -> p a c", c=1).broadcast_to([P, DB, P]),
                           ALU.mult))
                dve.wait_ge(sem("S0_product"), 2 * h + 2)
                bank = [6, 4][h % 2]
                TT(S0[h % 4].rearrange("p b v -> p (b v)"), S0[h % 4].rearrange("p b v -> p (b v)"),
                   ps[:, bank:bank + 2, :].rearrange("p a c -> p (a c)"), ALU.add).then_inc(sem("S0_new"), 1)

            dve.wait_ge(sem("gelu_ready"), 3)
            ch.link(TS(msum, msum, 1.0 / D, None, ALU.mult))
            for tt, (t0, tn) in enumerate(TILES):
                TS(vtok[0:tn, tt, :], vtok[0:tn, tt, :], msum[0:tn, tt:tt + 1], None, ALU.subtract).then_inc(sem("vc_ready"), 1)
            dve.wait_ge(sem("ln_std_ready"), 1)
            ch.link(dve.reciprocal(mrs, mrs))
            dve.wait_ge(sem("mlp_in"), 16 * 12)
            dve.wait_ge(sem("vc_ready"), 3)
            for tt, (t0, tn) in enumerate(TILES):
                ch.link(STT(vtok[0:tn, tt, :], vtok[0:tn, tt, :], mrs[0:tn, tt:tt + 1], lng[0:tn], ALU.mult, ALU.mult))
                TT(vtok[0:tn, tt, :], vtok[0:tn, tt, :], lnb[0:tn], ALU.add).then_inc(sem("vnorm_ready"), 1)
            dve.wait_ge(sem("branch_sig_ready"), 1)
            dve.wait_ge(sem("o_normed"), 3)
            ch(TT(gateT, gateT, sgm, ALU.mult))
            ch.wait()
            STT(oT, oT, dng, gateT, ALU.mult, ALU.mult).then_inc(sem("gated_ready"), 1)
            dve.wait_ge(sem("wT_done"), 1)
            TT(WT, G01(), over_heads(cst("tri"), P, P), ALU.mult).then_inc(sem("WT_ready"), 1)
            TT(WT8[0:64], G23(64)[0:64], over_heads(cst("tri8", 64, 64), 64, 64), ALU.mult).then_inc(sem("WT_ready"), 1)

            def merge_a(i):
                n = N_YA + i
                dve.wait_ge(proj_done, n + 1)
                dve.wait_ge(sem("gated_ready"), 1)
                TT(mixT[:, i, :], maT[:, i, :], pj[n % 2][:, 0:TOK], ALU.mult).then_inc(bank_free[n % 2], 1)

            dve.wait_ge(sem("branch_sig_ready"), 3)
            for i in range(8):
                merge_a(i)
            dve.wait_ge(sem("ugelu_ready"), 1)
            for tt, (t0, tn) in enumerate(TILES):
                for a in range(2):
                    k = 2 * tt + a
                    dve.wait_ge(sem("mix_done"), k + 1)
                    sv = ps[:, 2 + k, :].rearrange("p (g c) -> p g c", g=4)[:, :, 0:tn]
                    st = [stmp, stmp2][k % 2].rearrange("p (g c) -> p g c", g=4)[:, :, 0:tn]
                    if k >= 2:
                        dve.wait_ge(sem("us_ready"), k - 1)
                    if tt < 2:
                        ch.link(TT(st, sv, bsb[:, 4 * a:4 * a + 4, :], ALU.add))
                    else:
                        for g in range(4):
                            bias = bsb[:, 4 * a + g, 0:DS].rearrange("p (b j) -> p b j", b=1).broadcast_to([P, DB, DS])
                            m = TT(st[:, g, :].rearrange("p (b j) -> p b j", b=DB), sv[:, g, :].rearrange("p (b j) -> p b j", b=DB), bias, ALU.add)
                        ch.link(m)
                    TT(uT[:, 4 * a:4 * a + 4, t0:t0 + tn], uT[:, 4 * a:4 * a + 4, t0:t0 + tn], st, ALU.mult).then_inc(sem("us_ready"), 1)
            dve.wait_ge(sem("us_ready"), 6)
            for i in range(8):
                n = N_YB + i
                dve.wait_ge(proj_done, n + 1)
                evacuated(dve, N_YA + 6)
                evacuated(dve, N_YA + 7)
                tmp = [stmp, stmp2][i % 2][:, 0:TOK]
                if i >= 2:
                    dve.wait_ge(sem("merged"), i - 1)
                TT(tmp, mbT[:, i, :], pj[n % 2][:, 0:TOK], ALU.mult).then_inc(bank_free[n % 2], 1)
                evacuated(dve, n)
                TT(mixT[:, i, :], mixT[:, i, :], tmp, ALU.add).then_inc(sem("merged"), 1)
            dve.wait_ge(sem("x_in"), 64)
            for half in range(2):
                for tt, (t0, tn) in enumerate(TILES):
                    n = N_WO + 3 * half + tt
                    dve.wait_ge(proj_done, n + 1)
                    xa = x[0:tn, tt, 512 * half:512 * half + 512]
                    TT(xa, xa, pj[n % 2][0:tn, :], ALU.add).then_inc(bank_free[n % 2], 1)

            for n in (N_WO + 4, N_WO + 5):
                evacuated(dve, n)
            for m in normalise(2, h2):
                m.then_inc(sem("xn_ready"), 1)
            dve.wait_ge(sem("router_in"), 16 * 4)
            ex = cst("expert")
            for tt, (t0, tn) in enumerate(TILES):
                R = slice(0, tn)
                dve.wait_ge(sem("logits_done"), tt + 1)
                ch.link(TT(logit[R, tt, :], ps[R, 5 + tt, 0:NE], rbias[R], ALU.add))
                ch.link(dve.max(top8[R, tt, :], logit[R, tt, :]))
                ch(dve.max_index(idx8[R, tt, :].bitcast(U32), top8[R, tt, :], logit[R, tt, :]))
                TS(gates[R, tt, 7:8], top8[R, tt, 0:1], -1.0, None, ALU.mult).then_inc(sem("top_ready"), 1)
                ch.wait()
                ch(dve.tensor_copy(idxf[R, tt, :], idx8[R, tt, :].bitcast(U32)))
                ch.link(dve.memset(mask[R, tt, :], 0.0))
                for k in range(TOPK):
                    ch.link(STT(mask[R, tt, :], ex[R], idxf[R, tt, k:k + 1], mask[R, tt, :], ALU.is_equal, ALU.add))
                dve.nop().then_inc(sem("mask_ready"), 1)
                dve.wait_ge(sem("gexp_ready"), tt + 1)
                ch.link(dve.reciprocal(gsum[R, tt:tt + 1], gsum[R, tt:tt + 1]))
                ch.link(TS(gates[R, tt, 0:TOPK], gates[R, tt, 0:TOPK], gsum[R, tt:tt + 1], None, ALU.mult))
                ch.link(TS(gmat[R, tt, :], ex[R], idxf[R, tt, 0:1], gates[R, tt, 0:1], ALU.is_equal, ALU.mult))
                for k in range(1, TOPK):
                    ch.link(TS(etmp[R, tt, :], ex[R], idxf[R, tt, k:k + 1], gates[R, tt, k:k + 1], ALU.is_equal, ALU.mult))
                    ch.link(TT(gmat[R, tt, :], gmat[R, tt, :], etmp[R, tt, :], ALU.add))
            dve.wait_ge(sem("rank_done"), 1)
            q = slice(0, NE)
            ch.link(dve.tensor_copy(cnt[q, 8:9], ps[q, 4, 0:1]))
            ch.link(TS(cnt[q, 0:4], cst("thr", NE), cnt[q, 8:9], None, ALU.is_lt))
            ch.link(dve.tensor_reduce(cnt[q, 9:10], cnt[q, 0:4], AX.X, ALU.add))
            TS(cnt[q, 4:5], cnt[q, 9:10], 1.0, None, ALU.add).then_inc(sem("blocks_ready"), 1)
            for tt, (t0, tn) in enumerate(TILES):
                R = slice(0, tn)
                ch.link(TS(etmp[R, tt, :], mask[R, tt, :], -FAR, FAR, ALU.mult, ALU.add))
                TT(pos[R, tt, :], etmp[R, tt, :], ps[R, 3, NE * tt:NE * tt + NE], ALU.add).then_inc(sem("rank_ready"), 1)
            dve.wait_ge(sem("through_done"), 1)
            dve.wait_ge(sem("blocks_ready"), 1)
            ch.link(dve.tensor_copy(cnt[q, 5:6], ps[q, 4, 8:9]))
            ch.link(TT(cnt[q, 6:7], cnt[q, 5:6], cnt[q, 4:5], ALU.subtract))
            ch.link(TS(cnt[q, 7:8], cnt[q, 6:7], float(SLOTS), None, ALU.mult))
            ch.link(TS(Eb3f[q], cst("block", NE), cnt[q, 5:6], None, ALU.is_lt))
            ch.link(STT(Eb[q], cst("block", NE), cnt[q, 6:7], Eb3f[q], ALU.is_ge, ALU.mult))
            for i in range(3):
                m = dve.tensor_copy(Eb3[32 * i:32 * i + 32, :], Eb[q])
                ch(m)
            ch.wait()
            dve.nop().then_inc(sem("E_ready"), 1)
            dve.wait_ge(sem("rankT_done"), 1)
            TS(posT[q], ps[q, 5, 0:TOK], cnt[q, 7:8], None, ALU.add).then_inc(sem("rankT_ready"), 1)
            dve.tensor_copy(gmT[q], ps[q, 6, 0:TOK]).then_inc(sem("rankT_ready"), 1)
            dve.wait_ge(sem("perblock_done"), 1)
            for tt, (t0, tn) in enumerate(TILES):
                R = slice(0, tn)
                ch(STT(posb[R, tt, :], cst("block", tn), -float(SLOTS), ps[R, 7, SLOTS * tt:SLOTS * tt + SLOTS], ALU.mult, ALU.add))
                ch(dve.tensor_copy(gateb[R, tt, :], ps[R, 7, 256 + SLOTS * tt:256 + SLOTS * tt + SLOTS]))
            ch(dve.tensor_copy(tab[0:1, 0:64], ps[0:1, 4, 128:192]))
            ch.link(dve.tensor_copy(tab[0:1, 96:128], ps[0:1, 4, 192:224]))
            dve.nop().then_inc(sem("tables_ready"), 1)

            dve.memset(y_sb, 0.0).then_inc(sem("ysb_ready"), 1)
            dve.memset(PgT, 0.0).then_inc(sem("pgT_ready"), 1)
            dve.nop().then_inc(sem("hid_free"), 1)
            dve.nop().then_inc(sem("comb_free"), 1)
            nb = dve.value_load(tab[0:1, 96 + NE - 1:96 + NE], min_val=1, max_val=MAXB)

            def pick(b):
                for tt, (t0, tn) in enumerate(TILES):
                    m = TS(Psel[0:tn, tt, :], cst("slot", tn, SLOTS), posb[0:tn, tt, bass.ds(b, 1)] if not isinstance(b, int)
                           else posb[0:tn, tt, b:b + 1], None, ALU.is_equal)
                m.then_inc(sem("psel_ready"), 1)

            def rows_turned(value):
                dve.wait_ge(sem("xT_done"), value)
                TT(xselT.rearrange("p (g j) s -> p g j s", g=2), ps[:, 5, :].rearrange("p (j g s) -> p g j s", j=4, g=2),
                   g2.rearrange("p (g j a) -> p g j a", g=2, a=1).broadcast_to([P, 2, 4, SLOTS]), ALU.mult).then_inc(sem("xselT_ready"), 1)

            pick(0)
            rows_turned(1)
            with dve.Fori(0, nb) as b:
                dve.wait_ge(sem("pgT_done"), b + 1)
                dve.tensor_copy(Ebc[0:96, :], Eb3[0:96, bass.ds(b, 1)].broadcast_to([96, SLOTS])).then_inc(sem("ebc_ready"), 1)
                for tt, (t0, tn) in enumerate(TILES):
                    m = TS(Pg[0:tn, tt, :], cst("slot", tn), posb[0:tn, tt, bass.ds(b, 1)], gateb[0:tn, tt, bass.ds(b, 1)], ALU.is_equal, ALU.mult)
                m.then_inc(sem("pg_ready"), 1)
                dve.wait_ge(sem("sel_done"), b + 1)
                pick(b + 1)
                for tt, (t0, tn) in enumerate(TILES):
                    dve.wait_ge(sem("comb_done"), b * 3 + tt + 1)
                    dve.wait_ge(sem("comb_free"), b * 3 + 1)
                    TT(x[0:tn, tt, :], x[0:tn, tt, :], ps[0:tn, 6:8, :].rearrange("p a c -> p (a c)"), ALU.add).then_inc(sem("comb_free"), 1)
                dve.wait_ge(sem("hid_done"), b + 1)
                TS(g_sb, ps[:, 0, :], LIMIT, None, ALU.min).then_inc(sem("glu_gate_ready"), 1)
                TS(u_sb, ps[:, 1, :], LIMIT, -LIMIT, ALU.min, ALU.max).then_inc(sem("hid_free"), 1)
                dve.wait_ge(sem("hid_free"), b + 2)
                STT(u_sb, u_sb, 1.0, g_sb, ALU.add, ALU.mult).then_inc(sem("glu_up_ready"), 1)
                dve.wait_ge(sem("glu_up_ready"), b + 1)
                dve.wait_ge(sem("glu_sig_ready"), b + 1)
                TT(a_sb, u_sb, s_sb, ALU.mult).then_inc(sem("act_ready"), 1)
                rows_turned(b + 2)
            for tt, (t0, tn) in enumerate(TILES):
                dve.wait_ge(sem("comb_done"), nb * 3 + tt + 1)
                dve.wait_ge(sem("comb_free"), nb * 3 + 1)
                TT(x[0:tn, tt, :], x[0:tn, tt, :], ps[0:tn, 6:8, :].rearrange("p a c -> p (a c)"), ALU.add).then_inc(sem("comb_free"), 1)

            dve.wait_ge(sem("comb_free"), nb * 3 + 4)
            for m in normalise(3, h2):
                m.then_inc(sem("xn_ready"), 1)
            for n in range(6):
                tt, half = n % 3, n // 3
                tn = TILES[tt][1]
                dve.wait_ge(sem("ple_sig_ready"), n + 1)
                dve.wait_ge(sem("ple_done"), 2 * n + 2)
                s_ = [g_sb, u_sb][n % 2][0:tn]
                xa = x[0:tn, tt, 512 * half:512 * half + 512]
                ch.link(TT(s_, s_, ps[0:tn, 4 + n % 2, :], ALU.mult))
                TT(xa, xa, s_, ALU.add).then_inc(sem("ple_added"), 1)
            dve.wait_ge(sem("ple_added"), 6)
            gen = normalise(4, x)
            for tt, m in enumerate(gen):
                ch.link(m)
                tn = TILES[tt][1]
                TT(x[0:tn, tt, :], x[0:tn, tt, :], fng[0:tn], ALU.mult).then_inc(sem("y_ready"), 1)


INS = ("x_prompt", "x_sample", "state_delta", "state_conv", "p_prompt", "p_sample", "norm1_g", "w_in", "conv_w",
       "a_log", "dt_bias", "dn_norm_g", "w_proj_a", "gm_ln_g", "gm_ln_b", "gm_ws", "gm_bs", "w_proj_b", "w_out",
       "norm2_g", "router_w", "router_b", "moe_w1", "moe_b1", "moe_w2", "moe_b2", "norm3_g", "ple_w", "ple_gate_w",
       "final_norm_g")
OUTS = (("out_yp", (1, SEQ, D)), ("out_ys", (DB, DS, D)), ("out_sd_p", (1, 1, H, P, P)), ("out_sc_p", (1, 1, TAPS - 1, QKV)),
        ("out_sd_s", (1, DB, H, P, P)), ("out_sc_s", (1, DB, TAPS - 1, QKV)), ("out_gv", (1, DB, DS, D)))


def kernel(**inputs):
    import concourse.bacc as bacc
    from concourse.bass_utils import run_bass_kernel_spmd

    nc = bacc.Bacc("TRN2", target_bir_lowering=False, num_devices=1)
    arrays, tensors = {}, {}
    for name in INS:
        a = np.ascontiguousarray(inputs[name])
        arrays[f"in_{name}"] = a
        tensors[name] = nc.dram_tensor(f"in_{name}", a.shape, mybir.dt.from_np(a.dtype), kind="ExternalInput").ap()
    arrays["in_consts"] = CONSTS
    tensors["consts"] = nc.dram_tensor("in_consts", CONSTS.shape, F32, kind="ExternalInput").ap()
    for name, shape in OUTS:
        tensors[name] = nc.dram_tensor(name, shape, F32, kind="ExternalOutput").ap()
    hybrid_layer(nc, tensors)
    r = run_bass_kernel_spmd(nc, [arrays], core_ids=[0])
    return tuple(r.results[0][name] for name, _ in OUTS)
```

```python
from contextlib import ExitStack

import numpy as np
import concourse.bass as bass
from concourse import mybir

F32 = mybir.dt.float32
BF16 = mybir.dt.bfloat16
I32 = mybir.dt.int32
U32 = mybir.dt.uint32
ALU = mybir.AluOpType
ACT = mybir.ActivationFunctionType
AX = mybir.AxisListType

P = 128
D = 1024
KD = D // P
SEQ, DB, DS = 256, 8, 8
TOK = SEQ + DB * DS
TILES = ((0, 128), (128, 128), (256, 64))
H = 8
QKV = 3 * D
FT = QKV // P
TAPS = 4
G = 8
NE, TOPK = 32, 4
SLOTS = 64
MAXB = NE + TOK * TOPK // SLOTS
PLE = 256
EPS = 1e-6
LIMIT, ALPHA = 7.0, 1.702
COL_AB, COL_GATE, COL_U, COL_V, COL_MA, COL_MB = 3072, 3088, 4112, 5136, 6160, 7184
HB = 64
LEVELS = (7, 7, 3)
FAR = 16384.0

CONST = {}


def _constants():
    i = np.arange(P)
    row, col = i[:, None], i[None, :]
    same8 = (row // DS == col // DS)
    parts = [("ident", row == col), ("ones", np.ones((P, P))),
             ("tri", col >= row), ("tri8", (col >= row) & same8), ("same8", same8),
             ("before", row < col)]
    row64, col64 = row % HB, col[:, :HB]
    parts.append(("ident64", row64 == col64))
    for lev in range(6):
        n = 1 << lev
        parts.append((f"level{lev}", (row64 // (2 * n) == col64 // (2 * n)) & ((row64 // n) % 2 == 0) & ((col64 // n) % 2 == 1)))
    parts += [("seq8", row % 64 // DS == i[None, :DB]),
              ("slot", np.broadcast_to(i[None, :] % SLOTS, (P, P))),
              ("block", np.broadcast_to(i[None, :SLOTS], (P, SLOTS))),
              ("expert", np.broadcast_to(i[None, :NE], (P, NE))),
              ("eps", np.full((P, 1), EPS)), ("qscale", np.full((P, 1), -0.5 * np.log(128.0))),
              ("thr", np.broadcast_to(64.0 * np.arange(1, 5)[None, :], (P, 4))),
              ("eid", np.arange(P)[:, None] % NE)]
    at, out = 0, []
    for name, a in parts:
        CONST[name] = (at, a.shape[1])
        at += a.shape[1]
        out.append(np.asarray(a, np.float32))
    return np.ascontiguousarray(np.concatenate(out, axis=1))


CONSTS = _constants()
NCONST = CONSTS.shape[1]


def hybrid_layer(nc, t):
    ctx = ExitStack()
    with ctx:
        sems = {}

        def sem(name):
            if name not in sems:
                sems[name] = ctx.enter_context(nc.semaphore(name))
            return sems[name]

        arena_words = 53000
        arena = ctx.enter_context(nc.sbuf_tensor("arena", [P, arena_words], F32))
        top = [0]

        def region(words):
            at = top[0]
            top[0] += words
            assert top[0] <= arena_words, top[0]
            return at

        def view(at, *dims):
            n = int(np.prod(dims))
            v = arena[:, at:at + n]
            if len(dims) == 1:
                return v
            names = "abcd"[:len(dims)]
            return v.rearrange(f"p ({' '.join(names)}) -> p {' '.join(names)}",
                               **{k: d for k, d in zip(names, dims)})

        UNIT = 4096
        slot_at = [region(UNIT) for _ in range(6)]
        FRONT_SLOTS = 2
        scratch = slot_at[4]
        cst_at = region(NCONST)
        x_at = region(3 * D)
        hT_at = region(KD * TOK)
        qkv_at = region(FT * TOK)
        gate_at = region(KD * TOK)
        u_at = region(KD * TOK)
        v_at = region(3 * D)
        big_at = region(3 * D)
        small_at = region(1100)

        def cst(name, rows=P, cols=None):
            at, n = CONST[name]
            return arena[0:rows, cst_at + at:cst_at + at + (n if cols is None else cols)]

        ident = cst("ident")
        slots = [view(a, KD, 512) for a in slot_at]

        x = view(x_at, 3, D)
        hT = view(hT_at, KD, TOK)
        qkvT = view(qkv_at, FT, TOK)
        gateT = view(gate_at, KD, TOK)
        uT = view(u_at, KD, TOK)
        vtok = view(slot_at[2], 3, D)
        oT = view(qkv_at, H, TOK)
        maT = view(slot_at[2] + 3 * D, H, TOK)
        mbT = view(slot_at[2] + 3 * D + H * TOK, H, TOK)
        rs = view(slot_at[2], 2 * H, TOK)

        ZW = 3 + SEQ + DB * (3 + DS)
        CW = ZW - 3
        zpad = [view(scratch + i * ZW, ZW) for i in range(3)]
        cv = [view(scratch + (3 + i) * ZW, ZW) for i in range(2)]
        sg = [view(scratch + (5 + i) * ZW, ZW) for i in range(2)]
        last_at = scratch + 7 * ZW
        last3 = view(last_at, FT, 27)
        oldT = view(last_at + FT * 27, FT, 24)
        sc_rows = view(v_at, QKV)
        new_rows = view(big_at, QKV)
        sq = [view(last_at + FT * 51 + i * TOK, TOK) for i in range(2)]
        assert last_at + FT * 51 + 2 * TOK <= scratch + 8192

        def heads(at):
            return view(at, H, P)
        DBm, _, mT, X, XT, W, rT, r = [heads(scratch + i * 1024) for i in range(8)]
        half_heads = lambda at: view(at, H, HB)
        Al = [half_heads(scratch), half_heads(scratch + 7 * 1024)]
        ATd = half_heads(scratch + 1024)
        AToff = half_heads(scratch + 1536)
        Xd = half_heads(scratch + 3 * 1024)
        XTd = half_heads(scratch + 3 * 1024 + 512)
        Wd = half_heads(scratch + 5 * 1024)
        qd, kd, qS = [heads(x_at + i * 1024) for i in range(3)]
        GR, S, S0x = [heads(big_at + i * 1024) for i in range(3)]
        S0 = [view(v_at + i * 1024, DB, P) for i in range(3)] + [view(big_at + 2048, DB, P)]
        sgm = view(scratch, KD, TOK)
        bsb = view(scratch + 2560, G, P)
        wnat = view(scratch + 3584, G, P)
        wnat8 = view(scratch + 4608, G, 64)
        WT = view(scratch + 5120, G, P)
        WT8 = view(scratch + 6144, G, 64)
        stmp = view(scratch + 6656, 512)
        stmp2 = view(scratch + 7168, 512)
        lng = view(big_at, D)
        lnb = view(big_at + D, D)
        moved = view(big_at, 512)[0:64, 0:256]
        mixT = gateT

        sm = [small_at]

        def small(*dims):
            n = int(np.prod(dims))
            v = view(sm[0], *dims) if len(dims) > 1 else arena[:, sm[0]:sm[0] + n]
            sm[0] += n
            assert sm[0] <= small_at + 1100
            return v

        wab = small(KD, 16)
        rows_in = small(P)
        colsT = small(P)
        ssq = small(3)
        rstd = small(3)
        ab = small(3, 16)
        gg = small(3, 8)
        beta = small(3, 8)
        alog = small(8)
        dtb = small(8)
        gce = small(3, 16)
        dcol = small(3, 8)
        gend = small(3, 8)
        kdec = small(8)
        tA = small(3, 8)
        tB = small(3, 8)
        msum = small(3)
        mvar = small(3)
        mrs = small(3)
        g_conv = colsT[:, 0:FT * TAPS].rearrange("p (t f) -> p t f", f=FT)
        g1, g2, g3 = (colsT[:, 96 + 8 * i:104 + 8 * i] for i in range(3))
        dng = colsT[:, 120:121]

        mo = [hT_at]
        uslot3 = 5

        def moe(*dims):
            n = int(np.prod(dims))
            if mo[0] < big_at and mo[0] + n > v_at:
                mo[0] = big_at
            v = view(mo[0], *dims) if len(dims) > 1 else arena[:, mo[0]:mo[0] + n]
            mo[0] += n
            assert mo[0] <= small_at
            return v

        h2T = moe(KD, TOK)
        h2 = moe(3, D)
        rw = moe(KD, NE)
        rbias = moe(NE)
        b12 = moe(D + 2 * D)
        b12c = arena[:, v_at:v_at + 3 * D // 2].bitcast(BF16)
        b12s = arena[:, v_at + 3 * D // 2:v_at + 3 * D].bitcast(BF16)
        logit = moe(3, NE)
        top8 = moe(3, 8)
        idx8 = moe(3, 8)
        idxf = moe(3, 8)
        gates = moe(3, 8)
        gsum = moe(3)
        mask = moe(3, NE)
        gmat = moe(3, NE)
        pos = moe(3, NE)
        etmp = moe(3, NE)
        chosen = moe(3 * TOPK * NE)
        chosen_g = moe(3 * TOPK * NE)
        logitT = moe(TOK)
        posT = moe(TOK)
        gmT = moe(TOK)
        cnt = moe(16)
        Eb = moe(SLOTS)
        Eb3 = moe(SLOTS // 2).bitcast(BF16)
        Eb3f = moe(SLOTS)
        posb = moe(3, SLOTS)
        gateb = moe(3, SLOTS)
        tabf = moe(160)
        tab = moe(160).bitcast(I32)
        Psel = moe(3, SLOTS)
        Pg = moe(3, P)
        PgT = moe(3 * P)
        xsel = moe(512)
        xselT = moe(KD, SLOTS)
        Ebc = moe(SLOTS // 2).bitcast(BF16)
        g_sb, u_sb, s_sb, a_sb = moe(512), moe(512), moe(512), moe(512)
        actT = moe(4, P)
        y_sb = moe(512)
        fng = view(slot_at[uslot3], D)
        ptok = view(slot_at[uslot3] + D, 3, PLE)
        pT = moe(2, TOK)
        h3T = h2T
        LAST_BANKS = (6, 0, 2)
        PLE_BANKS = (4, 5, 6, 7, 2)
        ple_moved = y_sb[0:64]
        assert mo[0] <= small_at, (mo[0], small_at)

        ps = ctx.enter_context(nc.psum_tensor("ps", [P, 8, 512], F32))
        pj = [ps[:, 0, :], ps[:, 1, :]]

        def pair(b, n=P):
            return ps[:, b:b + 2, :].rearrange("p a (h c) -> p (a h) c", c=P)[:, :, 0:n]

        G01, G23, G45 = (lambda n=P: pair(2, n)), (lambda n=P: pair(4, n)), (lambda n=P: pair(6, n))

        def blocks64(bank):
            return ps[:, bank, :].rearrange("p (h c) -> p h c", c=HB)

        def masks_before(tt):
            return sum(min(n, 6) for n in LEVELS[:tt])

        w_in = t["w_in"][0].rearrange("(k p) n -> p k n", p=P)
        chunk_src = [w_in[:, :, c * 512:(c + 1) * 512] for c in range(6)]
        for col in (COL_GATE, COL_U, COL_V, COL_MA, COL_MB):
            chunk_src += [w_in[:, :, col + c * 512:col + (c + 1) * 512] for c in range(2)]
        for name in ("w_proj_a", "w_proj_b", "w_out"):
            w = t[name][0].rearrange("(k p) n -> p k n", p=P)
            chunk_src += [w[:, :, c * 512:(c + 1) * 512] for c in range(2)]
        NCH = len(chunk_src)
        C_GATE, C_U, C_V, C_MA, C_MB, C_PA, C_PB, C_WO = 6, 8, 10, 12, 14, 16, 18, 20
        landed = [sem(f"weights_landed{s}") for s in range(6)]
        used = [sem(f"weights_used{s}") for s in range(6)]

        N_QKV, N_AB, N_GATE, N_U, N_V, N_MA, N_MB, N_YA, N_YB, N_WO, N_END = (
            0, 24, 25, 33, 41, 47, 55, 63, 71, 79, 85)
        free_at = [4 * (c + 1) for c in range(6)]
        for n0, per in ((N_GATE, 4), (N_U, 4), (N_V, 3), (N_MA, 4), (N_MB, 4), (N_YA, 4), (N_YB, 4), (N_WO, 3)):
            free_at += [n0 + per, n0 + 2 * per]
        proj_done = sem("projection_done")
        bank_free = [sem("projection_bank0_free"), sem("projection_bank1_free")]

        def bank_wait(pe, n):
            if n >= 2:
                pe.wait_ge(bank_free[n % 2], n // 2)

        def evacuated(eng, n):
            eng.wait_ge(bank_free[n % 2], n // 2 + 1)

        def chunk_wait(eng, c):
            eng.wait_ge(landed[c % FRONT_SLOTS], 16 * (c // FRONT_SLOTS + 1))
        before = [len([c for c in range(NCH) if c % FRONT_SLOTS == s]) for s in range(6)]
        uslot = [(u + 2) % 6 for u in range(6)]

        class Chain:

            def __init__(self, eng, s):
                self.eng, self.s, self.n = eng, s, 0

            def __call__(self, ins):
                self.n += 1
                ins.then_inc(self.s, 1)

            def wait(self):
                self.eng.wait_ge(self.s, self.n)

            def link(self, ins):
                self(ins)
                self.wait()

        block = ctx.enter_context(nc.Block())

        @block.sync
        def _(sp):
            sp.dma_start(arena[:, cst_at:cst_at + NCONST], t["consts"]).then_inc(sem("consts_in"), 16)
            sp.dma_start(x[:, 0:2, :], t["x_prompt"][0].rearrange("(a p) d -> p a d", p=P)).then_inc(sem("x_in"), 16)
            sp.dma_start(x[0:64, 2, :], t["x_sample"].rearrange("b s d -> (b s) d")).then_inc(sem("x_in"), 16)
            sp.dma_start(rows_in[0:96, :], t["conv_w"][0].rearrange("t (f p) -> (t f) p", p=P)).then_inc(sem("rows_loaded"), 16)
            for i, name in enumerate(("norm1_g", "norm2_g", "norm3_g")):
                sp.dma_start(rows_in[96 + 8 * i:104 + 8 * i, :],
                             t[name][0].rearrange("(k p) -> k p", p=P)).then_inc(sem("rows_loaded"), 16)
            sp.dma_start(rows_in[120:121, :], t["dn_norm_g"]).then_inc(sem("rows_loaded"), 16)
            sp.dma_start(sc_rows[0:24, :], t["state_conv"][0].rearrange("b r n -> (b r) n")).then_inc(sem("rows_loaded"), 16)
            for c in range(FRONT_SLOTS):
                sp.dma_start(slots[c], chunk_src[c]).then_inc(landed[c], 16)
                if c == 0:
                    sp.dma_start(wab, w_in[:, :, COL_AB:COL_AB + 16]).then_inc(sem("ab_in"), 16)
                    sp.dma_start(alog, t["a_log"].broadcast_to([P, H])).then_inc(sem("ab_in"), 16)
                    sp.dma_start(dtb, t["dt_bias"].broadcast_to([P, H])).then_inc(sem("ab_in"), 16)

            def chunk(c):
                sp.wait_ge(proj_done, free_at[c - FRONT_SLOTS])
                sp.dma_start(slots[c % FRONT_SLOTS], chunk_src[c]).then_inc(landed[c % FRONT_SLOTS], 16)

            for c in range(FRONT_SLOTS, C_PA + 1):
                chunk(c)
            sp.wait_ge(sem("S_ready"), 2)
            sp.dma_start(t["out_sd_p"][0, 0].rearrange("h k v -> k h v"), S[:, :, :]).then_inc(sem("stored"), 16)
            for h in range(H):
                sp.wait_ge(sem("S0_new"), h + 1)
                sp.dma_start(t["out_sd_s"][0, :, h].rearrange("b k v -> k b v"), S0[h % 4]).then_inc(sem(f"S0_stored{h % 4}"), 16)
            chunk(C_PA + 1)
            sp.wait_ge(sem("o_normed"), 3)
            sp.wait_ge(sem("S0_product"), 2 * H)
            sp.wait_ge(sem("stored"), 16)
            sp.dma_start(lng, t["gm_ln_g"].broadcast_to([P, D])).then_inc(sem("mlp_in"), 16)
            sp.dma_start(lnb, t["gm_ln_b"].broadcast_to([P, D])).then_inc(sem("mlp_in"), 16)
            sp.dma_start(bsb.rearrange("p g t -> p (g t)"),
                         t["gm_bs"].rearrange("a g t -> a (g t)").broadcast_to([P, G * P])).then_inc(sem("mlp_in"), 16)
            sp.dma_start(wnat, t["gm_ws"][0].rearrange("g t s -> t g s")).then_inc(sem("mlp_in"), 16)
            sp.wait_ge(sem("wnat8_zero"), 1)
            for b in range(DB):
                sp.dma_start(wnat8[DS * b:DS * b + DS, :, DS * b:DS * b + DS],
                             t["gm_ws"][0, :, 0:DS, 0:DS].rearrange("g t s -> t g s")).then_inc(sem("mlp_in"), 16)
            sp.dma_start(rw, t["router_w"][0].rearrange("(k p) e -> p k e", p=P)).then_inc(sem("router_in"), 16)
            sp.dma_start(rbias, t["router_b"].broadcast_to([P, NE])).then_inc(sem("router_in"), 16)
            sp.dma_start(b12[0:NE, 0:2 * D], t["moe_b1"][0]).then_inc(sem("router_in"), 16)
            sp.dma_start(b12[0:NE, 2 * D:3 * D], t["moe_b2"][0]).then_inc(sem("router_in"), 16)
            sp.dma_start(x[:, 0:2, :], t["x_prompt"][0].rearrange("(a p) d -> p a d", p=P)).then_inc(sem("x_in"), 16)
            sp.dma_start(x[0:64, 2, :], t["x_sample"].rearrange("b s d -> (b s) d")).then_inc(sem("x_in"), 16)
            for c in range(C_PA + 2, NCH):
                chunk(c)
            sp.wait_ge(sem("vnorm_ready"), 3)
            sp.dma_start(t["out_gv"][0].rearrange("b s d -> (b s) d"), vtok[0:64, 2, :]).then_inc(sem("stored"), 16)

            def unit_src(e, u):
                if u < 4:
                    return t["moe_w1"][0, e, u * 256:(u + 1) * 256, :].rearrange("(k p) n -> p k n", p=P)
                return t["moe_w2"][0, e, (u - 4) * 512:(u - 3) * 512, :].rearrange("(k p) n -> p k n", p=P)

            def unit_dst(u):
                return slots[uslot[u]].rearrange("p k n -> p (k n)").rearrange("p (k n) -> p k n", k=2 if u < 4 else 4)

            for u in range(6):
                s = uslot[u]
                if s < FRONT_SLOTS:
                    sp.wait_ge(proj_done, free_at[NCH - FRONT_SLOTS + s])
                elif u == 0:
                    sp.wait_ge(sem("merged"), KD)
                    sp.wait_ge(sem("stored"), 32)
                sp.dma_start(unit_dst(u), t["moe_w1"][0, 0, u * 256:(u + 1) * 256, :].rearrange("(k p) n -> p k n", p=P)
                             if u < 4 else unit_src(0, u)).then_inc(landed[s], 16)
            sp.wait_ge(sem("tables_ready"), 1)
            w1 = t["moe_w1"][0].rearrange("e (u k p) n -> (e u) p k n", u=4, p=P)
            w2 = t["moe_w2"][0].rearrange("e (u k p) n -> (e u) p k n", u=2, p=P)
            with sp.Fori(0, NE - 1) as e:
                through = sp.value_load(tab[0:1, bass.ds(96 + e, 1)], min_val=1, max_val=MAXB)
                for u in range(6):
                    s = uslot[u]
                    sp.wait_ge(used[s], through)
                    src = w1[bass.ds(e * 4 + 4 + u, 1)] if u < 4 else w2[bass.ds(e * 2 + 2 + u - 4, 1)]
                    sp.dma_start(unit_dst(u), src.rearrange("a p k n -> p (a k) n")).then_inc(landed[s], 16)
            wg = t["ple_gate_w"][0].rearrange("(k p) n -> p k n", p=P)
            nb = sp.value_load(tab[0:1, 96 + NE - 1:96 + NE], min_val=1, max_val=MAXB)
            for c in range(2):
                sp.wait_ge(used[uslot[c]], nb)
                sp.dma_start(slots[uslot[c]], wg[:, :, c * 512:(c + 1) * 512]).then_inc(landed[uslot[c]], 16)
            sp.wait_ge(used[uslot[2]], nb)
            sp.dma_start(slots[uslot[2]].rearrange("p k n -> p (k n)")[:, 0:2048].rearrange("p (k n) -> p k n", k=2),
                         t["ple_w"][0].rearrange("(k p) n -> p k n", p=P)).then_inc(landed[uslot[2]], 16)
            sp.wait_ge(used[uslot[3]], nb)
            sp.dma_start(ptok[:, 0:2, :], t["p_prompt"][0, 0].rearrange("(a p) d -> p a d", p=P)).then_inc(sem("ple_in"), 16)
            sp.dma_start(ptok[0:64, 2, :], t["p_sample"][0].rearrange("b s d -> (b s) d")).then_inc(sem("ple_in"), 16)
            sp.dma_start(fng, t["final_norm_g"].rearrange("(a d) -> a d", a=1).broadcast_to([P, D])).then_inc(sem("ple_in"), 16)
            for tt, (t0, tn) in enumerate(TILES):
                sp.wait_ge(sem("y_ready"), tt + 1)
                dst = t["out_yp"][0, t0:t0 + tn, :] if tt < 2 else t["out_ys"].rearrange("b s d -> (b s) d")
                sp.dma_start(dst, x[0:tn, tt, :]).then_inc(sem("stored"), 16)
            sp.wait_ge(sem("stored"), 16 * 5)
            sp.wait_ge(sem("newrows_stored"), 32)

        @block.gpsimd
        def _(pool):
            for i in range(3):
                pool.memset(zpad[i], 0.0).then_inc(sem("pool_zeroed"), 1)
            pool.wait_ge(sem("pool_zeroed"), 3)

            def fill_old(n):
                if n >= 3:
                    pool.wait_ge(sem("conv_done"), n - 2)
                    pool.wait_ge(sem("last3_done"), 2 * (n - 2))
                pool.wait_ge(sem("old_turned"), n // 4 + 1)
                zs = zpad[n % 3][:, 3 + SEQ:].rearrange("p (b j) -> p b j", b=DB)
                pool.tensor_copy(zs[:, :, 0:3], oldT[:, n, :].rearrange("p (b j) -> p b j", b=DB)).then_inc(sem("old_filled"), 1)

            def keep_last(n):
                evacuated(pool, n)
                zs = zpad[n % 3][:, 3 + SEQ:].rearrange("p (b j) -> p b j", b=DB)
                pool.tensor_copy(last3[:, n, 0:3], zpad[n % 3][:, SEQ:SEQ + 3]).then_inc(sem("last3_done"), 1)
                pool.tensor_copy(last3[:, n, 3:27].rearrange("p (b j) -> p b j", b=DB), zs[:, :, DS:DS + 3]).then_inc(sem("last3_done"), 1)

            fill_old(0)
            for n in range(FT):
                if n + 1 < FT:
                    fill_old(n + 1)
                keep_last(n)
                m = n - 2
                if 0 <= m < 2 * H:
                    pool.wait_ge(sem("silu_done"), 2 * (m + 1))
                    if m >= 2:
                        pool.wait_ge(sem("sumsq_done"), m - 1)
                    pool.tensor_tensor(sq[m % 2], qkvT[:, m, :], qkvT[:, m, :], ALU.mult).then_inc(sem("sq_ready"), 1)

            def load_state(i):
                pool.dma_start(S0[i % 4], t["state_delta"][0, :, i % H].rearrange("b k v -> k b v")).then_inc(sem(f"S0_in{i % 4}"), 16)

            pool.wait_ge(sem("newrows_ready"), 6)
            pool.dma_start(t["out_sc_p"][0, 0], new_rows[0:3, :]).then_inc(sem("newrows_stored"), 16)
            pool.dma_start(t["out_sc_s"][0].rearrange("b r n -> (b r) n"), new_rows[3:27, :]).then_inc(sem("newrows_stored"), 16)
            pool.wait_ge(sem("newrows_stored"), 32)
            pool.wait_ge(sem("old_turned"), 6)
            pool.memset(XT[64:128, :, 0:HB], 0.0).then_inc(sem("pool_zeroed"), 1)
            pool.wait_ge(sem("pool_zeroed"), 4)
            for i in range(4):
                load_state(i)
            for tt, (t0, tn) in enumerate(TILES):
                pool.wait_ge(sem("GR_ready"), tt + 1)
                pool.wait_ge(sem("qk_normed"), 2)
                if tt == 2:
                    pool.wait_ge(sem("kS_done"), 1)
                pool.tensor_tensor(qd[:, :, 0:tn], qkvT[:, 0:H, t0:t0 + tn], GR[:, :, 0:tn], ALU.mult).then_inc(sem("qd_ready"), 1)
                pool.wait_ge(sem("AT_ready"), tt + 1)
                pool.wait_ge(sem("mT_ready"), tt + 1)
                for lev in range(min(LEVELS[tt], 6)):
                    done = sum(LEVELS[:tt]) + lev
                    if lev == 0 and tt:
                        pool.wait_ge(sem("u_done"), tt)
                    if lev >= 2:
                        pool.wait_ge(sem("W_done"), done - 1)
                    if lev == 2:
                        pool.wait_ge(sem("X_ready"), done - 1)
                    pool.tensor_tensor(Al[lev % 2][0:tn], ATd[0:tn],
                                       cst(f"level{lev}", tn).rearrange("p (a c) -> p a c", a=1).broadcast_to([tn, H, HB]),
                                       ALU.mult).then_inc(sem("Al_ready"), 1)
            for i in range(4, 12):
                pool.wait_ge(sem("kS_head"), i - 3)
                load_state(i)
            for h in range(H):
                if h >= 4:
                    pool.wait_ge(sem(f"S0_stored{h % 4}"), 16)
                    load_state(8 + h)
                pool.wait_ge(sem("u_ready"), 3)
                if h >= 2:
                    pool.wait_ge(sem("S0_product"), 2 * (h - 1))
                pool.tensor_tensor([X, XT][h % 2][0:64], W[0:64, h, :].rearrange("p (a c) -> p a c", a=1).broadcast_to([64, DB, P]),
                                   cst("seq8", 64).rearrange("p (a c) -> p a c", c=1).broadcast_to([64, DB, P]),
                                   ALU.mult).then_inc(sem("uexp_ready"), 1)
            pool.wait_ge(sem("o_normed"), 3)
            pool.wait_ge(sem("S0_product"), 2 * H)
            pool.memset(wnat8[0:64], 0.0).then_inc(sem("wnat8_zero"), 1)
            pool.wait_ge(sem("router_in"), 16 * 4)
            for i in range(3):
                pool.wait_ge(sem(f"S0_stored{i}"), 32)
            part0, part1 = b12s[0:NE, :], b12c[0:NE, :]
            link = lambda ins, n: (ins.then_inc(sem("bias_chain"), 1), pool.wait_ge(sem("bias_chain"), n))
            link(pool.tensor_copy(part0, b12[0:NE, :]), 1)
            link(pool.tensor_tensor(b12[0:NE, :], b12[0:NE, :], part0, ALU.subtract), 2)
            link(pool.tensor_copy(part1, b12[0:NE, :]), 3)
            pool.dma_start(b12s[32:64, :], part1).then_inc(sem("bias_moved"), 16)
            link(pool.tensor_tensor(b12[0:NE, :], b12[0:NE, :], part1, ALU.subtract), 4)
            pool.wait_ge(sem("bias_moved"), 16)
            link(pool.tensor_copy(part1, b12[0:NE, :]), 5)
            pool.dma_start(b12s[64:96, :], part1).then_inc(sem("bias_moved"), 16)

        @block.tensor
        def _(pe):
            def mm(out, lhsT, rhs, first, last):
                return pe.matmul(out, lhsT, rhs, start=first, stop=last, skip_group_check=True)

            pe.wait_ge(sem("consts_in"), 16)
            pe.wait_ge(sem("rows_loaded"), 16 * 6)
            pe.transpose(ps[:, 0, 0:121], rows_in[0:121, :], ident[0:121, 0:121]).then_inc(sem("rows_turned"), 1)
            for g in range(6):
                for i in range(4):
                    f = 4 * g + i
                    m = pe.transpose(ps[:, 2 + g, 24 * i:24 * i + 24], sc_rows[0:24, f * P:(f + 1) * P], ident[0:24, 0:24])
                m.then_inc(sem("old_done"), 1)
            pe.wait_ge(sem("xn_ready"), 3)
            pe.wait_ge(sem("cols_ready"), 1)
            for k in range(KD):
                if k >= 2:
                    pe.wait_ge(sem("hT_ready"), k - 1)
                for tt, (t0, tn) in enumerate(TILES):
                    m = pe.transpose(pj[k % 2][:, t0:t0 + tn], x[0:tn, tt, k * P:(k + 1) * P], ident[0:tn, 0:tn])
                m.then_inc(sem("hT_done"), 1)

            def features(n, c, m, rhs):
                chunk_wait(pe, c)
                bank_wait(pe, n)
                for k in range(KD):
                    last = mm(pj[n % 2][:, 0:TOK], slots[c % FRONT_SLOTS][:, k, m * P:(m + 1) * P], rhs[:, k, :], k == 0, k == KD - 1)
                last.then_inc(proj_done, 1)

            def rows(n, c, tt, lhs):
                t0, tn = TILES[tt]
                chunk_wait(pe, c)
                bank_wait(pe, n)
                if tt == 2:
                    for k in range(KD):
                        for g in range(2):
                            last = mm(pj[n % 2][64 * g:64 * g + 64, 0:256], lhs[:, k, t0:t0 + tn],
                                      slots[c % FRONT_SLOTS][:, k, 256 * g:256 * g + 256], k == 0, k == KD - 1)
                    last.then_inc(proj_done, 1)
                    return
                for k in range(KD):
                    last = mm(pj[n % 2][0:tn, :], lhs[:, k, t0:t0 + tn], slots[c % FRONT_SLOTS][:, k, :], k == 0, k == KD - 1)
                last.then_inc(proj_done, 1)

            pe.wait_ge(sem("hT_ready"), KD)
            for n in range(FT):
                features(n, n // 4, n % 4, hT)
                m = n - 3
                if 0 <= m < 2 * H:
                    pe.wait_ge(sem("sq_ready"), m + 1)
                    if m >= 6:
                        pe.wait_ge(sem("ln_done"), m - 5)
                    else:
                        pe.wait_ge(sem("old_turned"), 6)
                    mm(ps[:, 2 + m % 6, 0:TOK], cst("ones"), sq[m % 2], True, True).then_inc(sem("sumsq_done"), 1)
            pe.wait_ge(sem("ab_in"), 48)
            bank_wait(pe, N_AB)
            for tt, (t0, tn) in enumerate(TILES):
                for k in range(KD):
                    last = mm(pj[0][0:tn, 16 * tt:16 * tt + 16], hT[:, k, t0:t0 + tn], wab[:, k, :], k == 0, k == KD - 1)
            last.then_inc(proj_done, 1)
            pe.wait_ge(sem("last3_done"), 2 * FT)
            pe.wait_ge(sem("ln_done"), 2 * H)
            for g in range(6):
                for i in range(4):
                    m = pe.transpose(ps[0:27, 2 + g, P * i:P * i + P], last3[:, 4 * g + i, :], ident)
                m.then_inc(sem("newrows_done"), 1)
            filled = [N_GATE]

            def fill(count=1):
                for _ in range(count):
                    n = filled[0]
                    filled[0] += 1
                    if n < N_V:
                        features(n, C_GATE + (n - N_GATE) // 4, (n - N_GATE) % 4, hT)
                    elif n < N_MA:
                        rows(n, C_V + (n - N_V) // 3, (n - N_V) % 3, hT)
                    else:
                        features(n, C_MA + (n - N_MA) // 4, (n - N_MA) % 4, hT)

            pe.wait_ge(sem("newrows_ready"), 6)
            pe.wait_ge(sem("g_ready"), 3)
            for tt, (t0, tn) in enumerate(TILES):
                mm(ps[0:tn, 7, 16 * tt:16 * tt + 8], cst("tri8" if tt == 2 else "tri", tn, tn), gg[0:tn, tt, :], True, True)
                m = mm(ps[0:tn, 7, 16 * tt + 8:16 * tt + 16], cst("same8" if tt == 2 else "ones", tn, tn), gg[0:tn, tt, :], True, True)
            m.then_inc(sem("cum_done"), 1)
            fill(3)
            pe.wait_ge(sem("qk_normed"), 2)
            pe.wait_ge(sem("silu_done"), 2 * FT)

            for tt, (t0, tn) in enumerate(TILES):
                L0 = sum(LEVELS[:tt])
                pe.wait_ge(sem("RH_ready"), tt + 1)
                if tt == 0:
                    pe.wait_ge(sem("gce_ready"), 1)
                else:
                    pe.wait_ge(sem("S_ready"), tt)
                for a in range(2):
                    m = mm(G45(tn)[:, 4 * a:4 * a + 4, :], cst("ones", tn), X[0:tn, 4 * a:4 * a + 4, 0:tn], True, True)
                m.then_inc(sem("gcrow_done"), 1)
                if tt:
                    pe.wait_ge(sem("ln_done"), 2 * H + tt)
                    pe.wait_ge(sem("o_ready"), tt)
                for h in range(H):
                    mm(G01(tn)[0:tn, h, :], qkvT[:, H + h, t0:t0 + tn], qkvT[:, H + h, t0:t0 + tn], True, True)
                    m = mm(G23(tn)[0:tn, h, :], qkvT[:, H + h, t0:t0 + tn], qkvT[:, h, t0:t0 + tn], True, True)
                m.then_inc(sem("kk_done"), 1)
                fill()
                pe.wait_ge(sem("AT_ready"), tt + 1)
                for h in range(H):
                    m = pe.transpose(G01()[0:tn, h, :], qkvT[:, H + h, t0:t0 + tn], ident)
                m.then_inc(sem("kt_done"), 1)
                fill()
                for lev in range(LEVELS[tt]):
                    i = L0 + lev
                    joins = lev == 6
                    if not joins:
                        pe.wait_ge(sem("Al_ready"), masks_before(tt) + lev + 1)
                    if lev == 0:
                        pe.wait_ge(sem("dd_ready"), tt + 1)
                        pe.wait_ge(sem("GR_ready"), tt + 1)
                    else:
                        pe.wait_ge(sem("X_ready"), i)
                    for h in range(H):
                        if joins:
                            m = mm(blocks64(6)[64:128, h, :], AToff[0:64, h, :], Xd[0:64, h, :], True, True)
                        else:
                            for b in range(0, tn, HB):
                                blk = slice(b, b + HB)
                                rhs = cst("ident64")[blk, :] if lev == 0 else Xd[blk, h, :]
                                m = mm(blocks64(6)[blk, h, :], Al[lev % 2][blk, h, :], rhs, True, True)
                    m.then_inc(sem("W_done"), 1)
                    if lev or tt < 2:
                        fill()
                    if lev:
                        pe.wait_ge(sem("W_ready"), i - tt)
                        if lev == 1:
                            pe.wait_ge(sem("kd_ready"), tt + 1)
                            pe.wait_ge(sem("mT_ready"), tt + 1)
                        for h in range(H):
                            if joins:
                                m = mm(blocks64(4)[0:64, h, :], Wd[64:128, h, :], XTd[64:128, h, :], True, True)
                                continue
                            for b in range(0, tn, HB):
                                blk = slice(b, b + HB)
                                m = mm(blocks64(4)[blk, h, :], Wd[blk, h, :], XTd[blk, h, :], True, True)
                            if lev < LEVELS[tt] - 1:
                                for b in range(0, tn, HB):
                                    blk = slice(b, b + HB)
                                    m = mm(blocks64(2)[blk, h, :], XTd[blk, h, :], Wd[blk, h, :], True, True)
                        m.then_inc(sem("D_done"), 1)
                        if lev in (1, 3) and tt < 2:
                            fill()
                if tt:
                    pe.wait_ge(sem("X_ready"), L0 + LEVELS[tt])
                    pe.wait_ge(sem("qd_ready"), tt + 1)
                if tt == 1:
                    for h in range(H):
                        mm(G01(tn)[:, h, :], S[:, h, :], qkvT[:, H + h, t0:t0 + tn], True, True)
                        m = mm(G23(tn)[:, h, :], S[:, h, :], qd[:, h, 0:tn], True, True)
                    m.then_inc(sem("kS_done"), 1)
                if tt < 2:
                    pe.wait_ge(sem("rT_ready"), tt + 1)
                for h in range(H):
                    m = pe.transpose(G45()[0:tn, h, :], rT[:, h, 0:tn] if tt < 2 else qkvT[:, 2 * H + h, t0:t0 + tn], ident)
                m.then_inc(sem("r_done"), 1)
                if tt == 2:
                    for h in range(H):
                        pe.wait_ge(sem(f"S0_in{h % 4}"), 16 * (h // 4 + 1))
                        if h >= 2:
                            pe.wait_ge(sem("kS_read"), h - 1)
                        for a in range(2):
                            bank, states = 2 + 2 * (h % 2) + a, S0[h % 4][:, 4 * a:4 * a + 4, :]
                            mm(ps[0:64, bank, :], qkvT[:, H + h, t0:t0 + tn], states, True, True)
                            m = mm(ps[64:128, bank, :], qd[:, h, 0:tn], states, True, True)
                        m.then_inc(sem("kS_head"), 1)
                        if h % 4 == 3:
                            fill()
                pe.wait_ge(sem("r_ready"), tt + 1 if tt < 2 else 2 + H)
                pe.wait_ge(sem("X_ready"), L0 + LEVELS[tt])
                for h in range(H):
                    m = mm(G01()[0:tn, h, :], XT[0:tn, h, :] if tt < 2 else XTd[0:tn, h, :], r[0:tn, h, :], True, True)
                m.then_inc(sem("u_done"), 1)
                pe.wait_ge(sem("u_ready"), tt + 1)
                if tt == 1:
                    pe.wait_ge(sem("qS_ready"), 1)
                for h in range(H):
                    m = mm(G23(tn)[:, h, :], W[0:tn, h, :], mT[0:tn, h, 0:tn], True, tt < 2)
                    if tt == 2:
                        m = mm(G23(tn)[:, h, :], r[:, h, :], ident[:, 64:128], False, True)
                m.then_inc(sem("o_done"), 1)
                if tt < 2:
                    for h in range(H):
                        m = mm(G45()[:, h, :], kd[0:tn, h, :], W[0:tn, h, :], True, True)
                    m.then_inc(sem("S_done"), 1)
                fill()
                pe.wait_ge(sem("osq_ready"), tt + 1)
                for a in range(2):
                    m = mm(G01(tn)[:, 4 * a:4 * a + 4, :], cst("ones"), qS[:, 4 * a:4 * a + 4, 0:tn], True, True)
                m.then_inc(sem("sumsq_done"), 1)
                if tt < 2:
                    fill()
            for h in range(H):
                pe.wait_ge(sem("uexp_ready"), h + 1)
                if h >= 2:
                    pe.wait_ge(sem("S0_new"), h - 1)
                elif h == 1:
                    pe.wait_ge(sem("o_ready"), 3)
                for a in range(2):
                    mm(ps[:, [6, 4][h % 2] + a, :], kd[0:64, h, :], [X, XT][h % 2][0:64, 4 * a:4 * a + 4, :], True, True).then_inc(sem("S0_product"), 1)
                if h % 4 == 3:
                    fill()
            assert filled[0] == N_YA

            pe.wait_ge(sem("gated_ready"), 1)
            for i in range(4):
                features(N_YA + i, C_PA, i, oT)
            pe.wait_ge(sem("mlp_in"), 16 * 12)
            pe.wait_ge(sem("S0_new"), H)
            for g in range(G):
                pe.transpose(G01()[:, g, :], wnat[:, g, :], ident)
            for g in range(G):
                m = pe.transpose(G23(64)[0:64, g, :], wnat8[0:64, g, :], ident[0:64, 0:64])
            m.then_inc(sem("wT_done"), 1)
            for i in range(4, 6):
                features(N_YA + i, C_PA + 1, i - 4, oT)
            pe.wait_ge(sem("vnorm_ready"), 3)
            pe.wait_ge(sem("WT_ready"), 2)
            for tt, (t0, tn) in enumerate(TILES):
                for a in range(2):
                    for g in range(4 * a, 4 * a + 4):
                        wt = WT[:, g, :] if tt < 2 else WT8[0:64, g, :]
                        m = mm(ps[:, 2 + 2 * tt + a, P * (g % 4):P * (g % 4) + tn], vtok[0:tn, tt, g * P:(g + 1) * P], wt, True, True)
                    m.then_inc(sem("mix_done"), 1)
            for i in range(6, 8):
                features(N_YA + i, C_PA + 1, i - 4, oT)
            pe.wait_ge(sem("us_ready"), 6)
            for i in range(8):
                features(N_YB + i, C_PB + i // 4, i % 4, uT)
            pe.wait_ge(sem("merged"), KD)
            for half in range(2):
                for tt in range(3):
                    rows(N_WO + 3 * half + tt, C_WO + half, tt, mixT)

            pe.wait_ge(sem("xn_ready"), 6)
            pe.wait_ge(sem("router_in"), 16 * 4)
            for k in range(KD):
                bank_wait(pe, N_END + k)
                for tt, (t0, tn) in enumerate(TILES):
                    m = pe.transpose(pj[(N_END + k) % 2][:, t0:t0 + tn], h2[0:tn, tt, k * P:(k + 1) * P], ident[0:tn, 0:tn])
                m.then_inc(sem("hT_done"), 1)
                for j in ([k - 1] if 0 < k < KD - 1 else [k - 1, k] if k else []):
                    evacuated(pe, N_END + j)
                    m = mm(ps[0:NE, 5, 0:TOK], rw[:, j, :], h2T[:, j, :], j == 0, j == KD - 1)
            m.then_inc(sem("logits_done"), 1)
            pe.wait_ge(sem("logitT_ready"), 1)
            for tt, (t0, tn) in enumerate(TILES):
                m = pe.transpose(ps[0:tn, 6, NE * tt:NE * tt + NE], logitT[0:NE, t0:t0 + tn], ident[0:NE, 0:NE])
            m.then_inc(sem("logits_done"), 1)
            pe.wait_ge(sem("mask_ready"), 1)
            for tt, (t0, tn) in enumerate(TILES):
                for s in range(tt + 1):
                    lhs = cst("before", tn, tn) if s == tt else cst("ones", P, tn)
                    m = mm(ps[0:tn, 3, NE * tt:NE * tt + NE], lhs, mask[0:TILES[s][1], s, :], s == 0, s == tt)
            for tt, (t0, tn) in enumerate(TILES):
                m = mm(ps[0:NE, 4, 0:1], mask[0:tn, tt, :], cst("ones", tn, 1), tt == 0, tt == 2)
            m.then_inc(sem("rank_done"), 1)
            pe.wait_ge(sem("blocks_ready"), 1)
            mm(ps[0:NE, 4, 8:9], cst("tri", NE, NE), cnt[0:NE, 4:5], True, True).then_inc(sem("through_done"), 1)
            pe.wait_ge(sem("rank_ready"), 3)
            for tt, (t0, tn) in enumerate(TILES):
                pe.transpose(ps[0:NE, 5, t0:t0 + tn], pos[0:tn, tt, :], ident[0:tn, 0:tn])
                m = pe.transpose(ps[0:NE, 6, t0:t0 + tn], gmat[0:tn, tt, :], ident[0:tn, 0:tn])
            m.then_inc(sem("rankT_done"), 1)
            pe.wait_ge(sem("E_ready"), 1)
            pe.wait_ge(sem("rankT_ready"), 2)
            for tt, (t0, tn) in enumerate(TILES):
                mm(ps[0:tn, 7, SLOTS * tt:SLOTS * tt + SLOTS], posT[0:NE, t0:t0 + tn], Eb[0:NE, :], True, True)
                mm(ps[0:tn, 7, 256 + SLOTS * tt:256 + SLOTS * tt + SLOTS], gmT[0:NE, t0:t0 + tn], Eb[0:NE, :], True, True)
            mm(ps[0:1, 4, 128:192], cst("eid", NE), Eb[0:NE, :], True, True)
            mm(ps[0:1, 4, 192:224], cnt[0:NE, 5:6], ident[0:NE, 0:NE], True, True).then_inc(sem("perblock_done"), 1)

            def select(value):
                pe.wait_ge(sem("psel_ready"), value)
                for tt, (t0, tn) in enumerate(TILES):
                    for g in range(2):
                        m = mm(ps[64 * g:64 * g + 64, 3, :], Psel[0:tn, tt, :], h2[0:tn, tt, 512 * g:512 * g + 512], tt == 0, tt == 2)
                m.then_inc(sem("sel_done"), 1)

            def turn_rows(value):
                pe.wait_ge(sem("xsel_ready"), value)
                for j in range(4):
                    m = pe.transpose(ps[:, 5, P * j:P * j + P], xsel[:, P * j:P * j + P], ident)
                m.then_inc(sem("xT_done"), 1)

            def combine(tt, y_value, free_value):
                t0, tn = TILES[tt]
                if tt == 0:
                    pe.wait_ge(sem("ysb_ready"), y_value)
                    pe.wait_ge(sem("pgT_ready"), y_value)
                pe.wait_ge(sem("comb_free"), free_value)
                for g in range(2):
                    m = mm(ps[:, 6 + g, :], PgT[64 * g:64 * g + 64, t0:t0 + P], y_sb[64 * g:64 * g + 64, :], True, True)
                m.then_inc(sem("comb_done"), 1)

            pe.wait_ge(sem("tables_ready"), 1)
            nb = pe.value_load(tab[0:1, 96 + NE - 1:96 + NE], min_val=1, max_val=MAXB)
            pe.nop().then_inc(sem("pgT_done"), 1)
            select(1)
            turn_rows(1)
            pe.wait_ge(sem("bias_moved"), 32)
            pe.wait_ge(sem("bias_chain"), 5)
            with pe.Fori(0, nb) as b:
                e = pe.value_load(tab[0:1, bass.ds(b, 1)], min_val=0, max_val=NE - 1)
                hid_free = sem("hid_free")
                pe.wait_ge(hid_free, b + 1)
                pe.wait_ge(sem("xselT_ready"), b + 1)
                for u in range(4):
                    s = uslot[u]
                    w = slots[s].rearrange("p k n -> p (k n)").rearrange("p (k n) -> p k n", k=2)
                    pe.wait_ge(landed[s], e * 16 + 16 * (before[s] + 1))
                    for kk in range(2):
                        k = 2 * u + kk
                        for part in range(2):
                            for g in range(2):
                                c0 = 1024 * part + 512 * g
                                m = mm(ps[64 * g:64 * g + 64, part, :], xselT[:, k, :], w[:, kk, c0:c0 + 512], k == 0, False)
                    m.then_inc(used[s], 1)
                    if u < 3:
                        combine(u, b + 1, b * 3 + u + 1)
                pe.wait_ge(sem("ebc_ready"), b + 1)
                for part in range(2):
                    for g in range(2):
                        c0 = 1024 * part + 512 * g
                        m = mm(ps[64 * g:64 * g + 64, part, :], Ebc[0:96, :], b12s[0:96, c0:c0 + 512], False, True)
                m.then_inc(sem("hid_done"), 1)
                select(b + 2)
                turn_rows(b + 2)
                pe.wait_ge(sem("act_ready"), b + 1)
                for j in range(4):
                    m = pe.transpose(ps[:, 4, P * j:P * j + P], a_sb[:, P * j:P * j + P], ident)
                m.then_inc(sem("actT_done"), 1)
                pe.wait_ge(sem("actT_ready"), b + 1)
                for u in range(4, 6):
                    s = uslot[u]
                    w = slots[s].rearrange("p k n -> p (k n)").rearrange("p (k n) -> p k n", k=4)
                    pe.wait_ge(landed[s], e * 16 + 16 * (before[s] + 1))
                    for kk in range(4):
                        k = 4 * (u - 4) + kk
                        for g in range(2):
                            m = mm(ps[64 * g:64 * g + 64, 2, :], actT[:, k % 4, 64 * (k // 4):64 * (k // 4) + 64],
                                   w[:, kk, 512 * g:512 * g + 512], k == 0, False)
                    m.then_inc(used[s], 1)
                for g in range(2):
                    c0 = 2048 + 512 * g
                    m = mm(ps[64 * g:64 * g + 64, 2, :], Ebc[0:96, :], b12s[0:96, c0:c0 + 512], False, True)
                m.then_inc(sem("y_done"), 1)
                pe.wait_ge(sem("pg_ready"), b + 1)
                for tt, (t0, tn) in enumerate(TILES):
                    m = pe.transpose(ps[:, 4, t0:t0 + tn], Pg[0:tn, tt, :], ident[0:tn, 0:tn])
                m.then_inc(sem("pgT_done"), 1)
            pe.wait_ge(sem("ysb_ready"), nb + 1)
            pe.wait_ge(sem("pgT_ready"), nb + 1)
            for tt, (t0, tn) in enumerate(TILES):
                pe.wait_ge(sem(("comb_free", "hid_free", "xsel_ready")[tt]), (nb * 3 + 1, nb + 1, nb + 1)[tt])
                for g in range(2):
                    m = mm(ps[:, LAST_BANKS[tt] + g, :], PgT[64 * g:64 * g + 64, t0:t0 + P], y_sb[64 * g:64 * g + 64, :], True, True)
                m.then_inc(sem("comb_done"), 1)

            pe.wait_ge(sem("ple_in"), 48)
            pe.wait_ge(sem("xselT_ready"), nb + 1)
            for k in range(2):
                for tt, (t0, tn) in enumerate(TILES):
                    m = pe.transpose(ps[:, 4 + k, t0:t0 + tn], ptok[0:tn, tt, k * P:(k + 1) * P], ident[0:tn, 0:tn])
            m.then_inc(sem("pT_done"), 1)
            pe.wait_ge(sem("pT_ready"), 2)
            pe.wait_ge(landed[uslot[2]], 16 * (before[uslot[2]] + NE + 1))
            wp = slots[uslot[2]].rearrange("p k n -> p (k n)")[:, 0:2048].rearrange("p (k n) -> p k n", k=2)

            def ple_products(n, bank, lhsT, weights, kn):
                tt = min(n // 2, 2)
                t0, tn = TILES[tt]
                for k in range(kn):
                    if tt < 2:
                        m = mm(ps[:, bank, :], lhsT[:, k, t0:t0 + tn], weights(k, n % 2), k == 0, k == kn - 1)
                    else:
                        for g in range(2):
                            m = mm(ps[64 * g:64 * g + 64, bank, :], lhsT[:, k, t0:t0 + tn], weights(k, g), k == 0, k == kn - 1)
                return m

            for n in range(5):
                if n == 2:
                    pe.wait_ge(sem("comb_free"), nb * 3 + 2)
                elif n == 4:
                    pe.wait_ge(sem("comb_free"), nb * 3 + 4)
                ple_products(n, PLE_BANKS[n], pT, lambda k, g: wp[:, k, 512 * g:512 * g + 512], 2).then_inc(sem("ple_done"), 1)
            pe.wait_ge(sem("xn_ready"), 9)
            for k in range(KD):
                if k >= 2:
                    pe.wait_ge(sem("hT_ready"), KD + k - 1)
                for tt, (t0, tn) in enumerate(TILES):
                    m = pe.transpose(ps[:, k % 2, t0:t0 + tn], h2[0:tn, tt, k * P:(k + 1) * P], ident[0:tn, 0:tn])
                m.then_inc(sem("hT_done"), 1)
            pe.wait_ge(sem("hT_ready"), 2 * KD)
            for half in range(2):
                pe.wait_ge(landed[uslot[half]], 16 * (before[uslot[half]] + NE + 1))
            for n in range(5):
                if n >= 2:
                    pe.wait_ge(sem("ple_sig_ready"), n - 1)
                ple_products(n, n % 2, h3T, lambda k, g: slots[uslot[g]][:, k, :], KD).then_inc(sem("ple_done"), 1)

        @block.scalar
        def _(act):
            ch = Chain(act, sem("act_chain"))
            ACTF = nc.scalar.activation

            act.wait_ge(sem("x_in"), 32)
            act.wait_ge(sem("consts_in"), 16)
            act.wait_ge(sem("zeroed"), 4)
            for tt, (t0, tn) in enumerate(TILES):
                ch(ACTF(view(qkv_at + tt * D, D)[0:tn], x[0:tn, tt, :], ACT.Square, accum_out=ssq[0:tn, tt:tt + 1]))
            ch.wait()
            ACTF(rstd, ssq, ACT.Sqrt, bias=cst("eps"), scale=1.0 / D).then_inc(sem("rms_ready"), 1)
            act.wait_ge(sem("cols_ready"), 1)
            for k in range(KD):
                act.wait_ge(sem("hT_done"), k + 1)
                ACTF(hT[:, k, :], pj[k % 2][:, 0:TOK], ACT.Copy, scale=g1[:, k:k + 1]).then_inc(sem("hT_ready"), 1)

            def silu_part(n):
                act.wait_ge(sem("conv_done"), n + 1)
                if n >= 2:
                    act.wait_ge(sem("silu_done"), 2 * (n - 1))
                ACTF(sg[n % 2][:, 0:CW], cv[n % 2][:, 0:CW], ACT.Sigmoid).then_inc(sem("sig_done"), 1)

            act.wait_ge(sem("pool_zeroed"), 3)
            for n in range(FT):
                act.wait_ge(proj_done, n + 1)
                if n >= 3:
                    act.wait_ge(sem("conv_done"), n - 2)
                    act.wait_ge(sem("last3_done"), 2 * (n - 2))
                zs = zpad[n % 3][:, 3 + SEQ:].rearrange("p (b j) -> p b j", b=DB)
                ACTF(zs[:, :, 3:3 + DS], pj[n % 2][:, SEQ:TOK].rearrange("p (b j) -> p b j", b=DB), ACT.Copy)
                ACTF(zpad[n % 3][:, 3:3 + SEQ], pj[n % 2][:, 0:SEQ], ACT.Copy).then_inc(bank_free[n % 2], 1)
                if n:
                    silu_part(n - 1)
                m = n - 4
                if 0 <= m < 2 * H:
                    act.wait_ge(sem("sumsq_done"), m + 1)
                    ACTF(rs[:, m, :], ps[:, 2 + m % 6, 0:TOK], ACT.Copy).then_inc(sem("ln_done"), 1)
            silu_part(FT - 1)
            act.wait_ge(sem("ab_in"), 48)
            act.wait_ge(sem("abs_ready"), 1)
            ch(ACTF(alog, alog, ACT.Exp))
            ch(ACTF(beta, beta, ACT.Exp, scale=-1.0))
            ch.link(ACTF(tB, tB, ACT.Exp, scale=-1.0))
            ACTF(tB, tB, ACT.Ln, bias=1.0).then_inc(sem("softplus_ready"), 1)
            act.wait_ge(sem("ln_done"), 2 * H)
            ch.link(ACTF(rs, rs, ACT.Ln, bias=cst("eps")))
            ACTF(rs[:, 0:H], rs[:, 0:H], ACT.Exp, bias=cst("qscale"), scale=-0.5).then_inc(sem("rs_ready"), 1)
            ACTF(rs[:, H:2 * H], rs[:, H:2 * H], ACT.Exp, scale=-0.5).then_inc(sem("rs_ready"), 1)

            left = [N_GATE]

            def keep(count=1):
                for _ in range(count):
                    n = left[0]
                    left[0] += 1
                    act.wait_ge(proj_done, n + 1)
                    if N_V <= n < N_MA:
                        half, tt = divmod(n - N_V, 3)
                        if n == N_V:
                            act.wait_ge(sem("qk_normed"), 2)
                        if tt < 2:
                            m = ACTF(vtok[:, tt, 512 * half:512 * half + 512], pj[n % 2], ACT.Copy)
                        else:
                            for g in range(2):
                                c0 = 512 * half + 256 * g
                                m = ACTF(vtok[0:64, 2, c0:c0 + 256], pj[n % 2][64 * g:64 * g + 64, 0:256], ACT.Copy)
                        m.then_inc(bank_free[n % 2], 1)
                    else:
                        dst = gateT if n < N_U else uT if n < N_V else maT if n < N_MB else mbT
                        i = (n - N_GATE) % 8 if n < N_V else (n - N_MA) % 8
                        ACTF(dst[:, i, :], pj[n % 2][:, 0:TOK], ACT.Copy).then_inc(bank_free[n % 2], 1)

            act.wait_ge(sem("gce_ready"), 1)
            ch(ACTF(dcol, dcol, ACT.Exp))
            ch(ACTF(kdec[0:64], gce[0:64, 2, 0:8], ACT.Exp))
            ch.link(ACTF(gend, gend, ACT.Exp))
            keep(3)
            act.wait_ge(sem("newrows_stored"), 32)

            for tt, (t0, tn) in enumerate(TILES):
                L0 = sum(LEVELS[:tt])
                act.wait_ge(sem("gcrow_done"), tt + 1)
                if tt:
                    act.wait_ge(sem("qd_ready"), tt)
                    act.wait_ge(sem("rT_ready"), tt)
                ACTF(GR[:, :, 0:tn], G45(tn), ACT.Exp).then_inc(sem("GR_ready"), 1)
                act.wait_ge(sem("dd_ready"), tt + 1)
                ACTF(DBm[0:tn, :, 0:tn], DBm[0:tn, :, 0:tn], ACT.Exp).then_inc(sem("dec_ready"), 1)
                keep()
                act.wait_ge(sem("kt_done"), tt + 1)
                act.wait_ge(sem("dcol_ready"), 1)
                for h in range(H):
                    m = ACTF(kd[0:tn, h, :], G01()[0:tn, h, :], ACT.Copy, scale=dcol[0:tn, tt, h:h + 1])
                m.then_inc(sem("kd_ready"), 1)
                keep()
                for lev in range(LEVELS[tt]):
                    i = L0 + lev
                    if lev == 6:
                        act.wait_ge(sem("X_ready"), i)
                        for b in (0, HB):
                            ACTF(XT[b:b + HB, :, b:b + HB], XTd[b:b + HB], ACT.Copy)
                        act.wait_ge(sem("W_done"), i + 1)
                        ACTF(Wd[64:128], blocks64(6)[64:128], ACT.Copy).then_inc(sem("W_ready"), 1)
                    elif lev:
                        act.wait_ge(sem("W_done"), i + 1)
                        ACTF(Wd[0:tn], blocks64(6)[0:tn], ACT.Copy).then_inc(sem("W_ready"), 1)
                    if lev or tt < 2:
                        keep(2 if lev in (1, 3) and tt < 2 else 1)
                if tt < 2:
                    act.wait_ge(sem("r_done"), tt + 1)
                    ACTF(r[0:tn], G45()[0:tn], ACT.Copy).then_inc(sem("r_ready"), 1)
                else:
                    keep()
                    for s, (_, sn) in enumerate(TILES):
                        ACTF(vtok[0:sn, s, :], vtok[0:sn, s, :], ACT.Gelu, accum_out=msum[0:sn, s:s + 1]).then_inc(sem("gelu_ready"), 1)
                    ACTF(uT, uT, ACT.Gelu).then_inc(sem("ugelu_ready"), 1)
                    keep()
                act.wait_ge(sem("u_done"), tt + 1)
                ACTF(W[0:tn], G01()[0:tn], ACT.Copy).then_inc(sem("u_ready"), 1)
                keep()
                act.wait_ge(sem("sumsq_done"), 2 * H + tt + 1)
                ACTF(rT[:, :, 0:tn], G01(tn), ACT.Ln, bias=cst("eps"), scale=1.0 / P).then_inc(sem("ln_done"), 1)
                act.wait_ge(sem("ln_done"), 2 * H + tt + 1)
                ACTF(rT[:, :, 0:tn], rT[:, :, 0:tn], ACT.Exp, scale=-0.5).then_inc(sem("rs_ready"), 1)
                if tt < 2:
                    keep()

            act.wait_ge(sem("o_normed"), 3)
            ACTF(sgm, gateT, ACT.Sigmoid).then_inc(sem("branch_sig_ready"), 1)
            keep(2)
            assert left[0] == N_YA
            for n in (N_YA - 1, N_YA - 2):
                evacuated(act, n)
            ACTF(maT, maT, ACT.Sigmoid).then_inc(sem("branch_sig_ready"), 1)
            ACTF(mbT, mbT, ACT.Sigmoid).then_inc(sem("branch_sig_ready"), 1)
            for tt, (t0, tn) in enumerate(TILES):
                act.wait_ge(sem("vc_ready"), tt + 1)
                ch.link(ACTF(view(scratch + 6656, D)[0:tn], vtok[0:tn, tt, :], ACT.Square, accum_out=mvar[0:tn, tt:tt + 1]))
            ACTF(mrs, mvar, ACT.Sqrt, bias=cst("eps"), scale=1.0 / D).then_inc(sem("ln_std_ready"), 1)
            def rms(ready):
                for tt, (t0, tn) in enumerate(TILES):
                    ready(tt)
                    ch(ACTF(h2[0:tn, tt, :], x[0:tn, tt, :], ACT.Square, accum_out=ssq[0:tn, tt:tt + 1]))
                ch.wait()
                ACTF(rstd, ssq, ACT.Sqrt, bias=cst("eps"), scale=1.0 / D).then_inc(sem("rms_ready"), 1)

            rms(lambda tt: evacuated(act, N_WO + 3 + tt))
            for k in range(KD):
                n = N_END + k
                act.wait_ge(sem("hT_done"), KD + k + 1)
                ACTF(h2T[:, k, :], pj[n % 2][:, 0:TOK], ACT.Copy, scale=g2[:, k:k + 1]).then_inc(bank_free[n % 2], 1)
            act.wait_ge(sem("top_ready"), 1)
            ACTF(gates[:, :, 0:TOPK], gates[:, :, 0:TOPK], ACT.Exp).then_inc(sem("gexp_ready"), 1)

            act.wait_ge(sem("tables_ready"), 1)
            nb = act.value_load(tab[0:1, 96 + NE - 1:96 + NE], min_val=1, max_val=MAXB)

            def rows_out(value):
                act.wait_ge(sem("sel_done"), value)
                ACTF(xsel, ps[:, 3, :], ACT.Copy).then_inc(sem("xsel_ready"), 1)

            rows_out(1)
            with act.Fori(0, nb) as b:
                act.wait_ge(sem("glu_gate_ready"), b + 1)
                ACTF(s_sb, g_sb, ACT.Sigmoid, scale=ALPHA).then_inc(sem("glu_sig_ready"), 1)
                rows_out(b + 2)
                act.wait_ge(sem("actT_done"), b + 1)
                ACTF(actT.rearrange("p j c -> p (j c)"), ps[:, 4, :], ACT.Copy).then_inc(sem("actT_ready"), 1)
                act.wait_ge(sem("y_done"), b + 1)
                ACTF(y_sb, ps[:, 2, :], ACT.Copy).then_inc(sem("ysb_ready"), 1)
                act.wait_ge(sem("pgT_done"), b + 2)
                ACTF(PgT[:, 0:TOK], ps[:, 4, 0:TOK], ACT.Copy).then_inc(sem("pgT_ready"), 1)

            act.wait_ge(sem("pT_done"), 1)
            for k in range(2):
                ACTF(pT[:, k, :], ps[:, 4 + k, 0:TOK], ACT.Copy).then_inc(sem("pT_ready"), 1)
            rms(lambda tt: act.wait_ge(sem("comb_free"), nb * 3 + 2 + tt))
            for k in range(KD):
                act.wait_ge(sem("hT_done"), 2 * KD + k + 1)
                ACTF(h3T[:, k, :], ps[:, k % 2, 0:TOK], ACT.Copy, scale=g3[:, k:k + 1]).then_inc(sem("hT_ready"), 1)
            for n in range(5):
                act.wait_ge(sem("ple_done"), 5 + n + 1)
                if n >= 2:
                    act.wait_ge(sem("ple_added"), n - 1)
                ACTF([g_sb, u_sb][n % 2], ps[:, n % 2, :], ACT.Sigmoid).then_inc(sem("ple_sig_ready"), 1)
                if n % 2 or n == 4:
                    tt = n // 2
                    tn = TILES[tt][1]
                    act.wait_ge(sem("ple_added"), n + 1)
                    ch.link(ACTF(h2[0:tn, tt, :], x[0:tn, tt, :], ACT.Square, accum_out=ssq[0:tn, tt:tt + 1]))
                    ACTF(rstd[0:tn, tt:tt + 1], ssq[0:tn, tt:tt + 1], ACT.Sqrt, bias=cst("eps", tn), scale=1.0 / D).then_inc(sem("rms_ready"), 1)

        @block.vector
        def _(dve):
            ch = Chain(dve, sem("dve_chain"))
            TT, TS, STT = dve.tensor_tensor, dve.tensor_scalar, dve.scalar_tensor_tensor

            def over_heads(ap, rows, n):
                return ap.rearrange("p (a c) -> p a c", a=1).broadcast_to([rows, H, n])

            dve.memset(ssq, 1.0).then_inc(sem("zeroed"), 1)
            dve.memset(mvar, 1.0).then_inc(sem("zeroed"), 1)
            dve.memset(msum, 0.0).then_inc(sem("zeroed"), 1)
            dve.memset(ab, 0.0).then_inc(sem("zeroed"), 1)
            dve.wait_ge(sem("rows_turned"), 1)
            dve.tensor_copy(colsT[:, 0:121], ps[:, 0, 0:121]).then_inc(sem("cols_ready"), 1)
            for g in range(6):
                dve.wait_ge(sem("old_done"), g + 1)
                dve.tensor_copy(oldT[:, 4 * g:4 * g + 4, :], ps[:, 2 + g, 0:96].rearrange("p (f j) -> p f j", f=4)).then_inc(sem("old_turned"), 1)

            def normalise(k, dst):
                dve.wait_ge(sem("rms_ready"), k)
                ch.link(dve.reciprocal(rstd, rstd))
                for tt, (t0, tn) in enumerate(TILES):
                    yield TS(dst[0:tn, tt, :], x[0:tn, tt, :], rstd[0:tn, tt:tt + 1], None, ALU.mult)

            for m in normalise(1, x):
                m.then_inc(sem("xn_ready"), 1)

            def samples(w):
                return w[:, 3 + SEQ:3 + SEQ + DB * (3 + DS)].rearrange("p (b j) -> p b j", b=DB)[:, :, 0:DS]

            def silu_mul(n):
                dve.wait_ge(sem("sig_done"), n + 1)
                TT(qkvT[:, n, 0:SEQ], cv[n % 2][:, 0:SEQ], sg[n % 2][:, 0:SEQ], ALU.mult).then_inc(sem("silu_done"), 1)
                TT(qkvT[:, n, SEQ:TOK].rearrange("p (b j) -> p b j", b=DB), samples(cv[n % 2]), samples(sg[n % 2]),
                   ALU.mult).then_inc(sem("silu_done"), 1)

            dve.wait_ge(sem("cols_ready"), 1)
            for n in range(FT):
                evacuated(dve, n)
                dve.wait_ge(sem("old_filled"), n + 1)
                z, a = zpad[n % 3], cv[n % 2][:, 0:CW]
                if n >= 2:
                    dve.wait_ge(sem("silu_done"), 2 * (n - 1))
                ch.link(TS(a, z[:, 0:CW], g_conv[:, 0, n:n + 1], None, ALU.mult))
                for i in range(1, TAPS - 1):
                    ch.link(STT(a, z[:, i:i + CW], g_conv[:, i, n:n + 1], a, ALU.mult, ALU.add))
                STT(a, z[:, TAPS - 1:TAPS - 1 + CW], g_conv[:, TAPS - 1, n:n + 1], a, ALU.mult, ALU.add).then_inc(sem("conv_done"), 1)
                if n:
                    silu_mul(n - 1)
            silu_mul(FT - 1)

            dve.wait_ge(proj_done, N_AB + 1)
            dve.wait_ge(sem("zeroed"), 4)
            dve.wait_ge(sem("ab_in"), 48)
            ch(dve.tensor_copy(ab[0:64, 2, :], pj[0][0:64, 32:48]))
            dve.tensor_copy(ab[:, 0:2, :], pj[0][:, 0:32].rearrange("p (a c) -> p a c", a=2)).then_inc(bank_free[0], 1)
            evacuated(dve, N_AB)
            ch.wait()

            def wide8(ap):
                return ap.rearrange("p (a c) -> p a c", a=1).broadcast_to([P, 3, 8])
            ch(TS(beta, ab[:, :, 8:16], -80.0, None, ALU.max))
            ch.link(TT(tA, ab[:, :, 0:8], wide8(dtb), ALU.add))
            ch.link(TS(tB, tA, -1.0, None, ALU.mult))
            TT(tB, tB, tA, ALU.max).then_inc(sem("abs_ready"), 1)
            dve.wait_ge(sem("softplus_ready"), 1)
            ch(TS(beta, beta, 1.0, None, ALU.add))
            ch.link(STT(tA, tA, 0.0, tB, ALU.max, ALU.add))
            ch(dve.reciprocal(beta, beta))
            STT(gg, tA, -1.0, wide8(alog), ALU.mult, ALU.mult).then_inc(sem("g_ready"), 3)

            for g in range(6):
                dve.wait_ge(sem("newrows_done"), g + 1)
                dve.tensor_copy(new_rows[0:27, 512 * g:512 * g + 512], ps[0:27, 2 + g, :]).then_inc(sem("newrows_ready"), 1)
            for i in range(2):
                dve.wait_ge(sem("rs_ready"), i + 1)
                TT(qkvT[:, H * i:H * i + H, :], qkvT[:, H * i:H * i + H, :], rs[:, H * i:H * i + H, :], ALU.mult).then_inc(sem("qk_normed"), 1)
            dve.memset(gce, 0.0).then_inc(sem("zeroed"), 1)
            dve.wait_ge(sem("zeroed"), 5)
            dve.wait_ge(sem("cum_done"), 1)
            ch(dve.tensor_copy(gce[0:64, 2, :], ps[0:64, 7, 32:48]))
            ch.link(dve.tensor_copy(gce[:, 0:2, :], ps[:, 7, 0:32].rearrange("p (a c) -> p a c", a=2)))
            ch(dve.tensor_copy(gend, gce[:, :, 8:16]))
            TT(dcol, gce[:, :, 8:16], gce[:, :, 0:8], ALU.subtract).then_inc(sem("gce_ready"), 1)

            for tt, (t0, tn) in enumerate(TILES):
                L0 = sum(LEVELS[:tt])
                tri = cst("tri8" if tt == 2 else "tri", tn, tn)
                if tt:
                    dve.wait_ge(sem("u_done"), tt)
                else:
                    dve.wait_ge(sem("g_ready"), 3)
                    dve.wait_ge(sem("newrows_ready"), 6)
                TT(X[0:tn, :, 0:tn], over_heads(tri, tn, tn),
                   gg[0:tn, tt, :].rearrange("p (a c) -> p a c", c=1).broadcast_to([tn, H, tn]), ALU.mult).then_inc(sem("RH_ready"), 1)
                dve.wait_ge(sem("GR_ready"), tt + 1)
                if tt:
                    dve.wait_ge(sem("X_ready"), L0)
                for h in range(H):
                    m = TS(DBm[0:tn, h, 0:tn], G45(tn)[0:tn, h, :], gce[0:tn, tt, h:h + 1], 0.0, ALU.subtract, ALU.min)
                m.then_inc(sem("dd_ready"), 1)
                if tt == 0:
                    dve.wait_ge(sem("act_chain"), 10)
                    ch.link(TS(kdec[0:64], kdec[0:64], -1.0, None, ALU.mult))
                    TT(dcol, dcol, beta, ALU.mult).then_inc(sem("dcol_ready"), 1)
                dve.wait_ge(sem("dec_ready"), tt + 1)
                for h in range(H):
                    m = STT(DBm[0:tn, h, 0:tn], DBm[0:tn, h, 0:tn], beta[0:tn, tt, h:h + 1], tri, ALU.mult, ALU.mult)
                ch.link(m)
                dve.wait_ge(sem("kk_done"), tt + 1)
                if tt:
                    dve.wait_ge(sem("o_done"), tt)
                    dve.wait_ge(sem("Al_ready"), masks_before(tt))
                if tt < 2:
                    TT(AToff[0:64], G01()[0:64, :, HB:], DBm[0:64, :, HB:], ALU.mult)
                    TT(ATd[64:128], G01()[64:128, :, HB:], DBm[64:128, :, HB:], ALU.mult)
                TT(ATd[0:64], G01(tn)[0:64, :, 0:HB], DBm[0:64, :, 0:HB], ALU.mult).then_inc(sem("AT_ready"), 1)
                TT(mT[0:tn, :, 0:tn], G23(tn)[0:tn], DBm[0:tn, :, 0:tn], ALU.mult).then_inc(sem("mT_ready"), 1)
                for lev in range(LEVELS[tt]):
                    i = L0 + lev
                    last = lev == LEVELS[tt] - 1
                    if lev == 0:
                        dve.wait_ge(sem("Al_ready"), masks_before(tt) + 1)
                        dve.wait_ge(sem("W_done"), i + 1)
                        ch(TT(XTd[0:tn], over_heads(cst("ident64", tn), tn, HB), Al[0][0:tn], ALU.subtract))
                        TT(Xd[0:tn], over_heads(cst("ident64", tn), tn, HB), blocks64(6)[0:tn], ALU.subtract).then_inc(sem("X_ready"), 1)
                    elif lev == 6:
                        dve.wait_ge(sem("D_done"), i - tt)
                        TS(XT[0:64, :, HB:], blocks64(4)[0:64], -1.0, None, ALU.mult).then_inc(sem("X_ready"), 1)
                    else:
                        dve.wait_ge(sem("D_done"), i - tt)
                        dve.wait_ge(sem("X_ready"), i)
                        if not last:
                            ch(TT(Xd[0:tn], Xd[0:tn], blocks64(2)[0:tn], ALU.subtract))
                        TT(XTd[0:tn], XTd[0:tn], blocks64(4)[0:tn], ALU.subtract).then_inc(sem("X_ready"), 1)
                vT = qkvT[:, 2 * H:3 * H, t0:t0 + tn]
                if tt == 0:
                    dve.tensor_copy(rT[:, :, 0:tn], vT).then_inc(sem("rT_ready"), 1)
                elif tt == 1:
                    dve.wait_ge(sem("kS_done"), 1)
                    ch.link(TT(rT[:, :, 0:tn], G01(tn), GR[:, :, 0:tn], ALU.mult))
                    TT(rT[:, :, 0:tn], vT, rT[:, :, 0:tn], ALU.subtract).then_inc(sem("rT_ready"), 1)
                    dve.tensor_copy(qS[:, :, 0:tn], G23(tn)).then_inc(sem("qS_ready"), 1)
                else:
                    dve.wait_ge(sem("r_done"), 3)
                    for h in range(H):
                        dve.wait_ge(sem("kS_head"), h + 1)
                        bank = 2 + 2 * (h % 2)
                        mask8 = cst("seq8").rearrange("p (a c) -> p a c", c=1)
                        TT(W, ps[:, bank:bank + 2, :].rearrange("p a (b v) -> p (a b) v", v=P), mask8.broadcast_to([P, DB, P]),
                           ALU.mult).then_inc(sem("kS_read"), 1)
                        dve.wait_ge(sem("kS_read"), h + 1)
                        ch.link(dve.tensor_reduce(r[:, h, :], W.rearrange("p b v -> p v b"), AX.X, ALU.add))
                        STT(r[0:64, h, :], r[0:64, h, :], kdec[0:64, h:h + 1], G45()[0:64, h, :], ALU.mult, ALU.add).then_inc(sem("r_ready"), 1)
                o = oT[:, :, t0:t0 + tn]
                dve.wait_ge(sem("o_done"), tt + 1)
                dve.wait_ge(sem("qd_ready"), tt + 1)
                if tt != 1:
                    ch.link(dve.tensor_copy(o, G23(tn)))
                else:
                    dve.wait_ge(sem("qS_ready"), 1)
                    ch.link(TT(o, qS[:, :, 0:tn], G23(tn), ALU.add))
                TT(qS[:, :, 0:tn], o, o, ALU.mult).then_inc(sem("osq_ready"), 1)
                dve.wait_ge(sem("osq_ready"), tt + 1)
                dve.nop().then_inc(sem("o_ready"), 1)
                if tt == 0:
                    dve.wait_ge(sem("S_done"), 1)
                    dve.tensor_copy(S, G45()).then_inc(sem("S_ready"), 1)
                elif tt == 1:
                    dve.wait_ge(sem("S_done"), 2)
                    dve.wait_ge(sem("S_ready"), 1)
                    for h in range(H):
                        m = STT(S[:, h, :], S[:, h, :], gend[:, 1, h:h + 1], G45()[:, h, :], ALU.mult, ALU.add)
                    m.then_inc(sem("S_ready"), 1)
                dve.wait_ge(sem("rs_ready"), 2 + tt + 1)
                TT(o, o, rT[:, :, 0:tn], ALU.mult).then_inc(sem("o_normed"), 1)
            for h in range(H):
                dve.wait_ge(sem(f"S0_in{h % 4}"), 16 * (3 + h // 4))
                ch.link(TT(S0[h % 4], S0[h % 4], GR[:, h, DS - 1:64:DS].rearrange("p (a c) -> p a c", c=1).broadcast_to([P, DB, P]),
                           ALU.mult))
                dve.wait_ge(sem("S0_product"), 2 * h + 2)
                bank = [6, 4][h % 2]
                TT(S0[h % 4].rearrange("p b v -> p (b v)"), S0[h % 4].rearrange("p b v -> p (b v)"),
                   ps[:, bank:bank + 2, :].rearrange("p a c -> p (a c)"), ALU.add).then_inc(sem("S0_new"), 1)
                if h == 1:
                    dve.wait_ge(sem("branch_sig_ready"), 1)
                    dve.wait_ge(sem("o_normed"), 3)
                    ch.link(TT(gateT, gateT, sgm, ALU.mult))
                elif h == 4:
                    STT(oT, oT, dng, gateT, ALU.mult, ALU.mult).then_inc(sem("gated_ready"), 1)

            dve.wait_ge(sem("gelu_ready"), 3)
            ch.link(TS(msum, msum, 1.0 / D, None, ALU.mult))
            for tt, (t0, tn) in enumerate(TILES):
                TS(vtok[0:tn, tt, :], vtok[0:tn, tt, :], msum[0:tn, tt:tt + 1], None, ALU.subtract).then_inc(sem("vc_ready"), 1)

            def norm_v(tt):
                tn = TILES[tt][1]
                if tt == 0:
                    dve.wait_ge(sem("ln_std_ready"), 1)
                    ch.link(dve.reciprocal(mrs, mrs))
                    dve.wait_ge(sem("mlp_in"), 16 * 12)
                    dve.wait_ge(sem("vc_ready"), 3)
                ch.link(STT(vtok[0:tn, tt, :], vtok[0:tn, tt, :], mrs[0:tn, tt:tt + 1], lng[0:tn], ALU.mult, ALU.mult))
                TT(vtok[0:tn, tt, :], vtok[0:tn, tt, :], lnb[0:tn], ALU.add).then_inc(sem("vnorm_ready"), 1)

            def merge_a(i):
                n = N_YA + i
                dve.wait_ge(proj_done, n + 1)
                dve.wait_ge(sem("gated_ready"), 1)
                TT(mixT[:, i, :], maT[:, i, :], pj[n % 2][:, 0:TOK], ALU.mult).then_inc(bank_free[n % 2], 1)

            dve.wait_ge(sem("branch_sig_ready"), 3)
            for i in range(4):
                merge_a(i)
                if i:
                    norm_v(i - 1)
            dve.wait_ge(sem("wT_done"), 1)
            TT(WT, G01(), over_heads(cst("tri"), P, P), ALU.mult).then_inc(sem("WT_ready"), 1)
            TT(WT8[0:64], G23(64)[0:64], over_heads(cst("tri8", 64, 64), 64, 64), ALU.mult).then_inc(sem("WT_ready"), 1)
            for i in range(4, 6):
                merge_a(i)
            dve.wait_ge(sem("ugelu_ready"), 1)
            for tt, (t0, tn) in enumerate(TILES):
                for a in range(2):
                    k = 2 * tt + a
                    dve.wait_ge(sem("mix_done"), k + 1)
                    sv = ps[:, 2 + k, :].rearrange("p (g c) -> p g c", g=4)[:, :, 0:tn]
                    st = [stmp, stmp2][k % 2].rearrange("p (g c) -> p g c", g=4)[:, :, 0:tn]
                    if k >= 2:
                        dve.wait_ge(sem("us_ready"), k - 1)
                    if tt < 2:
                        ch.link(TT(st, sv, bsb[:, 4 * a:4 * a + 4, :], ALU.add))
                    else:
                        for g in range(4):
                            bias = bsb[:, 4 * a + g, 0:DS].rearrange("p (b j) -> p b j", b=1).broadcast_to([P, DB, DS])
                            m = TT(st[:, g, :].rearrange("p (b j) -> p b j", b=DB), sv[:, g, :].rearrange("p (b j) -> p b j", b=DB), bias, ALU.add)
                        ch.link(m)
                    TT(uT[:, 4 * a:4 * a + 4, t0:t0 + tn], uT[:, 4 * a:4 * a + 4, t0:t0 + tn], st, ALU.mult).then_inc(sem("us_ready"), 1)
            dve.wait_ge(sem("us_ready"), 6)
            for i in range(6, 8):
                merge_a(i)
            for i in range(8):
                n = N_YB + i
                dve.wait_ge(proj_done, n + 1)
                evacuated(dve, N_YA + 6)
                evacuated(dve, N_YA + 7)
                tmp = [stmp, stmp2][i % 2][:, 0:TOK]
                if i >= 2:
                    dve.wait_ge(sem("merged"), i - 1)
                TT(tmp, mbT[:, i, :], pj[n % 2][:, 0:TOK], ALU.mult).then_inc(bank_free[n % 2], 1)
                evacuated(dve, n)
                TT(mixT[:, i, :], mixT[:, i, :], tmp, ALU.add).then_inc(sem("merged"), 1)
            dve.wait_ge(sem("x_in"), 64)
            dve.wait_ge(sem("vnorm_ready"), 3)
            for half in range(2):
                for tt, (t0, tn) in enumerate(TILES):
                    n = N_WO + 3 * half + tt
                    dve.wait_ge(proj_done, n + 1)
                    if tt < 2:
                        xa = x[:, tt, 512 * half:512 * half + 512]
                        TT(xa, xa, pj[n % 2], ALU.add).then_inc(bank_free[n % 2], 1)
                    else:
                        xa, xb = (x[0:64, 2, 512 * half + 256 * g:512 * half + 256 * g + 256] for g in range(2))
                        ch.link(dve.tensor_copy(moved, pj[n % 2][64:128, 0:256]))
                        ch.link(TT(xb, xb, moved, ALU.add))
                        TT(xa, xa, pj[n % 2][0:64, 0:256], ALU.add).then_inc(bank_free[n % 2], 1)

            for n in (N_WO + 4, N_WO + 5):
                evacuated(dve, n)
            for m in normalise(2, h2):
                m.then_inc(sem("xn_ready"), 1)
            ch(dve.memset(logit[:, 2, :], 0.0))
            dve.wait_ge(sem("router_in"), 16 * 4)
            ex = cst("expert")
            dve.wait_ge(sem("logits_done"), 1)
            dve.tensor_copy(logitT[0:NE], ps[0:NE, 5, 0:TOK]).then_inc(sem("logitT_ready"), 1)
            dve.wait_ge(sem("logits_done"), 2)
            ch.wait()
            ch(TT(logit[0:64, 2, :], ps[0:64, 6, 2 * NE:3 * NE], rbias[0:64], ALU.add))
            ch.link(TT(logit[:, 0:2, :], ps[:, 6, 0:2 * NE].rearrange("p (t e) -> p t e", e=NE),
                       rbias.rearrange("p (a e) -> p a e", a=1).broadcast_to([P, 2, NE]), ALU.add))
            for tt in range(3):
                ch(dve.max(top8[:, tt, :], logit[:, tt, :]))
            ch.wait()
            TT(gates[:, :, 0:TOPK], top8[:, :, 0:TOPK], top8[:, :, 0:1].broadcast_to([P, 3, TOPK]), ALU.subtract).then_inc(sem("top_ready"), 1)
            for tt in range(3):
                ch(dve.max_index(idx8[:, tt, :].bitcast(U32), top8[:, tt, :], logit[:, tt, :]))
            ch.wait()
            ch.link(dve.tensor_copy(idxf, idx8.bitcast(U32)))

            def choices(ap):
                return ap.rearrange("p (t k e) -> p t k e", t=3, k=TOPK)
            ch.link(TT(choices(chosen), ex.rearrange("p (t k e) -> p t k e", t=1, k=1).broadcast_to([P, 3, TOPK, NE]),
                       idxf[:, :, 0:TOPK].rearrange("p t (k e) -> p t k e", e=1).broadcast_to([P, 3, TOPK, NE]), ALU.is_equal))
            dve.tensor_reduce(mask, choices(chosen).rearrange("p t k e -> p t e k"), AX.X, ALU.add).then_inc(sem("mask_ready"), 1)
            dve.wait_ge(sem("gexp_ready"), 1)
            ch.link(dve.tensor_reduce(gsum.rearrange("p (t a) -> p t a", a=1), gates[:, :, 0:TOPK], AX.X, ALU.add))
            ch.link(dve.reciprocal(gsum, gsum))
            ch.link(TT(gates[:, :, 0:TOPK], gates[:, :, 0:TOPK], gsum.rearrange("p (t a) -> p t a", a=1).broadcast_to([P, 3, TOPK]), ALU.mult))
            ch.link(TT(choices(chosen_g), choices(chosen),
                       gates[:, :, 0:TOPK].rearrange("p t (k e) -> p t k e", e=1).broadcast_to([P, 3, TOPK, NE]), ALU.mult))
            ch.link(dve.tensor_reduce(gmat, choices(chosen_g).rearrange("p t k e -> p t e k"), AX.X, ALU.add))
            dve.wait_ge(sem("mask_ready"), 1)
            dve.wait_ge(sem("rank_done"), 1)
            q = slice(0, NE)
            ch.link(dve.tensor_copy(cnt[q, 8:9], ps[q, 4, 0:1]))
            ch.link(TS(cnt[q, 0:4], cst("thr", NE), cnt[q, 8:9], None, ALU.is_lt))
            ch.link(dve.tensor_reduce(cnt[q, 9:10], cnt[q, 0:4], AX.X, ALU.add))
            TS(cnt[q, 4:5], cnt[q, 9:10], 1.0, None, ALU.add).then_inc(sem("blocks_ready"), 1)
            for tt, (t0, tn) in enumerate(TILES):
                R = slice(0, tn)
                ch.link(TS(etmp[R, tt, :], mask[R, tt, :], -FAR, FAR, ALU.mult, ALU.add))
                TT(pos[R, tt, :], etmp[R, tt, :], ps[R, 3, NE * tt:NE * tt + NE], ALU.add).then_inc(sem("rank_ready"), 1)
            dve.wait_ge(sem("through_done"), 1)
            dve.wait_ge(sem("blocks_ready"), 1)
            ch.link(dve.tensor_copy(cnt[q, 5:6], ps[q, 4, 8:9]))
            ch.link(TT(cnt[q, 6:7], cnt[q, 5:6], cnt[q, 4:5], ALU.subtract))
            ch.link(TS(cnt[q, 7:8], cnt[q, 6:7], float(SLOTS), None, ALU.mult))
            ch.link(TS(Eb3f[q], cst("block", NE), cnt[q, 5:6], None, ALU.is_lt))
            ch.link(STT(Eb[q], cst("block", NE), cnt[q, 6:7], Eb3f[q], ALU.is_ge, ALU.mult))
            for i in range(3):
                m = dve.tensor_copy(Eb3[32 * i:32 * i + 32, :], Eb[q])
                ch(m)
            ch.wait()
            dve.nop().then_inc(sem("E_ready"), 1)
            dve.wait_ge(sem("rankT_done"), 1)
            TS(posT[q], ps[q, 5, 0:TOK], cnt[q, 7:8], None, ALU.add).then_inc(sem("rankT_ready"), 1)
            dve.tensor_copy(gmT[q], ps[q, 6, 0:TOK]).then_inc(sem("rankT_ready"), 1)
            dve.wait_ge(sem("perblock_done"), 1)
            for tt, (t0, tn) in enumerate(TILES):
                R = slice(0, tn)
                ch(STT(posb[R, tt, :], cst("block", tn), -float(SLOTS), ps[R, 7, SLOTS * tt:SLOTS * tt + SLOTS], ALU.mult, ALU.add))
                ch(dve.tensor_copy(gateb[R, tt, :], ps[R, 7, 256 + SLOTS * tt:256 + SLOTS * tt + SLOTS]))
            ch(dve.tensor_copy(tab[0:1, 0:64], ps[0:1, 4, 128:192]))
            ch.link(dve.tensor_copy(tab[0:1, 96:128], ps[0:1, 4, 192:224]))
            dve.nop().then_inc(sem("tables_ready"), 1)

            dve.nop().then_inc(sem("hid_free"), 1)
            dve.nop().then_inc(sem("comb_free"), 1)
            nb = dve.value_load(tab[0:1, 96 + NE - 1:96 + NE], min_val=1, max_val=MAXB)

            def pick(b):
                for tt, (t0, tn) in enumerate(TILES):
                    m = TS(Psel[0:tn, tt, :], cst("slot", tn, SLOTS), posb[0:tn, tt, bass.ds(b, 1)] if not isinstance(b, int)
                           else posb[0:tn, tt, b:b + 1], None, ALU.is_equal)
                m.then_inc(sem("psel_ready"), 1)

            def rows_turned(value):
                dve.wait_ge(sem("xT_done"), value)
                TT(xselT.rearrange("p (g j) s -> p g j s", g=2), ps[:, 5, :].rearrange("p (j g s) -> p g j s", j=4, g=2),
                   g2.rearrange("p (g j a) -> p g j a", g=2, a=1).broadcast_to([P, 2, 4, SLOTS]), ALU.mult).then_inc(sem("xselT_ready"), 1)

            pick(0)
            dve.memset(y_sb, 0.0).then_inc(sem("ysb_ready"), 1)
            dve.memset(PgT, 0.0).then_inc(sem("pgT_ready"), 1)
            rows_turned(1)
            with dve.Fori(0, nb) as b:
                dve.wait_ge(sem("pgT_done"), b + 1)
                dve.tensor_copy(Ebc[0:96, :], Eb3[0:96, bass.ds(b, 1)].broadcast_to([96, SLOTS])).then_inc(sem("ebc_ready"), 1)
                for tt, (t0, tn) in enumerate(TILES):
                    m = TS(Pg[0:tn, tt, :], cst("slot", tn), posb[0:tn, tt, bass.ds(b, 1)], gateb[0:tn, tt, bass.ds(b, 1)], ALU.is_equal, ALU.mult)
                m.then_inc(sem("pg_ready"), 1)
                dve.wait_ge(sem("sel_done"), b + 1)
                pick(b + 1)
                for tt, (t0, tn) in enumerate(TILES):
                    dve.wait_ge(sem("comb_done"), b * 3 + tt + 1)
                    dve.wait_ge(sem("comb_free"), b * 3 + 1)
                    TT(x[0:tn, tt, :], x[0:tn, tt, :], ps[0:tn, 6:8, :].rearrange("p a c -> p (a c)"), ALU.add).then_inc(sem("comb_free"), 1)
                dve.wait_ge(sem("hid_done"), b + 1)
                TS(g_sb, ps[:, 0, :], LIMIT, None, ALU.min).then_inc(sem("glu_gate_ready"), 1)
                TS(u_sb, ps[:, 1, :], LIMIT, -LIMIT, ALU.min, ALU.max).then_inc(sem("hid_free"), 1)
                dve.wait_ge(sem("hid_free"), b + 2)
                STT(u_sb, u_sb, 1.0, g_sb, ALU.add, ALU.mult).then_inc(sem("glu_up_ready"), 1)
                dve.wait_ge(sem("glu_up_ready"), b + 1)
                dve.wait_ge(sem("glu_sig_ready"), b + 1)
                TT(a_sb, u_sb, s_sb, ALU.mult).then_inc(sem("act_ready"), 1)
                rows_turned(b + 2)
            for tt, (t0, tn) in enumerate(TILES):
                dve.wait_ge(sem("comb_done"), nb * 3 + tt + 1)
                dve.wait_ge(sem("comb_free"), nb * 3 + 1)
                b0 = LAST_BANKS[tt]
                TT(x[0:tn, tt, :], x[0:tn, tt, :], ps[0:tn, b0:b0 + 2, :].rearrange("p a c -> p (a c)"), ALU.add).then_inc(sem("comb_free"), 1)

            dve.wait_ge(sem("comb_free"), nb * 3 + 4)
            for m in normalise(3, h2):
                m.then_inc(sem("xn_ready"), 1)
            for n in range(5):
                tt = min(n // 2, 2)
                tn = TILES[tt][1]
                dve.wait_ge(sem("ple_sig_ready"), n + 1)
                dve.wait_ge(sem("ple_done"), n + 1)
                s_ = [g_sb, u_sb][n % 2]
                ch.link(TT(s_, s_, ps[:, PLE_BANKS[n], :], ALU.mult))
                if tt < 2:
                    xa = x[:, tt, 512 * (n % 2):512 * (n % 2) + 512]
                    TT(xa, xa, s_, ALU.add).then_inc(sem("ple_added"), 1)
                else:
                    xa, xb = x[0:64, 2, 0:512], x[0:64, 2, 512:1024]
                    ch(dve.tensor_copy(ple_moved, s_[64:128]))
                    ch.link(TT(xa, xa, s_[0:64], ALU.add))
                    TT(xb, xb, ple_moved, ALU.add).then_inc(sem("ple_added"), 1)
                if n % 2 or n == 4:
                    dve.wait_ge(sem("rms_ready"), 4 + tt)
                    ch.link(dve.reciprocal(rstd[0:tn, tt:tt + 1], rstd[0:tn, tt:tt + 1]))
                    STT(x[0:tn, tt, :], x[0:tn, tt, :], rstd[0:tn, tt:tt + 1], fng[0:tn], ALU.mult, ALU.mult).then_inc(sem("y_ready"), 1)


INS = ("x_prompt", "x_sample", "state_delta", "state_conv", "p_prompt", "p_sample", "norm1_g", "w_in", "conv_w",
       "a_log", "dt_bias", "dn_norm_g", "w_proj_a", "gm_ln_g", "gm_ln_b", "gm_ws", "gm_bs", "w_proj_b", "w_out",
       "norm2_g", "router_w", "router_b", "moe_w1", "moe_b1", "moe_w2", "moe_b2", "norm3_g", "ple_w", "ple_gate_w",
       "final_norm_g")
OUTS = (("out_yp", (1, SEQ, D)), ("out_ys", (DB, DS, D)), ("out_sd_p", (1, 1, H, P, P)), ("out_sc_p", (1, 1, TAPS - 1, QKV)),
        ("out_sd_s", (1, DB, H, P, P)), ("out_sc_s", (1, DB, TAPS - 1, QKV)), ("out_gv", (1, DB, DS, D)))


def kernel(**inputs):
    import concourse.bacc as bacc
    from concourse.bass_utils import run_bass_kernel_spmd

    nc = bacc.Bacc("TRN2", target_bir_lowering=False, num_devices=1)
    arrays, tensors = {}, {}
    for name in INS:
        a = np.ascontiguousarray(inputs[name])
        arrays[f"in_{name}"] = a
        tensors[name] = nc.dram_tensor(f"in_{name}", a.shape, mybir.dt.from_np(a.dtype), kind="ExternalInput").ap()
    arrays["in_consts"] = CONSTS
    tensors["consts"] = nc.dram_tensor("in_consts", CONSTS.shape, F32, kind="ExternalInput").ap()
    for name, shape in OUTS:
        tensors[name] = nc.dram_tensor(name, shape, F32, kind="ExternalOutput").ap()
    hybrid_layer(nc, tensors)
    r = run_bass_kernel_spmd(nc, [arrays], core_ids=[0])
    return tuple(r.results[0][name] for name, _ in OUTS)
```

```python
from contextlib import ExitStack

import numpy as np
import concourse.bass as bass
from concourse import mybir

F32 = mybir.dt.float32
BF16 = mybir.dt.bfloat16
I32 = mybir.dt.int32
U32 = mybir.dt.uint32
ALU = mybir.AluOpType
ACT = mybir.ActivationFunctionType
AX = mybir.AxisListType

P = 128
D = 1024
KD = D // P
SEQ, DB, DS = 256, 8, 8
TOK = SEQ + DB * DS
TILES = ((0, 128), (128, 128), (256, 64))
H = 8
QKV = 3 * D
FT = QKV // P
TAPS = 4
G = 8
NE, TOPK = 32, 4
SLOTS = 64
MAXB = NE + TOK * TOPK // SLOTS
PLE = 256
EPS = 1e-6
LIMIT, ALPHA = 7.0, 1.702
COL_AB, COL_GATE, COL_U, COL_V, COL_MA, COL_MB = 3072, 3088, 4112, 5136, 6160, 7184
HB = 64
LEVELS = (7, 7, 3)
FAR = 16384.0

CONST = {}


def _constants():
    i = np.arange(P)
    row, col = i[:, None], i[None, :]
    same8 = (row // DS == col // DS)
    parts = [("ident", row == col), ("ones", np.ones((P, P))),
             ("tri", col >= row), ("tri8", (col >= row) & same8), ("same8", same8),
             ("before", row < col)]
    row64, col64 = row % HB, col[:, :HB]
    parts.append(("ident64", row64 == col64))
    for lev in range(6):
        n = 1 << lev
        parts.append((f"level{lev}", (row64 // (2 * n) == col64 // (2 * n)) & ((row64 // n) % 2 == 0) & ((col64 // n) % 2 == 1)))
    parts += [("seq4", row % 32 // DS == i[None, :DB // 2]),
              ("slot", np.broadcast_to(i[None, :] % SLOTS, (P, P))),
              ("block", np.broadcast_to(i[None, :SLOTS], (P, SLOTS))),
              ("expert", np.broadcast_to(i[None, :NE], (P, NE))),
              ("eps", np.full((P, 1), EPS)), ("qscale", np.full((P, 1), -0.5 * np.log(128.0))),
              ("thr", np.broadcast_to(64.0 * np.arange(1, 5)[None, :], (P, 4))),
              ("eid", np.arange(P)[:, None] % NE)]
    at, out = 0, []
    for name, a in parts:
        CONST[name] = (at, a.shape[1])
        at += a.shape[1]
        out.append(np.asarray(a, np.float32))
    return np.ascontiguousarray(np.concatenate(out, axis=1))


CONSTS = _constants()
NCONST = CONSTS.shape[1]


def hybrid_layer(nc, t):
    ctx = ExitStack()
    with ctx:
        sems = {}

        def sem(name):
            if name not in sems:
                sems[name] = ctx.enter_context(nc.semaphore(name))
            return sems[name]

        arena_words = 53000
        arena = ctx.enter_context(nc.sbuf_tensor("arena", [P, arena_words], F32))
        top = [0]

        def region(words):
            at = top[0]
            top[0] += words
            assert top[0] <= arena_words, top[0]
            return at

        def view(at, *dims):
            n = int(np.prod(dims))
            v = arena[:, at:at + n]
            if len(dims) == 1:
                return v
            names = "abcd"[:len(dims)]
            return v.rearrange(f"p ({' '.join(names)}) -> p {' '.join(names)}",
                               **{k: d for k, d in zip(names, dims)})

        UNIT = 4096
        slot_at = [region(UNIT) for _ in range(6)]
        FRONT_SLOTS = 2
        scratch = slot_at[4]
        cst_at = region(NCONST)
        x_at = region(3 * D)
        hT_at = region(KD * TOK)
        qkv_at = region(FT * TOK)
        gate_at = region(KD * TOK)
        u_at = region(KD * TOK)
        v_at = region(3 * D)
        big_at = region(3 * D)
        small_at = region(1100)

        def cst(name, rows=P, cols=None):
            at, n = CONST[name]
            return arena[0:rows, cst_at + at:cst_at + at + (n if cols is None else cols)]

        ident = cst("ident")
        slots = [view(a, KD, 512) for a in slot_at]

        x = view(x_at, 3, D)
        hT = view(hT_at, KD, TOK)
        qkvT = view(qkv_at, FT, TOK)
        gateT = view(gate_at, KD, TOK)
        uT = view(u_at, KD, TOK)
        vtok = view(slot_at[2], 3, D)
        oT = view(qkv_at, H, TOK)
        maT = view(slot_at[2] + 3 * D, H, TOK)
        mbT = view(slot_at[2] + 3 * D + H * TOK, H, TOK)
        rs = view(slot_at[2], 2 * H, TOK)

        ZW = 3 + SEQ + DB * (3 + DS)
        CW = ZW - 3
        zpad = [view(scratch + i * ZW, ZW) for i in range(3)]
        cv = [view(scratch + (3 + i) * ZW, ZW) for i in range(2)]
        sg = [view(scratch + (5 + i) * ZW, ZW) for i in range(2)]
        last_at = scratch + 7 * ZW
        last3 = view(last_at, FT, 27)
        oldT = view(last_at + FT * 27, FT, 24)
        sc_rows = view(v_at, QKV)
        new_rows = view(big_at, QKV)
        sq = [view(last_at + FT * 51 + i * TOK, TOK) for i in range(2)]
        assert last_at + FT * 51 + 2 * TOK <= scratch + 8192

        def heads(at):
            return view(at, H, P)
        DBm, _, mT, X, XT, W, rT, r = [heads(scratch + i * 1024) for i in range(8)]
        half_heads = lambda at: view(at, H, HB)
        Al = [half_heads(scratch), half_heads(scratch + 7 * 1024)]
        ATd = half_heads(scratch + 1024)
        AToff = half_heads(scratch + 1536)
        Xd = half_heads(scratch + 3 * 1024)
        XTd = half_heads(scratch + 3 * 1024 + 512)
        Wd = half_heads(scratch + 5 * 1024)
        qd, kd, qS = [heads(x_at + i * 1024) for i in range(3)]
        GR, S, S0x = [heads(big_at + i * 1024) for i in range(3)]
        S0 = [view(v_at + i * 1024, DB, P) for i in range(3)] + [view(big_at + 2048, DB, P)]
        sgm = view(scratch, KD, TOK)
        wnat8 = view(scratch + 2560, G, 64)
        stmp = view(scratch + 3072, 512)
        stmp2 = view(scratch + 3584, 512)
        squares = view(scratch + 3072, D)
        WT8 = view(scratch + 4096, G, 64)
        WT = view(scratch + 5120, G, P)
        wnat = view(scratch + 6144, G, P)
        bsb = view(scratch + 7168, G, P)
        lng = view(hT_at, D)
        lnb = view(hT_at + D, D)
        moved = view(big_at, 512)[0:64, 0:256]
        mixT = gateT

        sm = [small_at]

        def small(*dims):
            n = int(np.prod(dims))
            v = view(sm[0], *dims) if len(dims) > 1 else arena[:, sm[0]:sm[0] + n]
            sm[0] += n
            assert sm[0] <= small_at + 1100
            return v

        wab = small(KD, 16)
        rows_in = small(P)
        colsT = small(P)
        ssq = small(3)
        eps_col = small(1)
        warm = small(1)
        rstd = small(3)
        ab = small(3, 16)
        gg = small(3, 8)
        beta = small(3, 8)
        alog = small(8)
        dtb = small(8)
        gce = small(3, 16)
        dcol = small(3, 8)
        gend = small(3, 8)
        kdec = small(8)
        tA = small(3, 8)
        tB = small(3, 8)
        msum = small(3)
        mvar = small(3)
        mrs = small(3)
        g_conv = colsT[:, 0:FT * TAPS].rearrange("p (t f) -> p t f", f=FT)
        g1, g2, g3 = (colsT[:, 96 + 8 * i:104 + 8 * i] for i in range(3))
        dng = colsT[:, 120:121]

        mo = [hT_at]
        uslot3 = 5

        def moe(*dims):
            n = int(np.prod(dims))
            if mo[0] < big_at and mo[0] + n > v_at:
                mo[0] = big_at
            v = view(mo[0], *dims) if len(dims) > 1 else arena[:, mo[0]:mo[0] + n]
            mo[0] += n
            assert mo[0] <= small_at
            return v

        h2T = moe(KD, TOK)
        h2 = moe(3, D)
        rw = moe(KD, NE)
        rbias = moe(NE)
        b12 = moe(D + 2 * D)
        b12c = arena[:, v_at:v_at + 3 * D // 2].bitcast(BF16)
        b12s = arena[:, v_at + 3 * D // 2:v_at + 3 * D].bitcast(BF16)
        logit = moe(3, NE)
        top8 = moe(3, 8)
        idx8 = moe(3, 8)
        idxf = moe(3, 8)
        gates = moe(3, 8)
        gsum = moe(3)
        mask = moe(3, NE)
        gmat = moe(3, NE)
        pos = moe(3, NE)
        etmp = moe(3, NE)
        chosen = moe(3 * TOPK * NE)
        chosen_g = moe(3 * TOPK * NE)
        logitT = moe(TOK)
        posT = moe(TOK)
        gmT = moe(TOK)
        cnt = moe(16)
        Eb = moe(SLOTS)
        Eb3 = moe(SLOTS // 2).bitcast(BF16)
        Eb3f = moe(SLOTS)
        posb = moe(3, SLOTS)
        gateb = moe(3, SLOTS)
        tabf = moe(160)
        tab = moe(160).bitcast(I32)
        Psel = moe(3, SLOTS)
        Pg = moe(3, P)
        PgT = moe(3 * P)
        xsel = moe(512)
        xselT = moe(KD, SLOTS)
        Ebc = moe(SLOTS // 2).bitcast(BF16)
        g_sb, u_sb, s_sb, a_sb = moe(512), moe(512), moe(512), moe(512)
        actT = moe(4, P)
        y_sb = moe(512)
        fng = view(slot_at[uslot3], D)
        ptok = view(slot_at[uslot3] + D, 3, PLE)
        pT = moe(2, TOK)
        h3T = h2T
        LAST_BANKS = (6, 0, 2)
        P_BANKS = (5, 3)
        PLE_BANKS = (4, 5, 6, 7, 2)
        H3_BANKS = (0, 1, 3)
        ple_moved = y_sb[0:64]
        assert mo[0] <= small_at, (mo[0], small_at)

        ps = ctx.enter_context(nc.psum_tensor("ps", [P, 8, 512], F32))
        pj = [ps[:, 0, :], ps[:, 1, :]]

        def pair(b, n=P):
            return ps[:, b:b + 2, :].rearrange("p a (h c) -> p (a h) c", c=P)[:, :, 0:n]

        G01, G23, G45 = (lambda n=P: pair(2, n)), (lambda n=P: pair(4, n)), (lambda n=P: pair(6, n))

        def blocks64(bank):
            return ps[:, bank, :].rearrange("p (h c) -> p h c", c=HB)

        def h2T_bank(k):
            return ps[:, 2 + k // 2, SEQ * (k % 2):SEQ * (k % 2) + SEQ]

        def fill_at_level(tt, lev):
            return 2 if (lev == 0) == (tt < 2) else 1

        def masks_before(tt):
            return sum(min(n, 6) for n in LEVELS[:tt])

        w_in = t["w_in"][0].rearrange("(k p) n -> p k n", p=P)
        chunk_src = [w_in[:, :, c * 512:(c + 1) * 512] for c in range(6)]
        for col in (COL_GATE, COL_U, COL_V, COL_MA, COL_MB):
            chunk_src += [w_in[:, :, col + c * 512:col + (c + 1) * 512] for c in range(2)]
        for name in ("w_proj_a", "w_proj_b", "w_out"):
            w = t[name][0].rearrange("(k p) n -> p k n", p=P)
            chunk_src += [w[:, :, c * 512:(c + 1) * 512] for c in range(2)]
        NCH = len(chunk_src)
        C_GATE, C_U, C_V, C_MA, C_MB, C_PA, C_PB, C_WO = 6, 8, 10, 12, 14, 16, 18, 20
        landed = [sem(f"weights_landed{s}") for s in range(6)]
        used = [sem(f"weights_used{s}") for s in range(6)]

        N_QKV, N_AB, N_GATE, N_U, N_V, N_MA, N_MB, N_YA, N_YB, N_WO, N_END = (
            0, 24, 25, 33, 41, 47, 55, 63, 71, 79, 85)
        free_at = [4 * (c + 1) for c in range(6)]
        for n0, per in ((N_GATE, 4), (N_U, 4), (N_V, 3), (N_MA, 4), (N_MB, 4), (N_YA, 4), (N_YB, 4), (N_WO, 3)):
            free_at += [n0 + per, n0 + 2 * per]
        proj_done = sem("projection_done")
        bank_free = [sem("projection_bank0_free"), sem("projection_bank1_free")]

        def bank_wait(pe, n):
            if n >= 2:
                pe.wait_ge(bank_free[n % 2], n // 2)

        def evacuated(eng, n):
            eng.wait_ge(bank_free[n % 2], n // 2 + 1)

        def chunk_wait(eng, c):
            eng.wait_ge(landed[c % FRONT_SLOTS], 16 * (c // FRONT_SLOTS + 1))
        before = [len([c for c in range(NCH) if c % FRONT_SLOTS == s]) for s in range(6)]
        uslot = [(u + 2) % 6 for u in range(6)]

        class Chain:

            def __init__(self, eng, s):
                self.eng, self.s, self.n = eng, s, 0

            def __call__(self, ins):
                self.n += 1
                ins.then_inc(self.s, 1)

            def wait(self):
                self.eng.wait_ge(self.s, self.n)

            def link(self, ins):
                self(ins)
                self.wait()

        block = ctx.enter_context(nc.Block())

        @block.sync
        def _(sp):
            sp.dma_start(x[:, 0:2, :], t["x_prompt"][0].rearrange("(a p) d -> p a d", p=P)).then_inc(sem("x_in"), 16)
            sp.dma_start(x[0:64, 2, :], t["x_sample"].rearrange("b s d -> (b s) d")).then_inc(sem("x_in"), 16)
            sp.dma_start(arena[:, cst_at:cst_at + NCONST], t["consts"]).then_inc(sem("consts_in"), 16)
            sp.dma_start(rows_in[0:96, :], t["conv_w"][0].rearrange("t (f p) -> (t f) p", p=P)).then_inc(sem("rows_loaded"), 16)
            for i, name in enumerate(("norm1_g", "norm2_g", "norm3_g")):
                sp.dma_start(rows_in[96 + 8 * i:104 + 8 * i, :],
                             t[name][0].rearrange("(k p) -> k p", p=P)).then_inc(sem("rows_loaded"), 16)
            sp.dma_start(rows_in[120:121, :], t["dn_norm_g"]).then_inc(sem("rows_loaded"), 16)
            sp.dma_start(sc_rows[0:24, :], t["state_conv"][0].rearrange("b r n -> (b r) n")).then_inc(sem("rows_loaded"), 16)
            for c in range(FRONT_SLOTS):
                sp.dma_start(slots[c], chunk_src[c]).then_inc(landed[c], 16)
                if c == 0:
                    sp.dma_start(wab, w_in[:, :, COL_AB:COL_AB + 16]).then_inc(sem("ab_in"), 16)
                    sp.dma_start(alog, t["a_log"].broadcast_to([P, H])).then_inc(sem("ab_in"), 16)
                    sp.dma_start(dtb, t["dt_bias"].broadcast_to([P, H])).then_inc(sem("ab_in"), 16)

            def chunk(c):
                sp.wait_ge(proj_done, free_at[c - FRONT_SLOTS])
                sp.dma_start(slots[c % FRONT_SLOTS], chunk_src[c]).then_inc(landed[c % FRONT_SLOTS], 16)

            for c in range(FRONT_SLOTS, C_PA + 1):
                chunk(c)
            sp.wait_ge(sem("S_ready"), 2)
            sp.dma_start(t["out_sd_p"][0, 0].rearrange("h k v -> k h v"), S[:, :, :]).then_inc(sem("stored"), 16)
            for h in range(H):
                sp.wait_ge(sem("S0_new"), h + 1)
                sp.dma_start(t["out_sd_s"][0, :, h].rearrange("b k v -> k b v"), S0[h % 4]).then_inc(sem(f"S0_stored{h % 4}"), 16)
                if h != 3:
                    continue
                chunk(C_PA + 1)
                sp.wait_ge(sem("o_normed"), 3)
                sp.dma_start(wnat, t["gm_ws"][0].rearrange("g t s -> t g s")).then_inc(sem("mlp_in"), 16)
                sp.wait_ge(sem("wnat8_zero"), 1)
                for b in range(DB):
                    sp.dma_start(wnat8[DS * b:DS * b + DS, :, DS * b:DS * b + DS],
                                 t["gm_ws"][0, :, 0:DS, 0:DS].rearrange("g t s -> t g s")).then_inc(sem("mlp_in"), 16)
                sp.dma_start(lng, t["gm_ln_g"].broadcast_to([P, D])).then_inc(sem("mlp_in"), 16)
                sp.dma_start(lnb, t["gm_ln_b"].broadcast_to([P, D])).then_inc(sem("mlp_in"), 16)
                sp.dma_start(bsb.rearrange("p g t -> p (g t)"),
                             t["gm_bs"].rearrange("a g t -> a (g t)").broadcast_to([P, G * P])).then_inc(sem("mlp_in"), 16)
            sp.wait_ge(sem("S0_product"), 2 * H)
            sp.wait_ge(sem("stored"), 16)
            sp.dma_start(rw, t["router_w"][0].rearrange("(k p) e -> p k e", p=P)).then_inc(sem("router_in"), 16)
            sp.dma_start(rbias, t["router_b"].broadcast_to([P, NE])).then_inc(sem("router_in"), 16)
            sp.dma_start(b12[0:NE, 0:2 * D], t["moe_b1"][0]).then_inc(sem("router_in"), 16)
            sp.dma_start(b12[0:NE, 2 * D:3 * D], t["moe_b2"][0]).then_inc(sem("router_in"), 16)
            sp.dma_start(x[:, 0:2, :], t["x_prompt"][0].rearrange("(a p) d -> p a d", p=P)).then_inc(sem("x_in"), 16)
            sp.dma_start(x[0:64, 2, :], t["x_sample"].rearrange("b s d -> (b s) d")).then_inc(sem("x_in"), 16)
            for c in range(C_PA + 2, NCH):
                chunk(c)
            sp.wait_ge(sem("vnorm_ready"), 3)
            sp.dma_start(t["out_gv"][0].rearrange("b s d -> (b s) d"), vtok[0:64, 2, :]).then_inc(sem("stored"), 16)

            def unit_src(e, u):
                if u < 4:
                    return t["moe_w1"][0, e, u * 256:(u + 1) * 256, :].rearrange("(k p) n -> p k n", p=P)
                return t["moe_w2"][0, e, (u - 4) * 512:(u - 3) * 512, :].rearrange("(k p) n -> p k n", p=P)

            def unit_dst(u):
                return slots[uslot[u]].rearrange("p k n -> p (k n)").rearrange("p (k n) -> p k n", k=2 if u < 4 else 4)

            for u in range(6):
                s = uslot[u]
                if s < FRONT_SLOTS:
                    sp.wait_ge(proj_done, free_at[NCH - FRONT_SLOTS + s])
                elif u == 0:
                    sp.wait_ge(sem("merged"), KD)
                    sp.wait_ge(sem("stored"), 32)
                sp.dma_start(unit_dst(u), t["moe_w1"][0, 0, u * 256:(u + 1) * 256, :].rearrange("(k p) n -> p k n", p=P)
                             if u < 4 else unit_src(0, u)).then_inc(landed[s], 16)
            sp.wait_ge(sem("tables_ready"), 1)
            w1 = t["moe_w1"][0].rearrange("e (u k p) n -> (e u) p k n", u=4, p=P)
            w2 = t["moe_w2"][0].rearrange("e (u k p) n -> (e u) p k n", u=2, p=P)
            with sp.Fori(0, NE - 1) as e:
                through = sp.value_load(tab[0:1, bass.ds(96 + e, 1)], min_val=1, max_val=MAXB)
                for u in range(6):
                    s = uslot[u]
                    sp.wait_ge(used[s], through)
                    src = w1[bass.ds(e * 4 + 4 + u, 1)] if u < 4 else w2[bass.ds(e * 2 + 2 + u - 4, 1)]
                    sp.dma_start(unit_dst(u), src.rearrange("a p k n -> p (a k) n")).then_inc(landed[s], 16)
            wg = t["ple_gate_w"][0].rearrange("(k p) n -> p k n", p=P)
            nb = sp.value_load(tab[0:1, 96 + NE - 1:96 + NE], min_val=1, max_val=MAXB)
            for c in range(2):
                sp.wait_ge(used[uslot[c]], nb)
                sp.dma_start(slots[uslot[c]], wg[:, :, c * 512:(c + 1) * 512]).then_inc(landed[uslot[c]], 16)
            sp.wait_ge(used[uslot[2]], nb)
            sp.dma_start(slots[uslot[2]].rearrange("p k n -> p (k n)")[:, 0:2048].rearrange("p (k n) -> p k n", k=2),
                         t["ple_w"][0].rearrange("(k p) n -> p k n", p=P)).then_inc(landed[uslot[2]], 16)
            sp.wait_ge(used[uslot[3]], nb)
            sp.dma_start(ptok[:, 0:2, :], t["p_prompt"][0, 0].rearrange("(a p) d -> p a d", p=P)).then_inc(sem("ple_in"), 16)
            sp.dma_start(ptok[0:64, 2, :], t["p_sample"][0].rearrange("b s d -> (b s) d")).then_inc(sem("ple_in"), 16)
            sp.dma_start(fng, t["final_norm_g"].rearrange("(a d) -> a d", a=1).broadcast_to([P, D])).then_inc(sem("ple_in"), 16)
            for tt, (t0, tn) in enumerate(TILES):
                sp.wait_ge(sem("y_ready"), tt + 1)
                dst = t["out_yp"][0, t0:t0 + tn, :] if tt < 2 else t["out_ys"].rearrange("b s d -> (b s) d")
                sp.dma_start(dst, x[0:tn, tt, :]).then_inc(sem("stored"), 16)
            sp.wait_ge(sem("stored"), 16 * 5)
            sp.wait_ge(sem("newrows_stored"), 32)

        @block.gpsimd
        def _(pool):
            for i in range(3):
                pool.memset(zpad[i], 0.0).then_inc(sem("pool_zeroed"), 1)
            pool.wait_ge(sem("pool_zeroed"), 3)

            def fill_old(n):
                if n >= 3:
                    pool.wait_ge(sem("conv_done"), n - 2)
                    pool.wait_ge(sem("last3_done"), 2 * (n - 2))
                pool.wait_ge(sem("old_turned"), n // 4 + 1)
                zs = zpad[n % 3][:, 3 + SEQ:].rearrange("p (b j) -> p b j", b=DB)
                pool.tensor_copy(zs[:, :, 0:3], oldT[:, n, :].rearrange("p (b j) -> p b j", b=DB)).then_inc(sem("old_filled"), 1)

            def keep_last(n):
                evacuated(pool, n)
                zs = zpad[n % 3][:, 3 + SEQ:].rearrange("p (b j) -> p b j", b=DB)
                pool.tensor_copy(last3[:, n, 0:3], zpad[n % 3][:, SEQ:SEQ + 3]).then_inc(sem("last3_done"), 1)
                pool.tensor_copy(last3[:, n, 3:27].rearrange("p (b j) -> p b j", b=DB), zs[:, :, DS:DS + 3]).then_inc(sem("last3_done"), 1)

            fill_old(0)
            for n in range(FT):
                if n + 1 < FT:
                    fill_old(n + 1)
                keep_last(n)
                m = n - 2
                if 0 <= m < 2 * H:
                    pool.wait_ge(sem("silu_done"), 2 * (m + 1))
                    if m >= 2:
                        pool.wait_ge(sem("sumsq_done"), m - 1)
                    pool.tensor_tensor(sq[m % 2], qkvT[:, m, :], qkvT[:, m, :], ALU.mult).then_inc(sem("sq_ready"), 1)

            def load_state(i):
                pool.dma_start(S0[i % 4], t["state_delta"][0, :, i % H].rearrange("b k v -> k b v")).then_inc(sem(f"S0_in{i % 4}"), 16)

            pool.wait_ge(sem("newrows_ready"), 6)
            pool.dma_start(t["out_sc_p"][0, 0], new_rows[0:3, :]).then_inc(sem("newrows_stored"), 16)
            pool.dma_start(t["out_sc_s"][0].rearrange("b r n -> (b r) n"), new_rows[3:27, :]).then_inc(sem("newrows_stored"), 16)
            pool.wait_ge(sem("newrows_stored"), 32)
            pool.wait_ge(sem("old_turned"), 6)
            pool.memset(XT[64:128, :, 0:HB], 0.0).then_inc(sem("pool_zeroed"), 1)
            pool.wait_ge(sem("pool_zeroed"), 4)
            for i in range(4):
                load_state(i)
            for tt, (t0, tn) in enumerate(TILES):
                pool.wait_ge(sem("GR_ready"), tt + 1)
                pool.wait_ge(sem("qk_normed"), 2)
                if tt == 2:
                    pool.wait_ge(sem("kS_done"), 1)
                pool.tensor_tensor(qd[:, :, 0:tn], qkvT[:, 0:H, t0:t0 + tn], GR[:, :, 0:tn], ALU.mult).then_inc(sem("qd_ready"), 1)
                pool.wait_ge(sem("AT_ready"), tt + 1)
                pool.wait_ge(sem("mT_ready"), tt + 1)
                for lev in range(min(LEVELS[tt], 6)):
                    done = sum(LEVELS[:tt]) + lev
                    if lev == 0 and tt:
                        pool.wait_ge(sem("u_done"), tt)
                    if lev >= 2:
                        pool.wait_ge(sem("W_done"), done - 1)
                    if lev == 2:
                        pool.wait_ge(sem("XT_ready"), done - 1)
                    pool.tensor_tensor(Al[lev % 2][0:tn], ATd[0:tn],
                                       cst(f"level{lev}", tn).rearrange("p (a c) -> p a c", a=1).broadcast_to([tn, H, HB]),
                                       ALU.mult).then_inc(sem("Al_ready"), 1)
            for i in range(4, 12):
                pool.wait_ge(sem("kS_head"), i - 3)
                load_state(i)
            for h in range(H):
                if h >= 4:
                    pool.wait_ge(sem(f"S0_stored{h % 4}"), 16)
                    load_state(8 + h)
                if h % 2:
                    continue
                pool.wait_ge(sem("u_ready"), 3)
                if h >= 2:
                    pool.wait_ge(sem("S0_product"), 2 * (h - 1))
                pool.tensor_tensor(X[0:64, 0:4], W[0:64, h, :].rearrange("p (a c) -> p a c", a=1).broadcast_to([64, 4, P]),
                                   cst("seq4", 64).rearrange("p (a c) -> p a c", c=1).broadcast_to([64, 4, P]),
                                   ALU.mult).then_inc(sem("uexp_ready"), 1)
                if h == 0:
                    pool.wait_ge(sem("o_normed"), 3)
                    pool.memset(wnat8[0:64], 0.0).then_inc(sem("wnat8_zero"), 1)
            pool.wait_ge(sem("router_in"), 16 * 4)
            for i in range(3):
                pool.wait_ge(sem(f"S0_stored{i}"), 32)
            part0, part1 = b12s[0:NE, :], b12c[0:NE, :]
            link = lambda ins, n: (ins.then_inc(sem("bias_chain"), 1), pool.wait_ge(sem("bias_chain"), n))
            link(pool.tensor_copy(part0, b12[0:NE, :]), 1)
            link(pool.tensor_tensor(b12[0:NE, :], b12[0:NE, :], part0, ALU.subtract), 2)
            link(pool.tensor_copy(part1, b12[0:NE, :]), 3)
            pool.dma_start(b12s[32:64, :], part1).then_inc(sem("bias_moved"), 16)
            link(pool.tensor_tensor(b12[0:NE, :], b12[0:NE, :], part1, ALU.subtract), 4)
            pool.wait_ge(sem("bias_moved"), 16)
            link(pool.tensor_copy(part1, b12[0:NE, :]), 5)
            pool.dma_start(b12s[64:96, :], part1).then_inc(sem("bias_moved"), 16)

        @block.tensor
        def _(pe):
            def mm(out, lhsT, rhs, first, last):
                return pe.matmul(out, lhsT, rhs, start=first, stop=last, skip_group_check=True)

            pe.wait_ge(sem("consts_in"), 16)
            pe.wait_ge(sem("rows_loaded"), 16 * 6)
            pe.transpose(pj[1][:, 0:121], rows_in[0:121, :], ident[0:121, 0:121]).then_inc(sem("rows_turned"), 1)
            for g in range(6):
                for i in range(4):
                    f = 4 * g + i
                    m = pe.transpose(ps[:, 2 + g, 24 * i:24 * i + 24], sc_rows[0:24, f * P:(f + 1) * P], ident[0:24, 0:24])
                m.then_inc(sem("old_done"), 1)
            pe.wait_ge(sem("xn_ready"), 3)
            for k in range(KD):
                if k == 1:
                    pe.wait_ge(sem("cols_ready"), 1)
                elif k >= 2:
                    pe.wait_ge(sem(("hT_ready", "hT_odd_ready")[k % 2]), k // 2)
                for tt, (t0, tn) in enumerate(TILES):
                    m = pe.transpose(pj[k % 2][:, t0:t0 + tn], x[0:tn, tt, k * P:(k + 1) * P], ident[0:tn, 0:tn])
                m.then_inc(sem("hT_done"), 1)

            def features(n, c, m, rhs, ks=range(KD)):
                chunk_wait(pe, c)
                bank_wait(pe, n)
                for k in ks:
                    last = mm(pj[n % 2][:, 0:TOK], slots[c % FRONT_SLOTS][:, k, m * P:(m + 1) * P], rhs[:, k, :], k == 0, k == KD - 1)
                if k == KD - 1:
                    last.then_inc(proj_done, 1)

            def rows(n, c, tt, lhs, ks=range(KD)):
                t0, tn = TILES[tt]
                chunk_wait(pe, c)
                bank_wait(pe, n)
                if tt == 2:
                    for k in ks:
                        for g in range(2):
                            last = mm(pj[n % 2][64 * g:64 * g + 64, 0:256], lhs[:, k, t0:t0 + tn],
                                      slots[c % FRONT_SLOTS][:, k, 256 * g:256 * g + 256], k == 0, k == KD - 1)
                else:
                    for k in ks:
                        last = mm(pj[n % 2][0:tn, :], lhs[:, k, t0:t0 + tn], slots[c % FRONT_SLOTS][:, k, :], k == 0, k == KD - 1)
                if k == KD - 1:
                    last.then_inc(proj_done, 1)

            pe.wait_ge(sem("hT_ready"), KD // 2)
            pe.wait_ge(sem("hT_odd_ready"), KD // 2)
            for n in range(FT):
                features(n, n // 4, n % 4, hT)
                m = n - 3
                if 0 <= m < 2 * H:
                    pe.wait_ge(sem("sq_ready"), m + 1)
                    if m >= 6:
                        pe.wait_ge(sem("ln_done"), m - 5)
                    else:
                        pe.wait_ge(sem("old_turned"), 6)
                    mm(ps[:, 2 + m % 6, 0:TOK], cst("ones"), sq[m % 2], True, True).then_inc(sem("sumsq_done"), 1)
            pe.wait_ge(sem("ab_in"), 48)
            bank_wait(pe, N_AB)
            for tt, (t0, tn) in enumerate(TILES):
                for k in range(KD):
                    last = mm(pj[0][0:tn, 16 * tt:16 * tt + 16], hT[:, k, t0:t0 + tn], wab[:, k, :], k == 0, k == KD - 1)
            last.then_inc(proj_done, 1)
            pe.wait_ge(sem("last3_done"), 2 * FT)
            pe.wait_ge(sem("ln_done"), 2 * H)
            for g in range(6):
                for i in range(4):
                    m = pe.transpose(ps[0:27, 2 + g, P * i:P * i + P], last3[:, 4 * g + i, :], ident)
                m.then_inc(sem("newrows_done"), 1)
            filled = [2 * N_GATE]

            def fill(halves=2):
                for _ in range(halves):
                    n, part = divmod(filled[0], 2)
                    filled[0] += 1
                    ks = range(KD // 2 * part, KD // 2 * (part + 1))
                    if n < N_V:
                        features(n, C_GATE + (n - N_GATE) // 4, (n - N_GATE) % 4, hT, ks)
                    elif n < N_MA:
                        rows(n, C_V + (n - N_V) // 3, (n - N_V) % 3, hT, ks)
                    else:
                        features(n, C_MA + (n - N_MA) // 4, (n - N_MA) % 4, hT, ks)

            fill(4)
            pe.wait_ge(sem("newrows_ready"), 6)
            pe.wait_ge(sem("g_ready"), 3)
            for tt, (t0, tn) in enumerate(TILES):
                mm(ps[0:tn, 7, 16 * tt:16 * tt + 8], cst("tri8" if tt == 2 else "tri", tn, tn), gg[0:tn, tt, :], True, True)
                m = mm(ps[0:tn, 7, 16 * tt + 8:16 * tt + 16], cst("same8" if tt == 2 else "ones", tn, tn), gg[0:tn, tt, :], True, True)
            m.then_inc(sem("cum_done"), 1)
            fill()
            pe.wait_ge(sem("qk_normed"), 2)
            pe.wait_ge(sem("silu_done"), 2 * FT)

            for tt, (t0, tn) in enumerate(TILES):
                L0 = sum(LEVELS[:tt])
                fill(1)
                pe.wait_ge(sem("RH_ready"), tt + 1)
                if tt == 0:
                    pe.wait_ge(sem("gce_ready"), 1)
                else:
                    pe.wait_ge(sem("S_ready"), tt)
                for a in range(2):
                    m = mm(G45(tn)[:, 4 * a:4 * a + 4, :], cst("ones", tn), X[0:tn, 4 * a:4 * a + 4, 0:tn], True, True)
                m.then_inc(sem("gcrow_done"), 1)
                if tt:
                    pe.wait_ge(sem("ln_done"), 2 * H + tt)
                    pe.wait_ge(sem("o_ready"), tt)
                for h in range(H):
                    mm(G01(tn)[0:tn, h, :], qkvT[:, H + h, t0:t0 + tn], qkvT[:, H + h, t0:t0 + tn], True, True)
                    m = mm(G23(tn)[0:tn, h, :], qkvT[:, H + h, t0:t0 + tn], qkvT[:, h, t0:t0 + tn], True, True)
                m.then_inc(sem("kk_done"), 1)
                fill(3 if tt < 2 else 2)
                pe.wait_ge(sem("AT_ready"), tt + 1)
                for h in range(H):
                    m = pe.transpose(G01()[0:tn, h, :], qkvT[:, H + h, t0:t0 + tn], ident)
                m.then_inc(sem("kt_done"), 1)
                fill(1 if tt < 2 else 2)
                for lev in range(LEVELS[tt]):
                    i = L0 + lev
                    joins = lev == 6
                    if not joins:
                        pe.wait_ge(sem("Al_ready"), masks_before(tt) + lev + 1)
                    if lev == 0:
                        pe.wait_ge(sem("dd_ready"), tt + 1)
                        pe.wait_ge(sem("GR_ready"), tt + 1)
                    else:
                        pe.wait_ge(sem("X_ready"), i - tt)
                    for h in range(H):
                        if joins:
                            m = mm(blocks64(6)[64:128, h, :], AToff[0:64, h, :], Xd[0:64, h, :], True, True)
                        else:
                            for b in range(0, tn, HB):
                                blk = slice(b, b + HB)
                                rhs = cst("ident64")[blk, :] if lev == 0 else Xd[blk, h, :]
                                m = mm(blocks64(6)[blk, h, :], Al[lev % 2][blk, h, :], rhs, True, True)
                    m.then_inc(sem("W_done"), 1)
                    fill(fill_at_level(tt, lev))
                    if lev:
                        pe.wait_ge(sem("W_ready"), i - tt)
                        if lev == 1:
                            pe.wait_ge(sem("kd_ready"), tt + 1)
                            pe.wait_ge(sem("mT_ready"), tt + 1)
                        pe.wait_ge(sem("XT_ready"), i)
                        if lev < LEVELS[tt] - 1:
                            for h in range(H):
                                for b in range(0, tn, HB):
                                    blk = slice(b, b + HB)
                                    m = mm(blocks64(2)[blk, h, :], XTd[blk, h, :], Wd[blk, h, :], True, True)
                            m.then_inc(sem("D_done"), 1)
                        for h in range(H):
                            if joins:
                                m = mm(blocks64(4)[0:64, h, :], Wd[64:128, h, :], XTd[64:128, h, :], True, True)
                                continue
                            for b in range(0, tn, HB):
                                blk = slice(b, b + HB)
                                m = mm(blocks64(4)[blk, h, :], Wd[blk, h, :], XTd[blk, h, :], True, True)
                        m.then_inc(sem("DT_done"), 1)
                fill(1)
                if tt:
                    pe.wait_ge(sem("XT_ready"), L0 + LEVELS[tt])
                    pe.wait_ge(sem("qd_ready"), tt + 1)
                if tt == 1:
                    for h in range(H):
                        mm(G01(tn)[:, h, :], S[:, h, :], qkvT[:, H + h, t0:t0 + tn], True, True)
                        m = mm(G23(tn)[:, h, :], S[:, h, :], qd[:, h, 0:tn], True, True)
                    m.then_inc(sem("kS_done"), 1)
                    fill()
                if tt < 2:
                    pe.wait_ge(sem("rT_ready"), tt + 1)
                for h in range(H):
                    m = pe.transpose(G45()[0:tn, h, :], rT[:, h, 0:tn] if tt < 2 else qkvT[:, 2 * H + h, t0:t0 + tn], ident)
                m.then_inc(sem("r_done"), 1)
                if tt < 2:
                    fill()
                if tt == 2:
                    for h in range(H):
                        pe.wait_ge(sem(f"S0_in{h % 4}"), 16 * (h // 4 + 1))
                        if h >= 4:
                            pe.wait_ge(sem("kS_read"), h - 3)
                        for a in range(2):
                            states, r0 = S0[h % 4][:, 4 * a:4 * a + 4, :], 32 * a
                            mm(ps[r0:r0 + 32, 2 + h % 4, :], qkvT[:, H + h, t0 + r0:t0 + r0 + 32], states, True, True)
                            m = mm(ps[64 + r0:96 + r0, 2 + h % 4, :], qd[:, h, r0:r0 + 32], states, True, True)
                        m.then_inc(sem("kS_head"), 1)
                        if h % 4 == 3:
                            fill()
                pe.wait_ge(sem("r_ready"), tt + 1 if tt < 2 else 2 + H)
                pe.wait_ge(sem("XT_ready"), L0 + LEVELS[tt])
                for h in range(H):
                    m = mm(G01()[0:tn, h, :], XT[0:tn, h, :] if tt < 2 else XTd[0:tn, h, :], r[0:tn, h, :], True, True)
                m.then_inc(sem("u_done"), 1)
                fill()
                pe.wait_ge(sem("u_ready"), tt + 1)
                if tt == 1:
                    pe.wait_ge(sem("qS_ready"), 1)
                for h in range(H):
                    m = mm(G23(tn)[:, h, :], W[0:tn, h, :], mT[0:tn, h, 0:tn], True, tt < 2)
                    if tt == 2:
                        m = mm(G23(tn)[:, h, :], r[:, h, :], ident[:, 64:128], False, True)
                m.then_inc(sem("o_done"), 1)
                if tt < 2:
                    for h in range(H):
                        m = mm(G45()[:, h, :], kd[0:tn, h, :], W[0:tn, h, :], True, True)
                    m.then_inc(sem("S_done"), 1)
                fill()
                pe.wait_ge(sem("osq_ready"), tt + 1)
                for a in range(2):
                    m = mm(G01(tn)[:, 4 * a:4 * a + 4, :], cst("ones"), qS[:, 4 * a:4 * a + 4, 0:tn], True, True)
                m.then_inc(sem("sumsq_done"), 1)
                fill()
            for h in range(H):
                pe.wait_ge(sem(("uexp_ready", "uexp_odd_ready")[h % 2]), h // 2 + 1)
                if h >= 2:
                    pe.wait_ge(sem("S0_new"), h - 1)
                elif h == 1:
                    pe.wait_ge(sem("o_ready"), 3)
                for a in range(2):
                    rows32 = slice(32 * a, 32 * a + 32)
                    mm(ps[:, [6, 4][h % 2] + a, :], kd[rows32, h, :], [X, XT][h % 2][rows32, 0:4, :], True, True).then_inc(sem("S0_product"), 1)
                if h == 1:
                    fill()
                elif h == 3:
                    fill(1)
                    assert filled[0] == 2 * N_YA
                elif h in (5, 7):
                    pe.wait_ge(sem("gated_ready"), 1)
                    for i in (h - 5, h - 4):
                        features(N_YA + i, C_PA, i, oT)

            features(N_YA + 4, C_PA + 1, 0, oT)
            pe.wait_ge(sem("mlp_in"), 16 * 12)
            pe.wait_ge(sem("S0_new"), H)
            for g in range(G):
                pe.transpose(G01()[:, g, :], wnat[:, g, :], ident)
            for g in range(G):
                m = pe.transpose(G23(64)[0:64, g, :], wnat8[0:64, g, :], ident[0:64, 0:64])
            m.then_inc(sem("wT_done"), 1)
            features(N_YA + 5, C_PA + 1, 1, oT)
            pe.wait_ge(sem("vnorm_ready"), 3)
            pe.wait_ge(sem("WT_ready"), 2)
            for tt, (t0, tn) in enumerate(TILES):
                for a in range(2):
                    for g in range(4 * a, 4 * a + 4):
                        wt = WT[:, g, :] if tt < 2 else WT8[0:64, g, :]
                        m = mm(ps[:, 2 + 2 * tt + a, P * (g % 4):P * (g % 4) + tn], vtok[0:tn, tt, g * P:(g + 1) * P], wt, True, True)
                    m.then_inc(sem("mix_done"), 1)
            for i in range(6, 8):
                features(N_YA + i, C_PA + 1, i - 4, oT)
            pe.wait_ge(sem("us_ready"), 6)
            for i in range(8):
                features(N_YB + i, C_PB + i // 4, i % 4, uT)
            pe.wait_ge(sem("merged"), KD)
            for half in range(2):
                for tt in range(3):
                    rows(N_WO + 3 * half + tt, C_WO + half, tt, mixT)

            def select(value, tiles=(0, 1, 2)):
                pe.wait_ge(sem("psel_ready"), value)
                for tt in tiles:
                    tn = TILES[tt][1]
                    for g in range(2):
                        m = mm(ps[64 * g:64 * g + 64, 3, :], Psel[0:tn, tt, :], h2[0:tn, tt, 512 * g:512 * g + 512], tt == 0, tt == 2)
                if tt == 2:
                    m.then_inc(sem("sel_done"), 1)

            pe.wait_ge(sem("xn_ready"), 5)
            pe.wait_ge(sem("router_in"), 16 * 4)
            for k in range(KD):
                for tt, (t0, tn) in enumerate(TILES[:2]):
                    m = pe.transpose(h2T_bank(k)[:, t0:t0 + tn], h2[0:tn, tt, k * P:(k + 1) * P], ident)
                m.then_inc(sem("hT_done"), 1)
            for k in range(KD):
                pe.wait_ge(sem(("hT_ready", "hT_odd_ready")[k // 2 % 2]), KD // 2 + k // 4 * 2 + k % 2 + 1)
                mm(ps[0:NE, 7, 0:SEQ], rw[:, k, :], h2T[:, k, 0:SEQ], k == 0, k == KD - 1)
            pe.wait_ge(sem("xn_ready"), 6)
            for k in range(KD):
                m = pe.transpose(ps[:, 6, 64 * k:64 * k + 64], h2[0:64, 2, k * P:(k + 1) * P], ident[0:64, 0:64])
            m.then_inc(sem("hT_done"), 1)
            pe.wait_ge(sem("hT_odd_ready"), KD + 1)
            for k in range(KD):
                m = mm(ps[0:NE, 7, SEQ:TOK], rw[:, k, :], h2T[:, k, SEQ:TOK], k == 0, k == KD - 1)
            m.then_inc(sem("logits_done"), 1)
            pe.wait_ge(sem("logitT_ready"), 1)
            for tt, (t0, tn) in enumerate(TILES):
                m = pe.transpose(ps[0:tn, 6, NE * tt:NE * tt + NE], logitT[0:NE, t0:t0 + tn], ident[0:NE, 0:NE])
            m.then_inc(sem("logits_done"), 1)
            pe.wait_ge(sem("mask_ready"), 1)
            for tt, (t0, tn) in enumerate(TILES):
                for s in range(tt + 1):
                    lhs = cst("before", tn, tn) if s == tt else cst("ones", P, tn)
                    m = mm(ps[0:tn, 3, NE * tt:NE * tt + NE], lhs, mask[0:TILES[s][1], s, :], s == 0, s == tt)
            for tt, (t0, tn) in enumerate(TILES):
                m = mm(ps[0:NE, 4, 0:1], mask[0:tn, tt, :], cst("ones", tn, 1), tt == 0, tt == 2)
            m.then_inc(sem("rank_done"), 1)
            pe.wait_ge(sem("blocks_ready"), 1)
            mm(ps[0:NE, 4, 8:9], cst("tri", NE, NE), cnt[0:NE, 4:5], True, True).then_inc(sem("through_done"), 1)
            pe.wait_ge(sem("rank_ready"), 3)
            for tt, (t0, tn) in enumerate(TILES):
                pe.transpose(ps[0:NE, 5, t0:t0 + tn], pos[0:tn, tt, :], ident[0:tn, 0:tn])
                m = pe.transpose(ps[0:NE, 6, t0:t0 + tn], gmat[0:tn, tt, :], ident[0:tn, 0:tn])
            m.then_inc(sem("rankT_done"), 1)
            select(1, (0,))
            pe.wait_ge(sem("E_ready"), 1)
            pe.wait_ge(sem("rankT_ready"), 2)
            for tt, (t0, tn) in enumerate(TILES):
                mm(ps[0:tn, 7, SLOTS * tt:SLOTS * tt + SLOTS], posT[0:NE, t0:t0 + tn], Eb[0:NE, :], True, True)
                mm(ps[0:tn, 7, 256 + SLOTS * tt:256 + SLOTS * tt + SLOTS], gmT[0:NE, t0:t0 + tn], Eb[0:NE, :], True, True)
            mm(ps[0:1, 4, 128:192], cst("eid", NE), Eb[0:NE, :], True, True)
            mm(ps[0:1, 4, 192:224], cnt[0:NE, 5:6], ident[0:NE, 0:NE], True, True).then_inc(sem("perblock_done"), 1)
            select(1, (1, 2))
            def turn_rows(value):
                pe.wait_ge(sem("xsel_ready"), value)
                for j in range(4):
                    m = pe.transpose(ps[:, 5, P * j:P * j + P], xsel[:, P * j:P * j + P], ident)
                m.then_inc(sem("xT_done"), 1)

            def combine(tt, y_value, free_value):
                t0, tn = TILES[tt]
                if tt == 0:
                    pe.wait_ge(sem("ysb_ready"), y_value)
                    pe.wait_ge(sem("pgT_ready"), y_value)
                pe.wait_ge(sem("comb_free"), free_value)
                for g in range(2):
                    m = mm(ps[:, 6 + g, :], PgT[64 * g:64 * g + 64, t0:t0 + P], y_sb[64 * g:64 * g + 64, :], True, True)
                m.then_inc(sem("comb_done"), 1)

            turn_rows(1)
            pe.wait_ge(sem("tables_ready"), 1)
            nb = pe.value_load(tab[0:1, 96 + NE - 1:96 + NE], min_val=1, max_val=MAXB)
            pe.nop().then_inc(sem("pgT_done"), 1)
            pe.wait_ge(sem("bias_moved"), 32)
            pe.wait_ge(sem("bias_chain"), 5)
            with pe.Fori(0, nb) as b:
                e = pe.value_load(tab[0:1, bass.ds(b, 1)], min_val=0, max_val=NE - 1)
                hid_free = sem("hid_free")
                pe.wait_ge(hid_free, b + 1)
                pe.wait_ge(sem("xselT_ready"), b + 1)
                for u in range(4):
                    s = uslot[u]
                    w = slots[s].rearrange("p k n -> p (k n)").rearrange("p (k n) -> p k n", k=2)
                    pe.wait_ge(landed[s], e * 16 + 16 * (before[s] + 1))
                    for kk in range(2):
                        k = 2 * u + kk
                        for part in range(2):
                            for g in range(2):
                                c0 = 1024 * part + 512 * g
                                m = mm(ps[64 * g:64 * g + 64, part, :], xselT[:, k, :], w[:, kk, c0:c0 + 512], k == 0, False)
                    m.then_inc(used[s], 1)
                    if u < 3:
                        combine(u, b + 1, b * 3 + u + 1)
                pe.wait_ge(sem("ebc_ready"), b + 1)
                for part in range(2):
                    for g in range(2):
                        c0 = 1024 * part + 512 * g
                        m = mm(ps[64 * g:64 * g + 64, part, :], Ebc[0:96, :], b12s[0:96, c0:c0 + 512], False, True)
                m.then_inc(sem("hid_done"), 1)
                select(b + 2)
                pe.wait_ge(sem("act_ready"), b + 1)
                for j in range(4):
                    m = pe.transpose(ps[:, 4, P * j:P * j + P], a_sb[:, P * j:P * j + P], ident)
                m.then_inc(sem("actT_done"), 1)
                turn_rows(b + 2)
                pe.wait_ge(sem("actT_ready"), b + 1)
                for u in range(4, 6):
                    s = uslot[u]
                    w = slots[s].rearrange("p k n -> p (k n)").rearrange("p (k n) -> p k n", k=4)
                    pe.wait_ge(landed[s], e * 16 + 16 * (before[s] + 1))
                    for kk in range(4):
                        k = 4 * (u - 4) + kk
                        for g in range(2):
                            m = mm(ps[64 * g:64 * g + 64, 2, :], actT[:, k % 4, 64 * (k // 4):64 * (k // 4) + 64],
                                   w[:, kk, 512 * g:512 * g + 512], k == 0, False)
                    m.then_inc(used[s], 1)
                for g in range(2):
                    c0 = 2048 + 512 * g
                    m = mm(ps[64 * g:64 * g + 64, 2, :], Ebc[0:96, :], b12s[0:96, c0:c0 + 512], False, True)
                m.then_inc(sem("y_done"), 1)
                pe.wait_ge(sem("pg_ready"), b + 1)
                for tt, (t0, tn) in enumerate(TILES):
                    m = pe.transpose(ps[:, 4, t0:t0 + tn], Pg[0:tn, tt, :], ident[0:tn, 0:tn])
                m.then_inc(sem("pgT_done"), 1)
            pe.wait_ge(sem("ple_in"), 48)
            pe.wait_ge(sem("xselT_ready"), nb + 1)
            pe.wait_ge(sem("xsel_ready"), nb + 1)
            for k in range(2):
                for tt, (t0, tn) in enumerate(TILES):
                    m = pe.transpose(ps[:, P_BANKS[k], t0:t0 + tn], ptok[0:tn, tt, k * P:(k + 1) * P], ident[0:tn, 0:tn])
            m.then_inc(sem("pT_done"), 1)
            pe.wait_ge(sem("ysb_ready"), nb + 1)
            pe.wait_ge(sem("pgT_ready"), nb + 1)
            for tt, (t0, tn) in enumerate(TILES):
                if tt < 2:
                    pe.wait_ge(sem(("comb_free", "hid_free")[tt]), (nb * 3 + 1, nb + 1)[tt])
                else:
                    pe.wait_ge(sem("pT_ready"), 2)
                for g in range(2):
                    m = mm(ps[:, LAST_BANKS[tt] + g, :], PgT[64 * g:64 * g + 64, t0:t0 + P], y_sb[64 * g:64 * g + 64, :], True, True)
                m.then_inc(sem("comb_done"), 1)

            pe.wait_ge(landed[uslot[2]], 16 * (before[uslot[2]] + NE + 1))
            wp = slots[uslot[2]].rearrange("p k n -> p (k n)")[:, 0:2048].rearrange("p (k n) -> p k n", k=2)

            def ple_products(n, bank, lhsT, weights, kn):
                tt = min(n // 2, 2)
                t0, tn = TILES[tt]
                for k in range(kn):
                    if tt < 2:
                        m = mm(ps[:, bank, :], lhsT[:, k, t0:t0 + tn], weights(k, n % 2), k == 0, k == kn - 1)
                    else:
                        for g in range(2):
                            m = mm(ps[64 * g:64 * g + 64, bank, :], lhsT[:, k, t0:t0 + tn], weights(k, g), k == 0, k == kn - 1)
                return m

            def turn_h3(ks):
                pe.wait_ge(sem("xn_ready"), 9)
                for k in ks:
                    if k >= 3:
                        odd = (k - 3) % 2
                        pe.wait_ge(sem(("hT_ready", "hT_odd_ready")[odd]), KD + odd + (k - 3) // 2 + 1)
                    for tt, (t0, tn) in enumerate(TILES):
                        m = pe.transpose(ps[:, H3_BANKS[k % 3], t0:t0 + tn], h2[0:tn, tt, k * P:(k + 1) * P], ident[0:tn, 0:tn])
                    m.then_inc(sem("hT_done"), 1)

            for n in range(5):
                if n == 2:
                    pe.wait_ge(sem("comb_free"), nb * 3 + 2)
                elif n == 4:
                    pe.wait_ge(sem("comb_free"), nb * 3 + 4)
                    turn_h3(range(3))
                ple_products(n, PLE_BANKS[n], pT, lambda k, g: wp[:, k, 512 * g:512 * g + 512], 2).then_inc(sem("ple_done"), 1)
            turn_h3(range(3, KD))
            pe.wait_ge(sem("hT_ready"), KD + KD // 2)
            pe.wait_ge(sem("hT_odd_ready"), KD + 1 + KD // 2)
            for half in range(2):
                pe.wait_ge(landed[uslot[half]], 16 * (before[uslot[half]] + NE + 1))
            for n in range(5):
                if n >= 2:
                    pe.wait_ge(sem("ple_sig_ready"), n - 1)
                ple_products(n, n % 2, h3T, lambda k, g: slots[uslot[g]][:, k, :], KD).then_inc(sem("ple_done"), 1)

        @block.scalar
        def _(act):
            ch = Chain(act, sem("act_chain"))
            ACTF = nc.scalar.activation

            def rms(tt, squares):
                tn = TILES[tt][1]
                ch.link(ACTF(squares[0:tn], x[0:tn, tt, :], ACT.Square, accum_out=ssq[0:tn, tt:tt + 1]))
                ACTF(rstd[0:tn, tt:tt + 1], ssq[0:tn, tt:tt + 1], ACT.Sqrt, bias=eps_col[0:tn], scale=1.0 / D).then_inc(sem("rms_ready"), 1)

            act.wait_ge(sem("zeroed"), 4)
            ACTF(warm, eps_col, ACT.Sqrt)
            act.wait_ge(sem("x_in"), 32)
            for tt in range(3):
                rms(tt, view(qkv_at + tt * D, D))
            act.wait_ge(sem("cols_ready"), 1)
            for k in range(0, KD, 2):
                act.wait_ge(sem("hT_done"), k + 1)
                ACTF(hT[:, k, :], pj[k % 2][:, 0:TOK], ACT.Copy, scale=g1[:, k:k + 1]).then_inc(sem("hT_ready"), 1)

            def silu_part(n):
                act.wait_ge(sem("conv_done"), n + 1)
                if n >= 2:
                    act.wait_ge(sem("silu_done"), 2 * (n - 1))
                ACTF(sg[n % 2][:, 0:CW], cv[n % 2][:, 0:CW], ACT.Sigmoid).then_inc(sem("sig_done"), 1)

            act.wait_ge(sem("pool_zeroed"), 3)
            for n in range(FT):
                act.wait_ge(proj_done, n + 1)
                if n >= 3:
                    act.wait_ge(sem("conv_done"), n - 2)
                    act.wait_ge(sem("last3_done"), 2 * (n - 2))
                zs = zpad[n % 3][:, 3 + SEQ:].rearrange("p (b j) -> p b j", b=DB)
                ACTF(zs[:, :, 3:3 + DS], pj[n % 2][:, SEQ:TOK].rearrange("p (b j) -> p b j", b=DB), ACT.Copy)
                ACTF(zpad[n % 3][:, 3:3 + SEQ], pj[n % 2][:, 0:SEQ], ACT.Copy).then_inc(bank_free[n % 2], 1)
                if n:
                    silu_part(n - 1)
                m = n - 4
                if 0 <= m < 2 * H:
                    act.wait_ge(sem("sumsq_done"), m + 1)
                    ACTF(rs[:, m, :], ps[:, 2 + m % 6, 0:TOK], ACT.Copy).then_inc(sem("ln_done"), 1)
            silu_part(FT - 1)
            act.wait_ge(sem("consts_in"), 16)
            act.wait_ge(sem("ab_in"), 48)
            act.wait_ge(sem("abs_ready"), 1)
            ch(ACTF(alog, alog, ACT.Exp))
            ch(ACTF(beta, beta, ACT.Exp, scale=-1.0))
            ch.link(ACTF(tB, tB, ACT.Exp, scale=-1.0))
            ACTF(tB, tB, ACT.Ln, bias=1.0).then_inc(sem("softplus_ready"), 1)
            act.wait_ge(sem("ln_done"), 2 * H)
            left = [2 * N_GATE]

            def keep(halves=2):
                for _ in range(halves):
                    n, part = divmod(left[0], 2)
                    left[0] += 1
                    if not part:
                        continue
                    act.wait_ge(proj_done, n + 1)
                    if N_V <= n < N_MA:
                        half, tt = divmod(n - N_V, 3)
                        if n == N_V:
                            act.wait_ge(sem("qk_normed"), 2)
                        if tt < 2:
                            m = ACTF(vtok[:, tt, 512 * half:512 * half + 512], pj[n % 2], ACT.Copy)
                        else:
                            for g in range(2):
                                c0 = 512 * half + 256 * g
                                m = ACTF(vtok[0:64, 2, c0:c0 + 256], pj[n % 2][64 * g:64 * g + 64, 0:256], ACT.Copy)
                        m.then_inc(bank_free[n % 2], 1)
                    else:
                        dst = gateT if n < N_U else uT if n < N_V else maT if n < N_MB else mbT
                        i = (n - N_GATE) % 8 if n < N_V else (n - N_MA) % 8
                        ACTF(dst[:, i, :], pj[n % 2][:, 0:TOK], ACT.Copy).then_inc(bank_free[n % 2], 1)

            ch(ACTF(rs, rs, ACT.Ln, bias=cst("eps")))
            keep()
            ch.wait()
            ACTF(rs[:, 0:H], rs[:, 0:H], ACT.Exp, bias=cst("qscale"), scale=-0.5).then_inc(sem("rs_ready"), 1)
            keep()
            ACTF(rs[:, H:2 * H], rs[:, H:2 * H], ACT.Exp, scale=-0.5).then_inc(sem("rs_ready"), 1)
            act.wait_ge(sem("gce_ready"), 1)
            ch(ACTF(dcol, dcol, ACT.Exp))
            ch(ACTF(kdec[0:64], gce[0:64, 2, 0:8], ACT.Exp))
            ch.link(ACTF(gend, gend, ACT.Exp))
            keep()
            act.wait_ge(sem("newrows_stored"), 32)

            for tt, (t0, tn) in enumerate(TILES):
                L0 = sum(LEVELS[:tt])
                keep(1)
                act.wait_ge(sem("gcrow_done"), tt + 1)
                if tt:
                    act.wait_ge(sem("qd_ready"), tt)
                    act.wait_ge(sem("rT_ready"), tt)
                ACTF(GR[:, :, 0:tn], G45(tn), ACT.Exp).then_inc(sem("GR_ready"), 1)
                act.wait_ge(sem("dd_ready"), tt + 1)
                ACTF(DBm[0:tn, :, 0:tn], DBm[0:tn, :, 0:tn], ACT.Exp).then_inc(sem("dec_ready"), 1)
                keep(3 if tt < 2 else 2)
                act.wait_ge(sem("kt_done"), tt + 1)
                act.wait_ge(sem("dcol_ready"), 1)
                for h in range(H):
                    m = ACTF(kd[0:tn, h, :], G01()[0:tn, h, :], ACT.Copy, scale=dcol[0:tn, tt, h:h + 1])
                m.then_inc(sem("kd_ready"), 1)
                keep(1 if tt < 2 else 2)
                for lev in range(LEVELS[tt]):
                    i = L0 + lev
                    if lev == 6:
                        act.wait_ge(sem("XT_ready"), i)
                        for b in (0, HB):
                            ACTF(XT[b:b + HB, :, b:b + HB], XTd[b:b + HB], ACT.Copy)
                        act.wait_ge(sem("W_done"), i + 1)
                        ACTF(Wd[64:128], blocks64(6)[64:128], ACT.Copy).then_inc(sem("W_ready"), 1)
                    elif lev:
                        act.wait_ge(sem("W_done"), i + 1)
                        ACTF(Wd[0:tn], blocks64(6)[0:tn], ACT.Copy).then_inc(sem("W_ready"), 1)
                    keep(fill_at_level(tt, lev))
                if tt == 1:
                    keep()
                keep(1)
                if tt < 2:
                    act.wait_ge(sem("r_done"), tt + 1)
                    ACTF(r[0:tn], G45()[0:tn], ACT.Copy).then_inc(sem("r_ready"), 1)
                    keep()
                else:
                    keep()
                    assert left[0] >= 2 * N_MA
                    for s, (_, sn) in enumerate(TILES):
                        ACTF(vtok[0:sn, s, :], vtok[0:sn, s, :], ACT.Gelu, accum_out=msum[0:sn, s:s + 1]).then_inc(sem("gelu_ready"), 1)
                    ACTF(uT, uT, ACT.Gelu).then_inc(sem("ugelu_ready"), 1)
                    keep()
                act.wait_ge(sem("u_done"), tt + 1)
                ACTF(W[0:tn], G01()[0:tn], ACT.Copy).then_inc(sem("u_ready"), 1)
                keep(4)
                act.wait_ge(sem("sumsq_done"), 2 * H + tt + 1)
                ACTF(rT[:, :, 0:tn], G01(tn), ACT.Ln, bias=cst("eps"), scale=1.0 / P).then_inc(sem("ln_done"), 1)
                act.wait_ge(sem("ln_done"), 2 * H + tt + 1)
                ACTF(rT[:, :, 0:tn], rT[:, :, 0:tn], ACT.Exp, scale=-0.5).then_inc(sem("rs_ready"), 1)
                if tt < 2:
                    keep()

            def spread_u(h):
                if h >= 3:
                    act.wait_ge(sem("S0_product"), 2 * (h - 1))
                for b in range(4):
                    m = ACTF(XT[0:64, b, :], W[0:64, h, :], ACT.Copy, scale=cst("seq4", 64)[:, b:b + 1])
                m.then_inc(sem("uexp_odd_ready"), 1)

            act.wait_ge(sem("u_ready"), 3)
            spread_u(1)
            act.wait_ge(sem("o_normed"), 3)
            ACTF(sgm, gateT, ACT.Sigmoid).then_inc(sem("branch_sig_ready"), 1)
            spread_u(3)
            keep()
            ACTF(maT, maT, ACT.Sigmoid).then_inc(sem("branch_sig_ready"), 1)
            keep(3)
            spread_u(5)
            spread_u(7)
            assert left[0] == 2 * N_YA
            for n in (N_YA - 1, N_YA - 2):
                evacuated(act, n)
            ACTF(mbT, mbT, ACT.Sigmoid).then_inc(sem("branch_sig_ready"), 1)
            for tt, (t0, tn) in enumerate(TILES):
                act.wait_ge(sem("vc_ready"), tt + 1)
                ch.link(ACTF(squares[0:tn], vtok[0:tn, tt, :], ACT.Square, accum_out=mvar[0:tn, tt:tt + 1]))
            ACTF(mrs, mvar, ACT.Sqrt, bias=cst("eps"), scale=1.0 / D).then_inc(sem("ln_std_ready"), 1)
            def turned(ks):
                for k in ks:
                    act.wait_ge(sem("hT_done"), KD + k // 2 * 2 + 2)
                    ACTF(h2T[:, k, 0:SEQ], h2T_bank(k), ACT.Copy, scale=g2[:, k:k + 1]).then_inc(sem("hT_ready"), 1)

            for tt in range(3):
                if tt == 2:
                    turned((0, 1))
                evacuated(act, N_WO + 3 + tt)
                rms(tt, h2[:, tt, :])
            turned((4, 5))
            act.wait_ge(sem("top_ready"), 1)
            ACTF(gates[:, :, 0:TOPK], gates[:, :, 0:TOPK], ACT.Exp).then_inc(sem("gexp_ready"), 1)

            def rows_out(value):
                act.wait_ge(sem("sel_done"), value)
                ACTF(xsel, ps[:, 3, :], ACT.Copy).then_inc(sem("xsel_ready"), 1)

            rows_out(1)
            act.wait_ge(sem("tables_ready"), 1)
            nb = act.value_load(tab[0:1, 96 + NE - 1:96 + NE], min_val=1, max_val=MAXB)
            with act.Fori(0, nb) as b:
                act.wait_ge(sem("glu_gate_ready"), b + 1)
                ACTF(s_sb, g_sb, ACT.Sigmoid, scale=ALPHA).then_inc(sem("glu_sig_ready"), 1)
                rows_out(b + 2)
                act.wait_ge(sem("actT_done"), b + 1)
                ACTF(actT.rearrange("p j c -> p (j c)"), ps[:, 4, :], ACT.Copy).then_inc(sem("actT_ready"), 1)
                act.wait_ge(sem("y_done"), b + 1)
                ACTF(y_sb, ps[:, 2, :], ACT.Copy).then_inc(sem("ysb_ready"), 1)
                act.wait_ge(sem("pgT_done"), b + 2)
                ACTF(PgT[:, 0:TOK], ps[:, 4, 0:TOK], ACT.Copy).then_inc(sem("pgT_ready"), 1)

            act.wait_ge(sem("pT_done"), 1)
            for k in range(2):
                ACTF(pT[:, k, :], ps[:, P_BANKS[k], 0:TOK], ACT.Copy).then_inc(sem("pT_ready"), 1)
            for tt in range(3):
                act.wait_ge(sem("comb_free"), nb * 3 + 2 + tt)
                rms(tt, h2[:, tt, :])
            for k in range(0, KD, 2):
                act.wait_ge(sem("hT_done"), 2 * KD + 1 + k + 1)
                ACTF(h3T[:, k, :], ps[:, H3_BANKS[k % 3], 0:TOK], ACT.Copy, scale=g3[:, k:k + 1]).then_inc(sem("hT_ready"), 1)
            for n in range(5):
                act.wait_ge(sem("ple_done"), 5 + n + 1)
                if n >= 2:
                    act.wait_ge(sem("ple_added"), n - 1)
                ACTF([g_sb, u_sb][n % 2], ps[:, n % 2, :], ACT.Sigmoid).then_inc(sem("ple_sig_ready"), 1)
                if n % 2 or n == 4:
                    tt = n // 2
                    act.wait_ge(sem("ple_added"), n + 1)
                    rms(tt, h2[:, tt, :])

        @block.vector
        def _(dve):
            ch = Chain(dve, sem("dve_chain"))
            TT, TS, STT = dve.tensor_tensor, dve.tensor_scalar, dve.scalar_tensor_tensor

            def over_heads(ap, rows, n):
                return ap.rearrange("p (a c) -> p a c", a=1).broadcast_to([rows, H, n])

            dve.memset(eps_col, EPS).then_inc(sem("zeroed"), 1)
            dve.memset(mvar, 1.0).then_inc(sem("zeroed"), 1)
            dve.memset(msum, 0.0).then_inc(sem("zeroed"), 1)
            dve.memset(ab, 0.0).then_inc(sem("zeroed"), 1)
            def normalise(k, tt, dst):
                tn = TILES[tt][1]
                dve.wait_ge(sem("rms_ready"), 3 * (k - 1) + tt + 1)
                ch.link(dve.reciprocal(rstd[0:tn, tt:tt + 1], rstd[0:tn, tt:tt + 1]))
                TS(dst[0:tn, tt, :], x[0:tn, tt, :], rstd[0:tn, tt:tt + 1], None, ALU.mult).then_inc(sem("xn_ready"), 1)

            for tt in range(3):
                if tt == 2:
                    dve.wait_ge(sem("rows_turned"), 1)
                    dve.tensor_copy(colsT[:, 0:121], pj[1][:, 0:121]).then_inc(sem("cols_ready"), 1)
                normalise(1, tt, x)
            dve.wait_ge(sem("cols_ready"), 1)
            for k in range(1, KD, 2):
                dve.wait_ge(sem("hT_done"), k + 1)
                TS(hT[:, k, :], pj[k % 2][:, 0:TOK], g1[:, k:k + 1], None, ALU.mult).then_inc(sem("hT_odd_ready"), 1)
            for g in range(6):
                dve.wait_ge(sem("old_done"), g + 1)
                dve.tensor_copy(oldT[:, 4 * g:4 * g + 4, :], ps[:, 2 + g, 0:96].rearrange("p (f j) -> p f j", f=4)).then_inc(sem("old_turned"), 1)

            def samples(w):
                return w[:, 3 + SEQ:3 + SEQ + DB * (3 + DS)].rearrange("p (b j) -> p b j", b=DB)[:, :, 0:DS]

            def silu_mul(n):
                dve.wait_ge(sem("sig_done"), n + 1)
                TT(qkvT[:, n, 0:SEQ], cv[n % 2][:, 0:SEQ], sg[n % 2][:, 0:SEQ], ALU.mult).then_inc(sem("silu_done"), 1)
                TT(qkvT[:, n, SEQ:TOK].rearrange("p (b j) -> p b j", b=DB), samples(cv[n % 2]), samples(sg[n % 2]),
                   ALU.mult).then_inc(sem("silu_done"), 1)

            dve.wait_ge(sem("cols_ready"), 1)
            for n in range(FT):
                evacuated(dve, n)
                dve.wait_ge(sem("old_filled"), n + 1)
                z, a = zpad[n % 3], cv[n % 2][:, 0:CW]
                if n >= 2:
                    dve.wait_ge(sem("silu_done"), 2 * (n - 1))
                ch.link(TS(a, z[:, 0:CW], g_conv[:, 0, n:n + 1], None, ALU.mult))
                for i in range(1, TAPS - 1):
                    ch.link(STT(a, z[:, i:i + CW], g_conv[:, i, n:n + 1], a, ALU.mult, ALU.add))
                STT(a, z[:, TAPS - 1:TAPS - 1 + CW], g_conv[:, TAPS - 1, n:n + 1], a, ALU.mult, ALU.add).then_inc(sem("conv_done"), 1)
                if n:
                    silu_mul(n - 1)
            silu_mul(FT - 1)

            dve.wait_ge(proj_done, N_AB + 1)
            dve.wait_ge(sem("zeroed"), 4)
            dve.wait_ge(sem("ab_in"), 48)
            ch(dve.tensor_copy(ab[0:64, 2, :], pj[0][0:64, 32:48]))
            dve.tensor_copy(ab[:, 0:2, :], pj[0][:, 0:32].rearrange("p (a c) -> p a c", a=2)).then_inc(bank_free[0], 1)
            evacuated(dve, N_AB)
            ch.wait()

            def wide8(ap):
                return ap.rearrange("p (a c) -> p a c", a=1).broadcast_to([P, 3, 8])
            ch(TS(beta, ab[:, :, 8:16], -80.0, None, ALU.max))
            ch.link(TT(tA, ab[:, :, 0:8], wide8(dtb), ALU.add))
            ch.link(TS(tB, tA, -1.0, None, ALU.mult))
            TT(tB, tB, tA, ALU.max).then_inc(sem("abs_ready"), 1)
            dve.wait_ge(sem("softplus_ready"), 1)
            ch(TS(beta, beta, 1.0, None, ALU.add))
            ch.link(STT(tA, tA, 0.0, tB, ALU.max, ALU.add))
            ch(dve.reciprocal(beta, beta))
            STT(gg, tA, -1.0, wide8(alog), ALU.mult, ALU.mult).then_inc(sem("g_ready"), 3)

            for g in range(6):
                dve.wait_ge(sem("newrows_done"), g + 1)
                dve.tensor_copy(new_rows[0:27, 512 * g:512 * g + 512], ps[0:27, 2 + g, :]).then_inc(sem("newrows_ready"), 1)
            for i in range(2):
                dve.wait_ge(sem("rs_ready"), i + 1)
                TT(qkvT[:, H * i:H * i + H, :], qkvT[:, H * i:H * i + H, :], rs[:, H * i:H * i + H, :], ALU.mult).then_inc(sem("qk_normed"), 1)
            dve.memset(gce, 0.0).then_inc(sem("zeroed"), 1)
            dve.wait_ge(sem("zeroed"), 5)
            dve.wait_ge(sem("cum_done"), 1)
            ch(dve.tensor_copy(gce[0:64, 2, :], ps[0:64, 7, 32:48]))
            ch.link(dve.tensor_copy(gce[:, 0:2, :], ps[:, 7, 0:32].rearrange("p (a c) -> p a c", a=2)))
            ch(dve.tensor_copy(gend, gce[:, :, 8:16]))
            TT(dcol, gce[:, :, 8:16], gce[:, :, 0:8], ALU.subtract).then_inc(sem("gce_ready"), 1)

            for tt, (t0, tn) in enumerate(TILES):
                L0 = sum(LEVELS[:tt])
                tri = cst("tri8" if tt == 2 else "tri", tn, tn)
                if tt:
                    dve.wait_ge(sem("u_done"), tt)
                else:
                    dve.wait_ge(sem("g_ready"), 3)
                    dve.wait_ge(sem("newrows_ready"), 6)
                TT(X[0:tn, :, 0:tn], over_heads(tri, tn, tn),
                   gg[0:tn, tt, :].rearrange("p (a c) -> p a c", c=1).broadcast_to([tn, H, tn]), ALU.mult).then_inc(sem("RH_ready"), 1)
                dve.wait_ge(sem("GR_ready"), tt + 1)
                if tt:
                    dve.wait_ge(sem("XT_ready"), L0)
                for h in range(H):
                    m = TS(DBm[0:tn, h, 0:tn], G45(tn)[0:tn, h, :], gce[0:tn, tt, h:h + 1], 0.0, ALU.subtract, ALU.min)
                m.then_inc(sem("dd_ready"), 1)
                if tt == 0:
                    dve.wait_ge(sem("act_chain"), 10)
                    ch.link(TS(kdec[0:64], kdec[0:64], -1.0, None, ALU.mult))
                    TT(dcol, dcol, beta, ALU.mult).then_inc(sem("dcol_ready"), 1)
                dve.wait_ge(sem("dec_ready"), tt + 1)
                for h in range(H):
                    m = STT(DBm[0:tn, h, 0:tn], DBm[0:tn, h, 0:tn], beta[0:tn, tt, h:h + 1], tri, ALU.mult, ALU.mult)
                ch.link(m)
                dve.wait_ge(sem("kk_done"), tt + 1)
                if tt:
                    dve.wait_ge(sem("o_done"), tt)
                    dve.wait_ge(sem("Al_ready"), masks_before(tt))
                if tt < 2:
                    TT(AToff[0:64], G01()[0:64, :, HB:], DBm[0:64, :, HB:], ALU.mult)
                    TT(ATd[64:128], G01()[64:128, :, HB:], DBm[64:128, :, HB:], ALU.mult)
                TT(ATd[0:64], G01(tn)[0:64, :, 0:HB], DBm[0:64, :, 0:HB], ALU.mult).then_inc(sem("AT_ready"), 1)
                TT(mT[0:tn, :, 0:tn], G23(tn)[0:tn], DBm[0:tn, :, 0:tn], ALU.mult).then_inc(sem("mT_ready"), 1)
                for lev in range(LEVELS[tt]):
                    i = L0 + lev
                    last = lev == LEVELS[tt] - 1
                    if lev == 0:
                        dve.wait_ge(sem("Al_ready"), masks_before(tt) + 1)
                        dve.wait_ge(sem("W_done"), i + 1)
                        TT(XTd[0:tn], over_heads(cst("ident64", tn), tn, HB), Al[0][0:tn], ALU.subtract).then_inc(sem("XT_ready"), 1)
                        TT(Xd[0:tn], over_heads(cst("ident64", tn), tn, HB), blocks64(6)[0:tn], ALU.subtract).then_inc(sem("X_ready"), 1)
                    elif lev == 6:
                        dve.wait_ge(sem("DT_done"), i - tt)
                        TS(XT[0:64, :, HB:], blocks64(4)[0:64], -1.0, None, ALU.mult).then_inc(sem("XT_ready"), 1)
                    else:
                        if not last:
                            dve.wait_ge(sem("D_done"), i - 2 * tt)
                            dve.wait_ge(sem("X_ready"), i - tt)
                            TT(Xd[0:tn], Xd[0:tn], blocks64(2)[0:tn], ALU.subtract).then_inc(sem("X_ready"), 1)
                        dve.wait_ge(sem("DT_done"), i - tt)
                        dve.wait_ge(sem("XT_ready"), i)
                        TT(XTd[0:tn], XTd[0:tn], blocks64(4)[0:tn], ALU.subtract).then_inc(sem("XT_ready"), 1)
                vT = qkvT[:, 2 * H:3 * H, t0:t0 + tn]
                if tt == 0:
                    dve.tensor_copy(rT[:, :, 0:tn], vT).then_inc(sem("rT_ready"), 1)
                elif tt == 1:
                    dve.wait_ge(sem("kS_done"), 1)
                    ch.link(TT(rT[:, :, 0:tn], G01(tn), GR[:, :, 0:tn], ALU.mult))
                    TT(rT[:, :, 0:tn], vT, rT[:, :, 0:tn], ALU.subtract).then_inc(sem("rT_ready"), 1)
                    dve.tensor_copy(qS[:, :, 0:tn], G23(tn)).then_inc(sem("qS_ready"), 1)
                else:
                    dve.wait_ge(sem("r_done"), 3)
                    for h in range(H):
                        dve.wait_ge(sem("kS_head"), h + 1)
                        mask4 = cst("seq4").rearrange("p (a c) -> p a c", c=1)
                        TT(W[:, 0:4, :], ps[:, 2 + h % 4, :].rearrange("p (b v) -> p b v", v=P), mask4.broadcast_to([P, 4, P]),
                           ALU.mult).then_inc(sem("kS_read"), 1)
                        dve.wait_ge(sem("kS_read"), h + 1)
                        ch.link(dve.tensor_reduce(r[:, h, :], W[:, 0:4, :].rearrange("p b v -> p v b"), AX.X, ALU.add))
                        STT(r[0:64, h, :], r[0:64, h, :], kdec[0:64, h:h + 1], G45()[0:64, h, :], ALU.mult, ALU.add).then_inc(sem("r_ready"), 1)
                o = oT[:, :, t0:t0 + tn]
                dve.wait_ge(sem("o_done"), tt + 1)
                dve.wait_ge(sem("qd_ready"), tt + 1)
                if tt != 1:
                    ch.link(dve.tensor_copy(o, G23(tn)))
                else:
                    dve.wait_ge(sem("qS_ready"), 1)
                    ch.link(TT(o, qS[:, :, 0:tn], G23(tn), ALU.add))
                TT(qS[:, :, 0:tn], o, o, ALU.mult).then_inc(sem("osq_ready"), 1)
                dve.wait_ge(sem("osq_ready"), tt + 1)
                dve.nop().then_inc(sem("o_ready"), 1)
                if tt == 0:
                    dve.wait_ge(sem("S_done"), 1)
                    dve.tensor_copy(S, G45()).then_inc(sem("S_ready"), 1)
                elif tt == 1:
                    dve.wait_ge(sem("S_done"), 2)
                    dve.wait_ge(sem("S_ready"), 1)
                    for h in range(H):
                        m = STT(S[:, h, :], S[:, h, :], gend[:, 1, h:h + 1], G45()[:, h, :], ALU.mult, ALU.add)
                    m.then_inc(sem("S_ready"), 1)
                dve.wait_ge(sem("rs_ready"), 2 + tt + 1)
                TT(o, o, rT[:, :, 0:tn], ALU.mult).then_inc(sem("o_normed"), 1)
            def merge_a(i):
                n = N_YA + i
                dve.wait_ge(proj_done, n + 1)
                dve.wait_ge(sem("gated_ready"), 1)
                dve.wait_ge(sem("branch_sig_ready"), 2)
                TT(mixT[:, i, :], maT[:, i, :], pj[n % 2][:, 0:TOK], ALU.mult).then_inc(bank_free[n % 2], 1)

            for h in range(H):
                dve.wait_ge(sem(f"S0_in{h % 4}"), 16 * (3 + h // 4))
                ch.link(TT(S0[h % 4], S0[h % 4], GR[:, h, DS - 1:64:DS].rearrange("p (a c) -> p a c", c=1).broadcast_to([P, DB, P]),
                           ALU.mult))
                dve.wait_ge(sem("S0_product"), 2 * h + 2)
                bank = [6, 4][h % 2]
                TT(S0[h % 4].rearrange("p b v -> p (b v)"), S0[h % 4].rearrange("p b v -> p (b v)"),
                   ps[:, bank:bank + 2, :].rearrange("p a c -> p (a c)"), ALU.add).then_inc(sem("S0_new"), 1)
                if h == 1:
                    dve.wait_ge(sem("branch_sig_ready"), 1)
                    dve.wait_ge(sem("o_normed"), 3)
                    ch.link(TT(gateT, gateT, sgm, ALU.mult))
                elif h == 2:
                    STT(oT, oT, dng, gateT, ALU.mult, ALU.mult).then_inc(sem("gated_ready"), 1)
                elif h == 5:
                    merge_a(0)
                    merge_a(1)

            dve.wait_ge(sem("gelu_ready"), 3)
            ch.link(TS(msum, msum, 1.0 / D, None, ALU.mult))
            for tt, (t0, tn) in enumerate(TILES):
                TS(vtok[0:tn, tt, :], vtok[0:tn, tt, :], msum[0:tn, tt:tt + 1], None, ALU.subtract).then_inc(sem("vc_ready"), 1)

            def norm_v(tt):
                tn = TILES[tt][1]
                if tt == 0:
                    dve.wait_ge(sem("ln_std_ready"), 1)
                    ch.link(dve.reciprocal(mrs, mrs))
                    dve.wait_ge(sem("mlp_in"), 16 * 12)
                    dve.wait_ge(sem("vc_ready"), 3)
                ch.link(STT(vtok[0:tn, tt, :], vtok[0:tn, tt, :], mrs[0:tn, tt:tt + 1], lng[0:tn], ALU.mult, ALU.mult))
                TT(vtok[0:tn, tt, :], vtok[0:tn, tt, :], lnb[0:tn], ALU.add).then_inc(sem("vnorm_ready"), 1)

            for i in range(2, 4):
                merge_a(i)
            dve.wait_ge(sem("branch_sig_ready"), 3)
            for tt in range(3):
                norm_v(tt)
            merge_a(4)
            dve.wait_ge(sem("wT_done"), 1)
            TT(WT, G01(), over_heads(cst("tri"), P, P), ALU.mult).then_inc(sem("WT_ready"), 1)
            TT(WT8[0:64], G23(64)[0:64], over_heads(cst("tri8", 64, 64), 64, 64), ALU.mult).then_inc(sem("WT_ready"), 1)
            merge_a(5)
            dve.wait_ge(sem("ugelu_ready"), 1)
            for tt, (t0, tn) in enumerate(TILES):
                for a in range(2):
                    k = 2 * tt + a
                    dve.wait_ge(sem("mix_done"), k + 1)
                    sv = ps[:, 2 + k, :].rearrange("p (g c) -> p g c", g=4)[:, :, 0:tn]
                    st = [stmp, stmp2][k % 2].rearrange("p (g c) -> p g c", g=4)[:, :, 0:tn]
                    if k >= 2:
                        dve.wait_ge(sem("us_ready"), k - 1)
                    if tt < 2:
                        ch.link(TT(st, sv, bsb[:, 4 * a:4 * a + 4, :], ALU.add))
                    else:
                        for g in range(4):
                            bias = bsb[:, 4 * a + g, 0:DS].rearrange("p (b j) -> p b j", b=1).broadcast_to([P, DB, DS])
                            m = TT(st[:, g, :].rearrange("p (b j) -> p b j", b=DB), sv[:, g, :].rearrange("p (b j) -> p b j", b=DB), bias, ALU.add)
                        ch.link(m)
                    TT(uT[:, 4 * a:4 * a + 4, t0:t0 + tn], uT[:, 4 * a:4 * a + 4, t0:t0 + tn], st, ALU.mult).then_inc(sem("us_ready"), 1)
            dve.wait_ge(sem("us_ready"), 6)
            for i in range(6, 8):
                merge_a(i)
            for i in range(8):
                n = N_YB + i
                dve.wait_ge(proj_done, n + 1)
                evacuated(dve, N_YA + 6)
                evacuated(dve, N_YA + 7)
                tmp = [stmp, stmp2][i % 2][:, 0:TOK]
                if i >= 2:
                    dve.wait_ge(sem("merged"), i - 1)
                TT(tmp, mbT[:, i, :], pj[n % 2][:, 0:TOK], ALU.mult).then_inc(bank_free[n % 2], 1)
                evacuated(dve, n)
                TT(mixT[:, i, :], mixT[:, i, :], tmp, ALU.add).then_inc(sem("merged"), 1)
            dve.wait_ge(sem("x_in"), 64)
            dve.wait_ge(sem("vnorm_ready"), 3)
            dve.wait_ge(sem("merged"), KD)
            for half in range(2):
                for tt, (t0, tn) in enumerate(TILES):
                    n = N_WO + 3 * half + tt
                    dve.wait_ge(proj_done, n + 1)
                    if tt < 2:
                        xa = x[:, tt, 512 * half:512 * half + 512]
                        TT(xa, xa, pj[n % 2], ALU.add).then_inc(bank_free[n % 2], 1)
                    else:
                        xa, xb = (x[0:64, 2, 512 * half + 256 * g:512 * half + 256 * g + 256] for g in range(2))
                        ch.link(dve.tensor_copy(moved, pj[n % 2][64:128, 0:256]))
                        ch.link(TT(xb, xb, moved, ALU.add))
                        TT(xa, xa, pj[n % 2][0:64, 0:256], ALU.add).then_inc(bank_free[n % 2], 1)
                    if half and tt < 2:
                        normalise(2, tt, h2)

            def turned(ks):
                for k in ks:
                    dve.wait_ge(sem("hT_done"), KD + k // 2 * 2 + 2)
                    TS(h2T[:, k, 0:SEQ], h2T_bank(k), g2[:, k:k + 1], None, ALU.mult).then_inc(sem("hT_odd_ready"), 1)

            turned((2, 3, 6))
            normalise(2, 2, h2)
            turned((7,))
            dve.wait_ge(sem("hT_done"), 2 * KD + 1)
            TT(h2T[:, :, SEQ:TOK], ps[:, 6, :].rearrange("p (k s) -> p k s", k=KD),
               g2.rearrange("p (k a) -> p k a", a=1).broadcast_to([P, KD, DB * DS]), ALU.mult).then_inc(sem("hT_odd_ready"), 1)

            def pick(column):
                for tt, (t0, tn) in enumerate(TILES):
                    m = TS(Psel[0:tn, tt, :], cst("slot", tn, SLOTS), column(tt, tn), None, ALU.is_equal)
                m.then_inc(sem("psel_ready"), 1)

            ch(dve.memset(logit[:, 2, :], 0.0))
            dve.memset(y_sb, 0.0).then_inc(sem("ysb_ready"), 1)
            dve.memset(PgT, 0.0).then_inc(sem("pgT_ready"), 1)
            dve.wait_ge(sem("router_in"), 16 * 4)
            ex = cst("expert")
            dve.wait_ge(sem("logits_done"), 1)
            dve.tensor_copy(logitT[0:NE], ps[0:NE, 7, 0:TOK]).then_inc(sem("logitT_ready"), 1)
            dve.wait_ge(sem("logits_done"), 2)
            ch.wait()
            ch(TT(logit[0:64, 2, :], ps[0:64, 6, 2 * NE:3 * NE], rbias[0:64], ALU.add))
            ch.link(TT(logit[:, 0:2, :], ps[:, 6, 0:2 * NE].rearrange("p (t e) -> p t e", e=NE),
                       rbias.rearrange("p (a e) -> p a e", a=1).broadcast_to([P, 2, NE]), ALU.add))
            for tt in range(3):
                ch(dve.max(top8[:, tt, :], logit[:, tt, :]))
            ch.wait()
            TT(gates[:, :, 0:TOPK], top8[:, :, 0:TOPK], top8[:, :, 0:1].broadcast_to([P, 3, TOPK]), ALU.subtract).then_inc(sem("top_ready"), 1)
            for tt in range(3):
                ch(dve.max_index(idx8[:, tt, :].bitcast(U32), top8[:, tt, :], logit[:, tt, :]))
            ch.wait()
            ch.link(dve.tensor_copy(idxf, idx8.bitcast(U32)))

            def choices(ap):
                return ap.rearrange("p (t k e) -> p t k e", t=3, k=TOPK)
            ch.link(TT(choices(chosen), ex.rearrange("p (t k e) -> p t k e", t=1, k=1).broadcast_to([P, 3, TOPK, NE]),
                       idxf[:, :, 0:TOPK].rearrange("p t (k e) -> p t k e", e=1).broadcast_to([P, 3, TOPK, NE]), ALU.is_equal))
            dve.tensor_reduce(mask, choices(chosen).rearrange("p t k e -> p t e k"), AX.X, ALU.add).then_inc(sem("mask_ready"), 1)
            dve.wait_ge(sem("gexp_ready"), 1)
            ch.link(dve.tensor_reduce(gsum.rearrange("p (t a) -> p t a", a=1), gates[:, :, 0:TOPK], AX.X, ALU.add))
            ch.link(dve.reciprocal(gsum, gsum))
            ch.link(TT(gates[:, :, 0:TOPK], gates[:, :, 0:TOPK], gsum.rearrange("p (t a) -> p t a", a=1).broadcast_to([P, 3, TOPK]), ALU.mult))
            ch.link(TT(choices(chosen_g), choices(chosen),
                       gates[:, :, 0:TOPK].rearrange("p t (k e) -> p t k e", e=1).broadcast_to([P, 3, TOPK, NE]), ALU.mult))
            ch.link(dve.tensor_reduce(gmat, choices(chosen_g).rearrange("p t k e -> p t e k"), AX.X, ALU.add))
            dve.wait_ge(sem("mask_ready"), 1)
            dve.wait_ge(sem("rank_done"), 1)
            q = slice(0, NE)
            ch.link(dve.tensor_copy(cnt[q, 8:9], ps[q, 4, 0:1]))
            ch.link(TS(cnt[q, 0:4], cst("thr", NE), cnt[q, 8:9], None, ALU.is_lt))
            ch.link(dve.tensor_reduce(cnt[q, 9:10], cnt[q, 0:4], AX.X, ALU.add))
            TS(cnt[q, 4:5], cnt[q, 9:10], 1.0, None, ALU.add).then_inc(sem("blocks_ready"), 1)
            for tt, (t0, tn) in enumerate(TILES):
                R = slice(0, tn)
                ch.link(TS(etmp[R, tt, :], mask[R, tt, :], -FAR, FAR, ALU.mult, ALU.add))
                TT(pos[R, tt, :], etmp[R, tt, :], ps[R, 3, NE * tt:NE * tt + NE], ALU.add).then_inc(sem("rank_ready"), 1)
            dve.wait_ge(sem("rank_ready"), 3)
            pick(lambda tt, tn: pos[0:tn, tt, 0:1])
            dve.wait_ge(sem("through_done"), 1)
            dve.wait_ge(sem("blocks_ready"), 1)
            ch.link(dve.tensor_copy(cnt[q, 5:6], ps[q, 4, 8:9]))
            ch.link(TT(cnt[q, 6:7], cnt[q, 5:6], cnt[q, 4:5], ALU.subtract))
            ch.link(TS(cnt[q, 7:8], cnt[q, 6:7], float(SLOTS), None, ALU.mult))
            ch.link(TS(Eb3f[q], cst("block", NE), cnt[q, 5:6], None, ALU.is_lt))
            ch.link(STT(Eb[q], cst("block", NE), cnt[q, 6:7], Eb3f[q], ALU.is_ge, ALU.mult))
            for i in range(3):
                m = dve.tensor_copy(Eb3[32 * i:32 * i + 32, :], Eb[q])
                ch(m)
            ch.wait()
            dve.nop().then_inc(sem("E_ready"), 1)
            dve.wait_ge(sem("rankT_done"), 1)
            TS(posT[q], ps[q, 5, 0:TOK], cnt[q, 7:8], None, ALU.add).then_inc(sem("rankT_ready"), 1)
            dve.tensor_copy(gmT[q], ps[q, 6, 0:TOK]).then_inc(sem("rankT_ready"), 1)
            dve.wait_ge(sem("perblock_done"), 1)
            for tt, (t0, tn) in enumerate(TILES):
                R = slice(0, tn)
                ch(STT(posb[R, tt, :], cst("block", tn), -float(SLOTS), ps[R, 7, SLOTS * tt:SLOTS * tt + SLOTS], ALU.mult, ALU.add))
                ch(dve.tensor_copy(gateb[R, tt, :], ps[R, 7, 256 + SLOTS * tt:256 + SLOTS * tt + SLOTS]))
            ch(dve.tensor_copy(tab[0:1, 0:64], ps[0:1, 4, 128:192]))
            ch.link(dve.tensor_copy(tab[0:1, 96:128], ps[0:1, 4, 192:224]))
            dve.nop().then_inc(sem("tables_ready"), 1)

            dve.nop().then_inc(sem("hid_free"), 1)
            dve.nop().then_inc(sem("comb_free"), 1)
            nb = dve.value_load(tab[0:1, 96 + NE - 1:96 + NE], min_val=1, max_val=MAXB)

            def rows_turned(value):
                dve.wait_ge(sem("xT_done"), value)
                TT(xselT.rearrange("p (g j) s -> p g j s", g=2), ps[:, 5, :].rearrange("p (j g s) -> p g j s", j=4, g=2),
                   g2.rearrange("p (g j a) -> p g j a", g=2, a=1).broadcast_to([P, 2, 4, SLOTS]), ALU.mult).then_inc(sem("xselT_ready"), 1)

            rows_turned(1)
            with dve.Fori(0, nb) as b:
                dve.wait_ge(sem("pgT_done"), b + 1)
                dve.tensor_copy(Ebc[0:96, :], Eb3[0:96, bass.ds(b, 1)].broadcast_to([96, SLOTS])).then_inc(sem("ebc_ready"), 1)
                for tt, (t0, tn) in enumerate(TILES):
                    m = TS(Pg[0:tn, tt, :], cst("slot", tn), posb[0:tn, tt, bass.ds(b, 1)], gateb[0:tn, tt, bass.ds(b, 1)], ALU.is_equal, ALU.mult)
                m.then_inc(sem("pg_ready"), 1)
                dve.wait_ge(sem("sel_done"), b + 1)
                pick(lambda tt, tn: posb[0:tn, tt, bass.ds(b + 1, 1)])
                for tt, (t0, tn) in enumerate(TILES):
                    dve.wait_ge(sem("comb_done"), b * 3 + tt + 1)
                    dve.wait_ge(sem("comb_free"), b * 3 + 1)
                    TT(x[0:tn, tt, :], x[0:tn, tt, :], ps[0:tn, 6:8, :].rearrange("p a c -> p (a c)"), ALU.add).then_inc(sem("comb_free"), 1)
                dve.wait_ge(sem("hid_done"), b + 1)
                TS(g_sb, ps[:, 0, :], LIMIT, None, ALU.min).then_inc(sem("glu_gate_ready"), 1)
                TS(u_sb, ps[:, 1, :], LIMIT, -LIMIT, ALU.min, ALU.max).then_inc(sem("hid_free"), 1)
                dve.wait_ge(sem("hid_free"), b + 2)
                STT(u_sb, u_sb, 1.0, g_sb, ALU.add, ALU.mult).then_inc(sem("glu_up_ready"), 1)
                dve.wait_ge(sem("glu_up_ready"), b + 1)
                dve.wait_ge(sem("glu_sig_ready"), b + 1)
                TT(a_sb, u_sb, s_sb, ALU.mult).then_inc(sem("act_ready"), 1)
                rows_turned(b + 2)
            for tt, (t0, tn) in enumerate(TILES):
                dve.wait_ge(sem("comb_done"), nb * 3 + tt + 1)
                dve.wait_ge(sem("comb_free"), nb * 3 + 1)
                b0 = LAST_BANKS[tt]
                TT(x[0:tn, tt, :], x[0:tn, tt, :], ps[0:tn, b0:b0 + 2, :].rearrange("p a c -> p (a c)"), ALU.add).then_inc(sem("comb_free"), 1)

            for tt in range(3):
                normalise(3, tt, h2)
            for k in range(1, KD, 2):
                dve.wait_ge(sem("hT_done"), 2 * KD + 1 + k + 1)
                TS(h3T[:, k, :], ps[:, H3_BANKS[k % 3], 0:TOK], g3[:, k:k + 1], None, ALU.mult).then_inc(sem("hT_odd_ready"), 1)
            for n in range(5):
                tt = min(n // 2, 2)
                tn = TILES[tt][1]
                dve.wait_ge(sem("ple_sig_ready"), n + 1)
                dve.wait_ge(sem("ple_done"), n + 1)
                s_ = [g_sb, u_sb][n % 2]
                ch.link(TT(s_, s_, ps[:, PLE_BANKS[n], :], ALU.mult))
                if tt < 2:
                    xa = x[:, tt, 512 * (n % 2):512 * (n % 2) + 512]
                    TT(xa, xa, s_, ALU.add).then_inc(sem("ple_added"), 1)
                else:
                    xa, xb = x[0:64, 2, 0:512], x[0:64, 2, 512:1024]
                    ch(dve.tensor_copy(ple_moved, s_[64:128]))
                    ch.link(TT(xa, xa, s_[0:64], ALU.add))
                    TT(xb, xb, ple_moved, ALU.add).then_inc(sem("ple_added"), 1)
                if n % 2 or n == 4:
                    dve.wait_ge(sem("rms_ready"), 10 + tt)
                    ch.link(dve.reciprocal(rstd[0:tn, tt:tt + 1], rstd[0:tn, tt:tt + 1]))
                    STT(x[0:tn, tt, :], x[0:tn, tt, :], rstd[0:tn, tt:tt + 1], fng[0:tn], ALU.mult, ALU.mult).then_inc(sem("y_ready"), 1)


INS = ("x_prompt", "x_sample", "state_delta", "state_conv", "p_prompt", "p_sample", "norm1_g", "w_in", "conv_w",
       "a_log", "dt_bias", "dn_norm_g", "w_proj_a", "gm_ln_g", "gm_ln_b", "gm_ws", "gm_bs", "w_proj_b", "w_out",
       "norm2_g", "router_w", "router_b", "moe_w1", "moe_b1", "moe_w2", "moe_b2", "norm3_g", "ple_w", "ple_gate_w",
       "final_norm_g")
OUTS = (("out_yp", (1, SEQ, D)), ("out_ys", (DB, DS, D)), ("out_sd_p", (1, 1, H, P, P)), ("out_sc_p", (1, 1, TAPS - 1, QKV)),
        ("out_sd_s", (1, DB, H, P, P)), ("out_sc_s", (1, DB, TAPS - 1, QKV)), ("out_gv", (1, DB, DS, D)))


def kernel(**inputs):
    import concourse.bacc as bacc
    from concourse.bass_utils import run_bass_kernel_spmd

    nc = bacc.Bacc("TRN2", target_bir_lowering=False, num_devices=1)
    arrays, tensors = {}, {}
    for name in INS:
        a = np.ascontiguousarray(inputs[name])
        arrays[f"in_{name}"] = a
        tensors[name] = nc.dram_tensor(f"in_{name}", a.shape, mybir.dt.from_np(a.dtype), kind="ExternalInput").ap()
    arrays["in_consts"] = CONSTS
    tensors["consts"] = nc.dram_tensor("in_consts", CONSTS.shape, F32, kind="ExternalInput").ap()
    for name, shape in OUTS:
        tensors[name] = nc.dram_tensor(name, shape, F32, kind="ExternalOutput").ap()
    hybrid_layer(nc, tensors)
    r = run_bass_kernel_spmd(nc, [arrays], core_ids=[0])
    return tuple(r.results[0][name] for name, _ in OUTS)
```
